# Optimizing a Trainium2 kernel written in Bass

```python
import math
import jax, jax.numpy as jnp
from jax import lax
import numpy as np

D_MODEL = 1024
BATCH = 1
SEQ = 256
DEPTH = 2

N_EVEN = (DEPTH + 1) // 2
N_ODD = DEPTH // 2

D_A = D_MODEL // 2
D_B = D_MODEL // 2
CONV_A = 31
CONV_B = 3
D_IN_EVEN = 2 * D_A + 3 * D_B

D_RNN = D_MODEL
RNN_BLOCK = 256
RNN_HEADS = D_RNN // RNN_BLOCK
CONV_C = 4
LRU_C = 8.0

N_EXPERTS = 16
N_EXPERT_GROUPS = 4
EXPERTS_PER_GROUP = N_EXPERTS // N_EXPERT_GROUPS
TOP_K = 2
D_EXPERT = D_MODEL
MOE_BLOCK = 128

LN_EPS = 1e-5
ALPHA = (2.0 * DEPTH) ** 0.25
BETA = (8.0 * DEPTH) ** -0.25


def layer_norm(x, g, b):
    xf = x.astype(jnp.float32)
    mu = jnp.mean(xf, axis=-1, keepdims=True)
    var = jnp.mean(jnp.square(xf - mu), axis=-1, keepdims=True)
    y = (xf - mu) * lax.rsqrt(var + LN_EPS)
    return (y * g.astype(jnp.float32) + b.astype(jnp.float32)).astype(x.dtype)

def causal_depthwise_conv(x, w):
    k, c = w.shape
    return lax.conv_general_dilated(
        x, w[:, None, :].astype(x.dtype), window_strides=(1,), padding=[(k - 1, 0)],
        dimension_numbers=("NWC", "WIO", "NWC"), feature_group_count=c)

def conv_mixer(x, w_in, a_dw, a_dw_b, a_ln_g, a_ln_b, b_dw, w_out):
    u = jnp.einsum("bsd,de->bse", x, w_in)
    a_val, a_gate, b_b, b_c, b_x = jnp.split(
        u, [D_A, 2 * D_A, 2 * D_A + D_B, 2 * D_A + 2 * D_B], axis=-1)
    a = a_val * jax.nn.sigmoid(a_gate)
    a = causal_depthwise_conv(a, a_dw) + a_dw_b
    a = jax.nn.silu(layer_norm(a, a_ln_g, a_ln_b))
    bb = b_b * causal_depthwise_conv(b_c * b_x, b_dw)
    return jnp.einsum("bse,ed->bsd", jnp.concatenate([a, bb], axis=-1), w_out)

def _linear_recurrence_combine(c1, c2):
    a1, b1 = c1
    a2, b2 = c2
    return a1 * a2, a2 * b1 + b2

def rglru_mixer(x, w_in, c_dw, c_dw_b, w_gate_a, b_gate_a, w_gate_x, b_gate_x, lam, w_out):
    bsz, seq, _ = x.shape
    u = jnp.einsum("bsd,de->bse", x, w_in)
    y_branch, xr = jnp.split(u, 2, axis=-1)
    xr = causal_depthwise_conv(xr, c_dw) + c_dw_b
    xh = xr.reshape(bsz, seq, RNN_HEADS, RNN_BLOCK)
    r = jax.nn.sigmoid(jnp.einsum("bshi,hij->bshj", xh, w_gate_a) + b_gate_a)
    i = jax.nn.sigmoid(jnp.einsum("bshi,hij->bshj", xh, w_gate_x) + b_gate_x)
    r = r.reshape(bsz, seq, D_RNN).astype(jnp.float32)
    i = i.reshape(bsz, seq, D_RNN)
    log_a = -LRU_C * r * jax.nn.softplus(-lam.astype(jnp.float32))
    a = jnp.exp(log_a)
    mult = jnp.sqrt(-jnp.expm1(2.0 * log_a))
    b = mult * (i * xr).astype(jnp.float32)
    _, h = lax.associative_scan(_linear_recurrence_combine, (a, b), axis=1)
    out = jax.nn.gelu(y_branch) * h.astype(x.dtype)
    return jnp.einsum("bse,ed->bsd", out, w_out)

def route(xf, w_router, b_router):
    t = xf.shape[0]
    logits = (xf @ w_router + b_router).astype(jnp.float32)
    probs = jax.nn.softmax(logits, axis=-1)
    pg = probs.reshape(t, N_EXPERT_GROUPS, EXPERTS_PER_GROUP)
    group_score = lax.top_k(pg, TOP_K)[0].sum(-1)
    g_sel = jnp.argmax(group_score, axis=-1)
    p_in = jnp.take_along_axis(pg, g_sel[:, None, None], axis=1)[:, 0]
    top_p, top_i = lax.top_k(p_in, TOP_K)
    expert_idx = g_sel[:, None] * EXPERTS_PER_GROUP + top_i
    gates = top_p / jnp.sum(top_p, axis=-1, keepdims=True)
    return expert_idx, gates

def moe(x, w_router, b_router, w1, w3, w2):
    bsz, seq, d = x.shape
    t = bsz * seq
    xf = x.reshape(t, d)
    e_idx, gates = route(xf, w_router, b_router)
    n_assign = t * TOP_K
    e_flat = e_idx.reshape(n_assign)
    tok_flat = jnp.repeat(jnp.arange(t, dtype=jnp.int32), TOP_K)
    g_flat = gates.reshape(n_assign)
    order = jnp.argsort(e_flat)
    e_s, tok_s, g_s = e_flat[order], tok_flat[order], g_flat[order]
    counts = jnp.bincount(e_flat, length=N_EXPERTS)
    padded = (counts + MOE_BLOCK - 1) // MOE_BLOCK * MOE_BLOCK
    start = jnp.cumsum(counts) - counts
    pend = jnp.cumsum(padded)
    pstart = pend - padded
    dest = pstart[e_s] + jnp.arange(n_assign, dtype=jnp.int32) - start[e_s]
    n_blocks = -(-n_assign // MOE_BLOCK) + N_EXPERTS
    n_pad = n_blocks * MOE_BLOCK
    x_pad = jnp.zeros((n_pad, d), x.dtype).at[dest].set(xf[tok_s])
    block_expert = jnp.minimum(
        jnp.searchsorted(pend, jnp.arange(n_blocks, dtype=pend.dtype) * MOE_BLOCK, side="right"),
        N_EXPERTS - 1)

    def expert_block(args):
        xb, e = args
        hb = jax.nn.silu(xb @ w1[e]) * (xb @ w3[e])
        return hb @ w2[e]

    y_pad = lax.map(expert_block, (x_pad.reshape(n_blocks, MOE_BLOCK, d), block_expert))
    y = y_pad.reshape(n_pad, d)[dest] * g_s[:, None].astype(x.dtype)
    out = jnp.zeros((t, d), x.dtype).at[tok_s].add(y)
    return out.reshape(bsz, seq, d)

def first_inputs(seed: int = 0) -> dict:
    key = jax.random.key(seed)
    ks = jax.random.split(key, 26)
    nrm = lambda k, shape, s: jax.random.normal(k, shape, jnp.float32) * s
    a0 = jax.random.uniform(ks[19], (N_ODD, D_RNN), jnp.float32, 0.9, 0.999)
    s0 = a0 ** (1.0 / LRU_C)
    lam = jnp.log(s0) - jnp.log1p(-s0)
    return {
        "x": nrm(ks[0], (BATCH, SEQ, D_MODEL), 1.0),
        "ln1_g": 1.0 + nrm(ks[1], (DEPTH, D_MODEL), 0.02),
        "ln1_b": nrm(ks[2], (DEPTH, D_MODEL), 0.02),
        "ln2_g": 1.0 + nrm(ks[3], (DEPTH, D_MODEL), 0.02),
        "ln2_b": nrm(ks[4], (DEPTH, D_MODEL), 0.02),
        "even_w_in": nrm(ks[5], (N_EVEN, D_MODEL, D_IN_EVEN), D_MODEL ** -0.5),
        "even_a_dw": nrm(ks[6], (N_EVEN, CONV_A, D_A), CONV_A ** -0.5),
        "even_a_dw_b": nrm(ks[7], (N_EVEN, D_A), 0.02),
        "even_a_ln_g": 1.0 + nrm(ks[8], (N_EVEN, D_A), 0.02),
        "even_a_ln_b": nrm(ks[9], (N_EVEN, D_A), 0.02),
        "even_b_dw": nrm(ks[10], (N_EVEN, CONV_B, D_B), CONV_B ** -0.5),
        "even_w_out": nrm(ks[11], (N_EVEN, D_A + D_B, D_MODEL), BETA * (D_A + D_B) ** -0.5),
        "odd_w_in": nrm(ks[12], (N_ODD, D_MODEL, 2 * D_RNN), D_MODEL ** -0.5),
        "odd_c_dw": nrm(ks[13], (N_ODD, CONV_C, D_RNN), CONV_C ** -0.5),
        "odd_c_dw_b": nrm(ks[14], (N_ODD, D_RNN), 0.02),
        "odd_w_gate_a": nrm(ks[15], (N_ODD, RNN_HEADS, RNN_BLOCK, RNN_BLOCK), RNN_BLOCK ** -0.5),
        "odd_b_gate_a": nrm(ks[16], (N_ODD, RNN_HEADS, RNN_BLOCK), 0.02),
        "odd_w_gate_x": nrm(ks[17], (N_ODD, RNN_HEADS, RNN_BLOCK, RNN_BLOCK), RNN_BLOCK ** -0.5),
        "odd_b_gate_x": nrm(ks[18], (N_ODD, RNN_HEADS, RNN_BLOCK), 0.02),
        "odd_lam": lam,
        "odd_w_out": nrm(ks[20], (N_ODD, D_RNN, D_MODEL), BETA * D_RNN ** -0.5),
        "w_router": nrm(ks[21], (D_MODEL, N_EXPERTS), D_MODEL ** -0.5),
        "b_router": nrm(ks[22], (N_EXPERTS,), 0.01),
        "moe_w1": nrm(ks[23], (DEPTH, N_EXPERTS, D_MODEL, D_EXPERT), D_MODEL ** -0.5),
        "moe_w3": nrm(ks[24], (DEPTH, N_EXPERTS, D_MODEL, D_EXPERT), D_MODEL ** -0.5),
        "moe_w2": nrm(ks[25], (DEPTH, N_EXPERTS, D_EXPERT, D_MODEL), BETA * D_EXPERT ** -0.5),
    }

def first_block(x, ln1_g, ln1_b, ln2_g, ln2_b, even_w_in, even_a_dw, even_a_dw_b, even_a_ln_g,
              even_a_ln_b, even_b_dw, even_w_out, odd_w_in, odd_c_dw, odd_c_dw_b, odd_w_gate_a,
              odd_b_gate_a, odd_w_gate_x, odd_b_gate_x, odd_lam, odd_w_out, w_router, b_router,
              moe_w1, moe_w3, moe_w2):
    for layer in range(DEPTH):
        j = layer // 2
        if layer % 2 == 0:
            m = conv_mixer(x, even_w_in[j], even_a_dw[j], even_a_dw_b[j], even_a_ln_g[j],
                           even_a_ln_b[j], even_b_dw[j], even_w_out[j])
        else:
            m = rglru_mixer(x, odd_w_in[j], odd_c_dw[j], odd_c_dw_b[j], odd_w_gate_a[j],
                            odd_b_gate_a[j], odd_w_gate_x[j], odd_b_gate_x[j], odd_lam[j],
                            odd_w_out[j])
        x = layer_norm(ALPHA * x + m, ln1_g[layer], ln1_b[layer])
        f = moe(x, w_router, b_router, moe_w1[layer], moe_w3[layer], moe_w2[layer])
        x = layer_norm(ALPHA * x + f, ln2_g[layer], ln2_b[layer])
    return x


N_A_LAYERS = DEPTH // 2
N_B_LAYERS = DEPTH - N_A_LAYERS

A_HEADS = 16
A_HEAD_DIM = D_MODEL // A_HEADS
A_QKV_WIDTH = 3 * A_HEADS * A_HEAD_DIM
Q_BLOCK = 128

B_GROUPS = ((128, 1), (512, 4), (2048, 16))
B_N_GROUPS = len(B_GROUPS)
B_HEADS_PER_GROUP = 8
B_HEAD_DIM = 64
B_WINDOW_STEPS = 128
B_Q_WIDTH = B_N_GROUPS * B_HEADS_PER_GROUP * B_HEAD_DIM
B_OUT_WIDTH = B_HEADS_PER_GROUP * B_HEAD_DIM
B_KV_WIDTH = 2 * B_Q_WIDTH
ALIBI_TOTAL_HEADS = B_N_GROUPS * B_HEADS_PER_GROUP

D_FF = 2816
CONV_WIDTH = 3

RMS_EPS = 1e-6


def rms_norm(x, g):
    xf = x.astype(jnp.float32)
    y = xf * lax.rsqrt(jnp.mean(xf * xf, axis=-1, keepdims=True) + RMS_EPS)
    return (y * g.astype(jnp.float32)).astype(x.dtype)

def conv_ffn(h, w_up, conv_w, conv_b, w_down):
    u = h @ w_up
    c = u.shape[-1]
    u = lax.conv_general_dilated(
        u, conv_w[:, None, :].astype(u.dtype), window_strides=(1,),
        padding=[(CONV_WIDTH - 1, 0)],
        dimension_numbers=("NWC", "WIO", "NWC"),
        feature_group_count=c) + conv_b
    a, gate = jnp.split(u, 2, axis=-1)
    return (jax.nn.silu(gate) * a) @ w_down

def forgetting_attention(q, k, v, log_f):
    S = q.shape[1]
    dh = q.shape[-1]
    scale = dh ** -0.5
    c = jnp.cumsum(log_f.astype(jnp.float32), axis=1).transpose(0, 2, 1)
    outs = []
    for i in range(S // Q_BLOCK):
        q0 = i * Q_BLOCK
        q1 = q0 + Q_BLOCK
        s = jnp.einsum("bqhd,bkhd->bhqk", q[:, q0:q1], k[:, :q1]).astype(jnp.float32) * scale
        s = s + c[:, :, q0:q1, None] - c[:, :, None, :q1]
        causal = jnp.arange(q0, q1)[:, None] >= jnp.arange(q1)[None, :]
        p = jax.nn.softmax(jnp.where(causal, s, -jnp.inf), axis=-1)
        outs.append(jnp.einsum("bhqk,bkhd->bqhd", p.astype(v.dtype), v[:, :q1]))
    return jnp.concatenate(outs, axis=1)

def dilated_branch(q, k, v, dil, slopes):
    B, S, H, Dh = q.shape
    W = B_WINDOW_STEPS
    period = dil * W
    Sp = -(-S // period) * period
    nb = Sp // period
    pad = ((0, 0), (0, Sp - S), (0, 0), (0, 0))

    def blocks(t):
        return jnp.pad(t, pad).reshape(B, nb, W, dil, H, Dh)

    def with_prev(t):
        prev = jnp.pad(t, ((0, 0), (1, 0), (0, 0), (0, 0), (0, 0), (0, 0)))[:, :nb]
        return jnp.concatenate([prev, t], axis=2)

    qb = blocks(q)
    kk = with_prev(blocks(k))
    vv = with_prev(blocks(v))
    s = jnp.einsum("bnirhd,bnjrhd->bnrhij", qb, kk).astype(jnp.float32) * (Dh ** -0.5)
    qi = jnp.arange(W)[:, None]
    kj = jnp.arange(2 * W)[None, :]
    dist = qi + W - kj
    band = (dist >= 0) & (dist <= W)
    first = (jnp.arange(nb)[:, None, None] == 0) & (kj < W)[None]
    valid = band[None] & ~first
    bias = -slopes[:, None, None] * (dil * dist).astype(jnp.float32)
    s = jnp.where(valid[None, :, None, None], s + bias, -jnp.inf)
    m = jnp.max(s, axis=-1, keepdims=True)
    p = jnp.exp(s - m)
    l = jnp.sum(p, axis=-1, keepdims=True)
    o = jnp.einsum("bnrhij,bnjrhd->bnirhd", (p / l).astype(v.dtype), vv)
    lse = (m + jnp.log(l))[..., 0]
    o = o.reshape(B, Sp, H, Dh)[:, :S]
    lse = lse.transpose(0, 1, 4, 2, 3).reshape(B, Sp, H)[:, :S]
    return o, lse

def second_inputs(seed: int = 0) -> dict:
    key = jax.random.key(seed)
    ks = jax.random.split(key, 16)
    f32 = jnp.float32

    def nrm(k, shape, fan_in):
        return jax.random.normal(k, shape, f32) * (fan_in ** -0.5)

    def gain(k, shape):
        return 1.0 + 0.05 * jax.random.normal(k, shape, f32)

    return {
        "x": jax.random.normal(ks[0], (BATCH, SEQ, D_MODEL), f32),
        "a_w_in": nrm(ks[1], (N_A_LAYERS, D_MODEL, A_QKV_WIDTH + A_HEADS), D_MODEL),
        "a_b_f": 2.0 + 0.1 * jax.random.normal(ks[2], (N_A_LAYERS, A_HEADS), f32),
        "a_w_out": nrm(ks[3], (N_A_LAYERS, A_HEADS * A_HEAD_DIM, D_MODEL), A_HEADS * A_HEAD_DIM),
        "b_w_q": nrm(ks[4], (N_B_LAYERS, D_MODEL, B_Q_WIDTH), D_MODEL),
        "b_w_out": nrm(ks[5], (N_B_LAYERS, B_OUT_WIDTH, D_MODEL), B_OUT_WIDTH),
        "kv_norm_g": gain(ks[6], (D_MODEL,)),
        "w_kv": nrm(ks[7], (D_MODEL, B_KV_WIDTH), D_MODEL),
        "mix_norm_g": gain(ks[8], (DEPTH, D_MODEL)),
        "ffn_norm_g": gain(ks[9], (DEPTH, D_MODEL)),
        "ffn_w_up": nrm(ks[10], (DEPTH, D_MODEL, 2 * D_FF), D_MODEL),
        "ffn_conv_w": nrm(ks[11], (DEPTH, CONV_WIDTH, 2 * D_FF), CONV_WIDTH),
        "ffn_conv_b": 0.02 * jax.random.normal(ks[12], (DEPTH, 2 * D_FF), f32),
        "ffn_w_down": nrm(ks[13], (DEPTH, D_FF, D_MODEL), D_FF),
        "final_norm_g": gain(ks[14], (D_MODEL,)),
    }

def second_block(x, a_w_in, a_b_f, a_w_out, b_w_q, b_w_out, kv_norm_g, w_kv,
              mix_norm_g, ffn_norm_g, ffn_w_up, ffn_conv_w, ffn_conv_b, ffn_w_down,
              final_norm_g):
    B, S, D = x.shape
    slopes = jnp.exp2(-8.0 * jnp.arange(1, ALIBI_TOTAL_HEADS + 1, dtype=jnp.float32)
                      / ALIBI_TOTAL_HEADS).reshape(B_N_GROUPS, B_HEADS_PER_GROUP)
    kv = None
    for layer in range(DEPTH):
        if layer < N_A_LAYERS:
            h = rms_norm(x, mix_norm_g[layer])
            proj = h @ a_w_in[layer]
            qkv = proj[..., :A_QKV_WIDTH].reshape(B, S, 3, A_HEADS, A_HEAD_DIM)
            log_f = jax.nn.log_sigmoid(
                proj[..., A_QKV_WIDTH:].astype(jnp.float32) + a_b_f[layer].astype(jnp.float32))
            o = forgetting_attention(qkv[:, :, 0], qkv[:, :, 1], qkv[:, :, 2], log_f)
            x = x + o.reshape(B, S, A_HEADS * A_HEAD_DIM) @ a_w_out[layer]
        else:
            if kv is None:
                kv = (rms_norm(x, kv_norm_g) @ w_kv).reshape(
                    B, S, 2, B_N_GROUPS, B_HEADS_PER_GROUP, B_HEAD_DIM)
            bl = layer - N_A_LAYERS
            h = rms_norm(x, mix_norm_g[layer])
            q = (h @ b_w_q[bl]).reshape(B, S, B_N_GROUPS, B_HEADS_PER_GROUP, B_HEAD_DIM)
            outs, lses = [], []
            for g, (window, dil) in enumerate(B_GROUPS):
                o_g, lse_g = dilated_branch(q[:, :, g], kv[:, :, 0, g], kv[:, :, 1, g],
                                            dil, slopes[g])
                outs.append(o_g)
                lses.append(lse_g)
            alpha = jax.nn.softmax(jnp.stack(lses, axis=0), axis=0)
            o = jnp.sum(alpha[..., None].astype(outs[0].dtype) * jnp.stack(outs, axis=0), axis=0)
            x = x + o.reshape(B, S, B_OUT_WIDTH) @ b_w_out[bl]
        h = rms_norm(x, ffn_norm_g[layer])
        x = x + conv_ffn(h, ffn_w_up[layer], ffn_conv_w[layer], ffn_conv_b[layer],
                         ffn_w_down[layer])
    return rms_norm(x, final_norm_g)


def setup_inputs(seed=0):
    out = dict(first_inputs(seed))
    for name, value in second_inputs(seed + 1).items():
        if name != "x":
            out[name + "_2"] = value
    return out


def reference(
    x, ln1_g, ln1_b, ln2_g, ln2_b, even_w_in, even_a_dw, even_a_dw_b, even_a_ln_g, even_a_ln_b,
    even_b_dw, even_w_out, odd_w_in, odd_c_dw, odd_c_dw_b, odd_w_gate_a, odd_b_gate_a,
    odd_w_gate_x, odd_b_gate_x, odd_lam, odd_w_out, w_router, b_router, moe_w1, moe_w3, moe_w2,
    a_w_in_2, a_b_f_2, a_w_out_2, b_w_q_2, b_w_out_2, kv_norm_g_2, w_kv_2, mix_norm_g_2,
    ffn_norm_g_2, ffn_w_up_2, ffn_conv_w_2, ffn_conv_b_2, ffn_w_down_2, final_norm_g_2,
):
    x = first_block(
        x, ln1_g, ln1_b, ln2_g, ln2_b, even_w_in, even_a_dw, even_a_dw_b, even_a_ln_g,
        even_a_ln_b, even_b_dw, even_w_out, odd_w_in, odd_c_dw, odd_c_dw_b, odd_w_gate_a,
        odd_b_gate_a, odd_w_gate_x, odd_b_gate_x, odd_lam, odd_w_out, w_router, b_router,
        moe_w1, moe_w3, moe_w2,
    )
    return second_block(
        x, a_w_in_2, a_b_f_2, a_w_out_2, b_w_q_2, b_w_out_2, kv_norm_g_2, w_kv_2, mix_norm_g_2,
        ffn_norm_g_2, ffn_w_up_2, ffn_conv_w_2, ffn_conv_b_2, ffn_w_down_2, final_norm_g_2,
    )


_drawn_inputs = setup_inputs


def setup_inputs(seed=0):
    import zlib

    import numpy as np

    out = dict(_drawn_inputs(seed))
    spreads = {}
    factors = {'odd_b_gate_a': 7.496, 'odd_b_gate_x': 7.231, 'kv_norm_g_2': 3.141, 'ffn_conv_b_2': 2.828}
    for name, (base, spread) in spreads.items():
        noise = np.random.default_rng([zlib.crc32(name.encode()), seed]).standard_normal(out[name].shape)
        drawn = base * np.exp(spread * noise) if base else spread * noise
        out[name] = __import__('jax').numpy.asarray(drawn.astype(out[name].dtype))
    for name, factor in factors.items():
        out[name] = (out[name] * factor).astype(out[name].dtype)
    return out
```

```python
from contextlib import ExitStack
import math

import numpy as np

import concourse.bass as bass
from concourse import mybir

F32 = mybir.dt.float32
I32 = mybir.dt.int32
ALU = mybir.AluOpType
ACT = mybir.ActivationFunctionType
AX = mybir.AxisListType.X

T, D, NT, KD = 256, 1024, 2, 8
E, CAP = 16, 64
ALPHA = 4.0 ** 0.25
LN_EPS, RMS_EPS = 1e-5, 1e-6
RING = 12
CH = 2048
NEG = -1e30

COLS = {}
_at = 0
for _n, _w in (("a_dw", 4 * 31), ("a_dw_b", 4), ("a_ln_g", 4), ("a_ln_b", 4), ("b_dw", 4 * 3),
               ("c_dw", 8 * 4), ("c_dw_b", 8), ("bga", 8), ("bgx", 8), ("lam", 8),
               ("mixg0", 8), ("mixg1", 8), ("kvg", 8), ("ffng0", 8), ("ffng1", 8),
               ("fcw0", 44 * 3), ("fcw1", 44 * 3), ("fcb0", 44), ("fcb1", 44),
               ("wr", 8 * 16), ("wf", 8 * 16)):
    COLS[_n] = (_at, _w)
    _at += _w
NCOLS = _at
ROWS = ("ln1_g0", "ln1_b0", "ln2_g0", "ln2_b0", "ln1_g1", "ln1_b1", "ln2_g1", "ln2_b1", "final")


class Eng:

    def __init__(self, engine, sem):
        self.e, self.sem, self.n, self.seen = engine, sem, 0, {}

    def wait(self, toks):
        for t in toks:
            if t is None:
                continue
            if isinstance(t, list):
                self.wait(t)
                continue
            sem, val = t
            if self.seen.get(sem.name, 0) < val:
                self.e.wait_ge(sem, val)
                self.seen[sem.name] = val

    def do(self, toks, fn):
        self.wait(toks)
        fn(self.e).then_inc(self.sem, 1)
        self.n += 1
        return (self.sem, self.n)

    def go(self, toks, fn):
        self.wait(toks)
        fn(self.e)


class Stream:

    def __init__(self, sp, ring, sems, plan):
        self.sp, self.ring, self.sems, self.plan = sp, ring, sems, plan
        self.used = 0
        for n in range(RING):
            self.load(n, None)

    def load(self, n, freed):
        if n < len(self.plan):
            s = n % RING
            self.sp.wait([freed])
            src = self.plan[n][1]
            self.sp.e.dma_start(self.ring[:, s, 0:src.shape[-1]], src).then_inc(self.sems[s], 16)

    def take(self, name):
        n = self.used
        assert self.plan[n][0] == name, (self.plan[n][0], name)
        self.used += 1
        return self.ring[:, n % RING, :], (self.sems[n % RING], 16 * (n // RING + 1))

    def give(self, tok):
        self.load(self.used - 1 + RING, tok)


def program(nc, A, out, dbg=None):
    ctx = ExitStack()
    with ctx:
        def sb(name, shape, dt=F32):
            return ctx.enter_context(nc.sbuf_tensor(name, shape, dt))

        def sem(name):
            return ctx.enter_context(nc.semaphore(name))

        PE = Eng(nc.tensor, sem("s_pe"))
        AC = Eng(nc.scalar, sem("s_act"))
        DV = Eng(nc.vector, sem("s_dve"))
        PL = Eng(nc.gpsimd, sem("s_pool"))
        SP = Eng(nc.sync, sem("s_sp"))
        ring_sems = [sem(f"s_w{i}") for i in range(RING)]
        s_c, s_x, s_br, s_bf, s_out = sem("s_c"), sem("s_x"), sem("s_br"), sem("s_bf"), sem("s_out")
        s_row = [sem("s_row0"), sem("s_row1")]

        ring = sb("ring", [128, RING, CH])
        PS = ctx.enter_context(nc.psum_tensor("PS", [128, 8, 512], F32))
        cols = sb("cols", [128, NCOLS])
        X = sb("X", [128, NT, D])
        Z = sb("Z", [128, NT, D])
        XT = sb("XT", [128, KD, T])
        rowbuf = sb("rowbuf", [128, 2, D])
        F = sb("F", [128, 14080])
        GT = F[:, 0:2048].rearrange("p (k t) -> p k t", k=8)
        ident = sb("ident", [128, 128])
        ones = sb("ones", [128, 256])
        mean512 = sb("mean512", [128, 128])
        upper = sb("upper", [128, 128])
        iota64 = sb("iota64", [128, 64])
        cmask = sb("cmask", [128, 256])
        mhalf = sb("mhalf", [128, 2])
        brt = sb("brt", [128, 16])
        bft = sb("bft", [16, 1])
        sm = sb("sm", [128, 512])
        it = sb("it", [128, 8], I32)

        def col(name):
            a, w = COLS[name]
            return cols[:, a:a + w]

        def fv(a, k, t=T):
            return F[:, a:a + k * t].rearrange("p (k t) -> p k t", k=k)

        AC.e.dma_start(X[:, :, :], A["x"].rearrange("(h p) d -> p h d", p=128)).then_inc(s_x, 16)
        AC.e.dma_start(cols[:, :], A["cols"]).then_inc(s_c, 16)
        AC.e.dma_start(brt[:, :], A["b_router_rows"]).then_inc(s_br, 16)
        AC.e.dma_start(bft[:, :], A["a_b_f"]).then_inc(s_bf, 16)
        c_ok, x_ok, br_ok, bf_ok = (s_c, 16), (s_x, 16), (s_br, 16), (s_bf, 16)

        t0 = PL.do([], lambda e: e.memset(ident[:, :], 0.0))
        k_ident = PL.do([t0], lambda e: e.affine_select(
            out=ident[:, :], in_=ident[:, :], compare_op=ALU.not_equal, fill=1.0, base=0,
            pattern=[[-1, 128]], channel_multiplier=1))
        k_ones = PL.do([], lambda e: e.memset(ones[:, :], 1.0))
        k_mean = PL.do([], lambda e: e.memset(mean512[:, :], 1.0 / 512))
        k_mhalf = PL.do([], lambda e: e.memset(mhalf[:, :], -0.5))
        t0 = PL.do([], lambda e: e.memset(upper[:, :], 1.0))
        k_upper = PL.do([t0], lambda e: e.affine_select(
            out=upper[:, :], in_=upper[:, :], compare_op=ALU.is_gt, fill=0.0, base=0,
            pattern=[[1, 128]], channel_multiplier=-1))
        k_iota = PL.do([], lambda e: e.iota(iota64[:, :], pattern=[[1, 64]], base=0, channel_multiplier=0,
                                            allow_small_or_imprecise_dtypes=True))
        t0 = PL.do([], lambda e: e.memset(cmask[:, :], 0.0))
        k_cmask = PL.do([t0], lambda e: e.affine_select(
            out=cmask[:, :], in_=cmask[:, :], compare_op=ALU.is_ge, fill=NEG, base=128,
            pattern=[[-1, 256]], channel_multiplier=1))
        plan = []

        def add(name, ap, order):
            for c in order:
                plan.append((name, ap[c]))

        def add_moe(layer):
            for e in range(E):
                for w in ("w1", "w3", "w2"):
                    add(f"{w}{layer}", A[w][layer, e], range(4))

        add("ew_in", A["even_w_in"], [2, 3, 0, 1, 6, 7, 8, 9, 4, 5])
        add("ew_out", A["even_w_out"], range(4))
        add_moe(0)
        add("ow_in", A["odd_w_in"], [4, 5, 6, 7, 0, 1, 2, 3])
        add("gates", A["odd_gates"], range(2))
        add("ow_out", A["odd_w_out"], range(4))
        add_moe(1)
        add("aw_in", A["a_w_in"], range(12))
        add("aw_out", A["a_w_out"], range(4))
        add("up0", A["ffn_up"][0], range(22))
        add("down0", A["ffn_down"][0], range(11))
        add("wkv", A["w_kv"], range(12))
        add("bwq", A["b_w_q"], range(6))
        add("bw_out", A["b_w_out"], range(2))
        add("up1", A["ffn_up"][1], range(22))
        add("down1", A["ffn_down"][1], range(11))
        if dbg and dbg.startswith(("att", "ffn", "all")):
            plan = plan[[n for n, _ in plan].index("aw_in"):]
        W = Stream(SP, ring, ring_sems, plan)

        free = [None] * 8
        rows_used = [0]
        row_free = [None, None]
        loaded = {}

        def want_row(name):
            n = rows_used[0]
            rows_used[0] += 1
            AC.wait([row_free[n % 2]])
            AC.e.dma_start(rowbuf[:, n % 2, :], A["rows"][ROWS.index(name), :].partition_broadcast(128)).then_inc(s_row[n % 2], 16)
            loaded[name] = (n % 2, (s_row[n % 2], 16 * (n // 2 + 1)))

        def row(name):
            return rowbuf[:, loaded[name][0], :], loaded[name][1]

        def row_done(name, toks):
            row_free[loaded[name][0]] = toks

        def to_features(src, src_tok, evac, first=0, nb=4):
            toks = []
            for q in range(4):
                b = first + q % nb
                for j in range(2):
                    k = 2 * q + j
                    for h in range(2):
                        w = [src_tok, k_ident, free[b]] if (j, h) == (0, 0) else []
                        o = PS[:, b, j * 256 + h * 128:j * 256 + h * 128 + 128]
                        s = src[:, h, k * 128:k * 128 + 128]
                        if (j, h) == (1, 1):
                            t = PE.do(w, lambda e: e.transpose(o, s, ident[:, :]))
                        else:
                            PE.go(w, lambda e: e.transpose(o, s, ident[:, :]))
                free[b] = evac(q, PS[:, b, :].rearrange("p (k t) -> p k t", k=2), t)
                toks.append(free[b])
            return toks

        def copy_xt(dst, after):
            def evac(q, ps, t):
                if q % 2:
                    return DV.do([t, after], lambda e: e.tensor_copy(dst[:, 2 * q:2 * q + 2, :], ps))
                return AC.do([t, after], lambda e: e.activation(dst[:, 2 * q:2 * q + 2, :], ps, ACT.Copy))
            return evac

        def proj_features(name, n, xt, xt_tok, evac, banks):
            for c in range(n):
                w, w_ok = W.take(name)
                b = banks[c % len(banks)]
                for j in range(2):
                    for k in range(8):
                        o = PS[:, b, j * 256:j * 256 + 256]
                        lt = w[:, k * 256 + j * 128:k * 256 + j * 128 + 128]
                        wt = [xt_tok, w_ok, free[b]] if (j, k) == (0, 0) else []
                        f = (lambda e: e.matmul(o, lt, xt[:, k, :], start=(k == 0), stop=(k == 7)))
                        if (j, k) == (1, 7):
                            t = PE.do(wt, f)
                        else:
                            PE.go(wt, f)
                W.give(t)
                free[b] = evac(c, PS[:, b, :].rearrange("p (k t) -> p k t", k=2), t)

        def proj_cols(name, n, xt, xt_tok, evac, banks):
            for c in range(n):
                w, w_ok = W.take(name)
                b = banks[c % len(banks)]
                for h in range(2):
                    for k in range(8):
                        o = PS[:, b, h * 256:h * 256 + 256]
                        lt = xt[:, k, h * 128:h * 128 + 128]
                        rt = w[:, k * 256:k * 256 + 256]
                        wt = [xt_tok, w_ok, free[b]] if (h, k) == (0, 0) else []
                        f = (lambda e: e.matmul(o, lt, rt, start=(k == 0), stop=(k == 7)))
                        if (h, k) == (1, 7):
                            t = PE.do(wt, f)
                        else:
                            PE.go(wt, f)
                W.give(t)
                free[b] = evac(c, PS[:, b, :].rearrange("p (k t) -> p k t", k=2), t)

        def proj_out(name, nk, gt, gt_toks, evac):
            for c in range(nk // 2):
                w, w_ok = W.take(name)
                for kk in range(2):
                    k = 2 * c + kk
                    for h in range(2):
                        for d in range(2):
                            b = 2 * h + d
                            o, lt = PS[:, b, :], gt[:, k, h * 128:h * 128 + 128]
                            rt = w[:, kk * 1024 + d * 512:kk * 1024 + d * 512 + 512]
                            wt = [w_ok, gt_toks[k], free[b] if k == 0 else None]
                            t = PE.do(wt, lambda e: e.matmul(o, lt, rt, start=(k == 0), stop=(k == nk - 1)))
                W.give(t)
            for h in range(2):
                for d in range(2):
                    free[2 * h + d] = evac(h, d, PS[:, 2 * h + d, :], t)

        def rstd(var, eps, n, toks):
            a = DV.do(toks, lambda e: e.tensor_scalar(sm[:, 490:490 + n], var, eps, None, ALU.add))
            return PL.do([a, k_mhalf], lambda e: e.tensor_tensor(
                sm[:, 500:500 + n], sm[:, 490:490 + n], mhalf[:, 0:n], ALU.pow))

        def layer_norm(src, src_toks, g, b, dst, dst_free):
            st = sm[:, 400:424].rearrange("p (h d s) -> p h d s", h=2, d=2)
            mv = sm[:, 424:428].rearrange("p (h s) -> p h s", h=2)
            ag = []
            for h in range(2):
                tt = [DV.do([src_toks], lambda e: e.bn_stats(st[:, h, d, :], src[:, h, d * 512:d * 512 + 512]))
                      for d in range(2)]
                ag.append(DV.do(tt, lambda e: e.bn_aggr(mv[:, h, :], st[:, h, :, :])))
            r = rstd(mv[:, :, 1], LN_EPS, 2, ag)
            (gr, g_ok), (br, b_ok) = row(g), row(b)
            done = []
            for h in range(2):
                n = DV.do([r, ag, dst_free], lambda e: e.tensor_scalar(
                    dst[:, h, :], src[:, h, :], mv[:, h, 0:1], sm[:, 500 + h:501 + h],
                    ALU.subtract, ALU.mult))
                en = DV if h else PL
                m = en.do([n, g_ok], lambda e: e.tensor_tensor(dst[:, h, :], dst[:, h, :], gr, ALU.mult))
                done.append(en.do([m, b_ok], lambda e: e.tensor_tensor(dst[:, h, :], dst[:, h, :], br, ALU.add)))
            row_done(g, done)
            row_done(b, done)
            return done

        def rms_scale(src, src_toks, dst, dst_free):
            s = []
            for h in range(2):
                s.append(AC.do([src_toks, dst_free], lambda e: e.activation(
                    dst[:, h, :], src[:, h, :], ACT.Square, accum_out=sm[:, 430 + h:431 + h])))
            a = DV.do(s, lambda e: e.tensor_scalar(sm[:, 490:492], sm[:, 430:432], 1.0 / D, RMS_EPS,
                                                   ALU.mult, ALU.add))
            r = PL.do([a, k_mhalf], lambda e: e.tensor_tensor(
                sm[:, 500:502], sm[:, 490:492], mhalf[:, 0:2], ALU.pow))
            done = []
            for h in range(2):
                done.append(DV.do([r, s, dst_free], lambda e: e.tensor_scalar(
                    dst[:, h, :], src[:, h, :], sm[:, 500 + h:501 + h], None, ALU.mult)))
            return done

        def scaled_xt(dst, gname, after):
            g = col(gname)

            def evac(q, ps, t):
                a = AC.do([t, after, c_ok], lambda e: e.activation(
                    dst[:, 2 * q, :], ps[:, 0, :], ACT.Copy, scale=g[:, 2 * q:2 * q + 1]))
                b = DV.do([t, after, c_ok, a], lambda e: e.tensor_scalar(
                    dst[:, 2 * q + 1, :], ps[:, 1, :], g[:, 2 * q + 1:2 * q + 2], None, ALU.mult))
                return [a, b]
            return evac

        def even_mixer():
            xt_ok = to_features(X, x_ok, copy_xt(XT, None))
            aP = F[:, 2048:2048 + 4 * 286].rearrange("p (k t) -> p k t", k=4)
            bP = F[:, 3200:3200 + 4 * 258].rearrange("p (k t) -> p k t", k=4)
            sg = fv(4300, 4)
            acc = fv(5400, 4)
            bc = fv(6500, 4)
            bacc = fv(7600, 4)
            sq = fv(8700, 4)
            rs = F[:, 9800:10056]
            gh, bh = sm[:, 0:4], sm[:, 4:8]
            z1 = DV.do([], lambda e: e.memset(aP[:, :, 0:30], 0.0))
            z2 = DV.do([], lambda e: e.memset(bP[:, :, 0:2], 0.0))
            h1 = DV.do([c_ok], lambda e: e.tensor_scalar(gh, col("a_ln_g"), 0.5, None, ALU.mult))
            h2 = DV.do([c_ok], lambda e: e.tensor_scalar(bh, col("a_ln_b"), 0.5, None, ALU.mult))
            tok = {}
            aw = col("a_dw").rearrange("p (c k) -> p c k", c=4)
            last = [None] * 4
            steps = [(k, c) for half in range(2) for k in range(31) for c in (2 * half, 2 * half + 1)]

            def convolve(n):
                for _ in range(min(n, len(steps))):
                    k, c = steps.pop(0)
                    src, wk = aP[:, c, k:k + 256], aw[:, c, k:k + 1]
                    if k == 0:
                        last[c] = DV.do([tok["a", c // 2], z1, c_ok], lambda e: e.tensor_scalar(
                            acc[:, c, :], src, wk, None, ALU.mult))
                    else:
                        last[c] = DV.do([last[c]], lambda e: e.scalar_tensor_tensor(
                            out=acc[:, c, :], in0=src, scalar=wk, in1=acc[:, c, :],
                            op0=ALU.mult, op1=ALU.add))

            def evac(c, ps, t):
                i = 2 * (c % 2)
                if c < 2:
                    tok["g", c] = AC.do([t], lambda e: e.activation(sg[:, i:i + 2, :], ps, ACT.Tanh, scale=0.5))
                    return tok["g", c]
                if c < 4:
                    tok["a", c - 2] = DV.do([t, tok["g", c - 2]], lambda e: e.scalar_tensor_tensor(
                        out=aP[:, i:i + 2, 30:286], in0=sg[:, i:i + 2, :], scalar=1.0, in1=ps,
                        op0=ALU.add, op1=ALU.mult))
                    return tok["a", c - 2]
                convolve(20)
                if c < 6:
                    tok["c", c - 4] = AC.do([t], lambda e: e.activation(bc[:, i:i + 2, :], ps, ACT.Copy))
                    return tok["c", c - 4]
                if c < 8:
                    tok["x", c - 6] = DV.do([t, tok["c", c - 6]], lambda e: e.tensor_tensor(
                        bP[:, i:i + 2, 2:258], bc[:, i:i + 2, :], ps, ALU.mult))
                    return tok["x", c - 6]
                tok["b", c - 8] = AC.do([t, tok["x", c - 8]], lambda e: e.activation(
                    bc[:, i:i + 2, :], ps, ACT.Copy))
                return tok["b", c - 8]

            proj_features("ew_in", 10, XT, xt_ok, evac, list(range(8)))
            convolve(len(steps))
            bw = col("b_dw").rearrange("p (c k) -> p c k", c=4)
            blast = [None] * 4
            for k in range(3):
                for c in range(4):
                    src, wk = bP[:, c, k:k + 256], bw[:, c, k:k + 1]
                    if k == 0:
                        blast[c] = DV.do([tok["x", c // 2], z2, c_ok], lambda e: e.tensor_scalar(
                            bacc[:, c, :], src, wk, None, ALU.mult))
                    else:
                        blast[c] = DV.do([blast[c]], lambda e: e.scalar_tensor_tensor(
                            out=bacc[:, c, :], in0=src, scalar=wk, in1=bacc[:, c, :],
                            op0=ALU.mult, op1=ALU.add))
            gt = [None] * 8
            for i in range(2):
                t = DV.do([blast, tok["b", i]], lambda e: e.tensor_tensor(
                    GT[:, 4 + 2 * i:6 + 2 * i, :], bacc[:, 2 * i:2 * i + 2, :], bc[:, 2 * i:2 * i + 2, :], ALU.mult))
                gt[4 + 2 * i] = gt[5 + 2 * i] = t
            for c in range(4):
                last[c] = DV.do([last[c], c_ok], lambda e: e.tensor_scalar(
                    acc[:, c, :], acc[:, c, :], 0.5, col("a_dw_b")[:, c:c + 1], ALU.mult, ALU.add))
            for c in range(4):
                m = PE.do([last[c], k_mean, free[0]], lambda e: e.matmul(
                    PS[:, 0, 0:256], mean512[:, :], acc[:, c, :], start=(c == 0), stop=(c == 3)))
            d = DV.do([m], lambda e: e.tensor_tensor(
                acc, acc, PS[:, 0, 0:256].unsqueeze(1).to_broadcast([128, 4, 256]), ALU.subtract))
            free[0] = d
            s = AC.do([d], lambda e: e.activation(sq, acc, ACT.Square))
            for c in range(4):
                m = PE.do([s, free[1]], lambda e: e.matmul(
                    PS[:, 1, 0:256], mean512[:, :], sq[:, c, :], start=(c == 0), stop=(c == 3)))
            v = DV.do([m], lambda e: e.tensor_scalar(rs, PS[:, 1, 0:256], LN_EPS, None, ALU.add))
            free[1] = v
            r = AC.do([v], lambda e: e.activation(rs, rs, ACT.Sqrt))
            r = DV.do([r], lambda e: e.reciprocal(rs, rs))
            d = DV.do([r, d, s], lambda e: e.tensor_tensor(
                acc, acc, rs.unsqueeze(1).to_broadcast([128, 4, 256]), ALU.mult))
            for c in range(4):
                y = DV.do([d, h1, h2], lambda e: e.tensor_scalar(
                    acc[:, c, :], acc[:, c, :], gh[:, c:c + 1], bh[:, c:c + 1], ALU.mult, ALU.add))
                th = AC.do([y, m], lambda e: e.activation(sq[:, c, :], acc[:, c, :], ACT.Tanh))
                gt[c] = DV.do([th], lambda e: e.scalar_tensor_tensor(
                    out=GT[:, c, :], in0=sq[:, c, :], scalar=1.0, in1=acc[:, c, :],
                    op0=ALU.add, op1=ALU.mult))
            return gt

        def add_residual(x, x_tok, scale, dst, dst_free):
            def evac(h, d, ps, t):
                sl = slice(d * 512, d * 512 + 512)
                if scale == 1.0:
                    return DV.do([t, x_tok, dst_free], lambda e: e.tensor_tensor(
                        dst[:, h, sl], x[:, h, sl], ps, ALU.add))
                return DV.do([t, x_tok, dst_free], lambda e: e.scalar_tensor_tensor(
                    out=dst[:, h, sl], in0=x[:, h, sl], scalar=scale, in1=ps, op0=ALU.mult, op1=ALU.add))
            return evac

        def odd_mixer(xt_ok):
            xP = F[:, 2048:2048 + 8 * 259].rearrange("p (k t) -> p k t", k=8)
            y = fv(4128, 8)
            xc = fv(6176, 8)
            r = fv(8224, 8)
            ig = fv(10272, 8)
            sp = [sm[:, i * 8:i * 8 + 8] for i in range(6)]
            hb = sm[:, 48:64]
            lam = col("lam")
            t = AC.do([c_ok], lambda e: e.activation(sp[0], lam, ACT.Abs))
            t = AC.do([t], lambda e: e.activation(sp[1], sp[0], ACT.Exp, scale=-1.0))
            u = DV.do([t], lambda e: e.tensor_scalar(sp[2], sp[1], 1.0, None, ALU.add))
            t = AC.do([u], lambda e: e.activation(sp[3], sp[2], ACT.Ln))
            t = AC.do([t], lambda e: e.activation(sp[4], sp[3], ACT.Tanh, scale=0.5))
            v = DV.do([t], lambda e: e.tensor_scalar(sp[5], sp[4], -1.0, 1.0, ALU.mult, ALU.add))
            v = DV.do([v], lambda e: e.reciprocal(sp[5], sp[5]))
            v = DV.do([v], lambda e: e.scalar_tensor_tensor(out=sp[4], in0=sp[4], scalar=2.0, in1=sp[5],
                                                            op0=ALU.mult, op1=ALU.mult))
            v = DV.do([v], lambda e: e.tensor_tensor(sp[4], sp[4], sp[1], ALU.subtract))
            u = DV.do([v], lambda e: e.reciprocal(sp[2], sp[2]))
            v = DV.do([u], lambda e: e.tensor_tensor(sp[4], sp[4], sp[2], ALU.mult))
            v = DV.do([v], lambda e: e.tensor_tensor(sp[3], sp[3], sp[4], ALU.subtract))
            u = DV.do([c_ok], lambda e: e.tensor_scalar(sp[0], lam, -1.0, 0.0, ALU.mult, ALU.max))
            v = DV.do([v, u], lambda e: e.tensor_tensor(sp[3], sp[3], sp[0], ALU.add))
            sp2 = sp[1]
            v_sp = DV.do([v], lambda e: e.tensor_scalar(sp2, sp[3], 2.0, None, ALU.mult))
            v_hb = DV.do([c_ok], lambda e: e.tensor_scalar(
                hb, cols[:, COLS["bga"][0]:COLS["bga"][0] + 16], 0.5, None, ALU.mult))
            z1 = DV.do([xt_ok], lambda e: e.memset(xP[:, :, 0:3], 0.0))
            tok = {}

            def evac(c, ps, t):
                if c < 4:
                    tok["x", c] = AC.do([t, xt_ok], lambda e: e.activation(xP[:, 2 * c:2 * c + 2, 3:259], ps, ACT.Copy))
                    return tok["x", c]
                i = 2 * (c - 4)
                tok["y", c - 4] = AC.do([t], lambda e: e.activation(y[:, i:i + 2, :], ps, ACT.Copy))
                return tok["y", c - 4]

            proj_features("ow_in", 8, XT, xt_ok, evac, list(range(8)))
            cw = col("c_dw").rearrange("p (c k) -> p c k", c=8)
            cb = col("c_dw_b")
            last = [None] * 8
            for k in range(4):
                for c in range(8):
                    src, wk = xP[:, c, k:k + 256], cw[:, c, k:k + 1]
                    if k == 0:
                        last[c] = DV.do([tok["x", c // 2], z1, c_ok], lambda e: e.tensor_scalar(
                            xc[:, c, :], src, wk, cb[:, c:c + 1], ALU.mult, ALU.add))
                    else:
                        last[c] = DV.do([last[c]], lambda e: e.scalar_tensor_tensor(
                            out=xc[:, c, :], in0=src, scalar=wk, in1=xc[:, c, :], op0=ALU.mult, op1=ALU.add))
            for g, dst in ((0, r), (1, ig)):
                w, w_ok = W.take("gates")
                wv = w.rearrange("p (h k n) -> p h k n", h=4, k=2)
                for h in range(4):
                    b = h + 4 * g
                    for j in range(2):
                        for k in range(2):
                            t = PE.do([w_ok, last[2 * h + k], free[b] if j == 0 else None], lambda e: e.matmul(
                                PS[:, b, j * 256:j * 256 + 256], wv[:, h, k, j * 128:j * 128 + 128],
                                xc[:, 2 * h + k, :], start=(k == 0), stop=(k == 1)))
                    for j in range(2):
                        c = 2 * h + j
                        tok[g, c] = AC.do([t, v_hb], lambda e: e.activation(
                            dst[:, c, :], PS[:, b, j * 256:j * 256 + 256], ACT.Tanh, scale=0.5,
                            bias=hb[:, 8 * g + c:8 * g + c + 1]))
                    free[b] = tok[g, c]
                W.give(t)
            Tt = fv(2048, 8)
            gt = [None] * 8
            r1 = DV.do([tok[0, 7]], lambda e: e.tensor_scalar(r, r, 1.0, None, ALU.add))
            bx = DV.do([tok[1, 7], last], lambda e: e.scalar_tensor_tensor(
                out=xc, in0=ig, scalar=1.0, in1=xc, op0=ALU.add, op1=ALU.mult))
            tt = [AC.do([r1, v_sp, last], lambda e: e.activation(
                Tt[:, c, :], r[:, c, :], ACT.Tanh, scale=sp2[:, c:c + 1])) for c in range(8)]
            ri = DV.do([tt], lambda e: e.tensor_scalar(r, Tt, 1.0, None, ALU.add))
            ri = DV.do([ri], lambda e: e.reciprocal(r, r))
            yt = [tok["y", i] for i in range(4)]
            g1 = AC.do([yt, bx], lambda e: e.activation(ig, y, ACT.Square))
            g2 = DV.do([g1], lambda e: e.tensor_scalar(ig, ig, 0.044715, 1.0, ALU.mult, ALU.add))
            g3 = DV.do([g2], lambda e: e.tensor_tensor(ig, ig, y, ALU.mult))
            g4 = AC.do([g3], lambda e: e.activation(ig, ig, ACT.Tanh, scale=math.sqrt(2.0 / math.pi)))
            g5 = DV.do([g4], lambda e: e.scalar_tensor_tensor(
                out=y, in0=ig, scalar=1.0, in1=y, op0=ALU.add, op1=ALU.mult))
            sq = AC.do([tt, g4, g5], lambda e: e.activation(ig, Tt, ACT.Sqrt))
            b1 = DV.do([sq, ri, bx], lambda e: e.tensor_tensor(xc, xc, ig, ALU.mult))
            b2 = DV.do([b1], lambda e: e.tensor_tensor(xc, xc, r, ALU.mult))
            a1 = DV.do([sq], lambda e: e.tensor_scalar(Tt, Tt, -1.0, 1.0, ALU.mult, ALU.add))
            a2 = DV.do([a1, ri], lambda e: e.tensor_tensor(Tt, Tt, r, ALU.mult))
            for c in range(8):
                s = DV.do([a2, b2], lambda e: e.tensor_tensor_scan(
                    ig[:, c, :], Tt[:, c, :], xc[:, c, :], 0.0, ALU.mult, ALU.add))
                gt[c] = DV.do([s, g5], lambda e: e.scalar_tensor_tensor(
                    out=GT[:, c, :], in0=y[:, c, :], scalar=0.5, in1=ig[:, c, :], op0=ALU.mult, op1=ALU.mult))
            return gt

        def moe(layer, x_tok, xt_ok):
            S = F[:, 0:2048].rearrange("p (h n) -> p h n", h=2)
            Gs = [F[:, 2048 + i * 2048:4096 + i * 2048].rearrange("p (h n) -> p h n", h=2) for i in range(2)]
            Gt = [F[:, 6144 + i * 512:6656 + i * 512].rearrange("p (h s t) -> p h s t", h=2, s=2)
                  for i in range(2)]
            xg = [F[:, 7168 + i * 1024:8192 + i * 1024].rearrange("p (k s) -> p k s", k=8) for i in range(2)]
            th, sl, hh = (F[:, 9216 + i * 512:9728 + i * 512] for i in range(3))
            hT = [F[:, 10752 + i * 512:11264 + i * 512] for i in range(2)]
            Y = [F[:, 11776 + i * 512:12288 + i * 512] for i in range(2)]

            def v2(a, n=16):
                return sm[:, a:a + 2 * n].rearrange("p (h e) -> p h e", h=2)

            wr = col("wr").rearrange("p (k e) -> p k e", k=8)
            for h in range(2):
                for k in range(8):
                    t = PE.do([xt_ok, c_ok, free[4]], lambda e: e.matmul(
                        PS[:, 4, h * 16:h * 16 + 16], XT[:, k, h * 128:h * 128 + 128], wr[:, k, :],
                        start=(k == 0), stop=(k == 7)))
            lg, pr, oh, tmp, m1, m2 = v2(0), v2(32), v2(64), v2(96), v2(128), v2(160)
            M, pos, gate, og = v2(192), v2(224), v2(256), v2(288)
            mx = sm[:, 320:322]
            gs = sm[:, 324:332].rearrange("p (h g) -> p h g", h=2)
            gp = sm[:, 332:340].rearrange("p (h g) -> p h g", h=2)
            p1, p2, den = sm[:, 340:342], sm[:, 342:344], sm[:, 344:346]
            pri = sm[:, 346:362]
            cnt = sm[:, 362:378]
            fl = sm[:, 378:379]

            def dv(toks, fn):
                return DV.do(toks, fn)

            def bc(ap, n=16):
                return ap.unsqueeze(2).to_broadcast([128, 2, n])

            t = dv([t, br_ok], lambda e: e.tensor_tensor(
                lg, PS[:, 4, 0:32].rearrange("p (h e) -> p h e", h=2),
                brt[:, :].unsqueeze(1).to_broadcast([128, 2, 16]), ALU.add))
            free[4] = t
            tp = PL.do([k_iota], lambda e: e.tensor_scalar(pri, iota64[:, 0:16], -1.0, 16.0, ALU.mult, ALU.add))
            t = dv([t], lambda e: e.tensor_reduce(mx, lg, AX, ALU.max))
            t = dv([t], lambda e: e.tensor_tensor(lg, lg, bc(mx), ALU.subtract))
            t = AC.do([t], lambda e: e.activation(pr, lg, ACT.Exp))
            t = dv([t], lambda e: e.tensor_reduce(den, pr, AX, ALU.add))
            t = dv([t], lambda e: e.reciprocal(den, den))
            t = dv([t], lambda e: e.tensor_tensor(pr, pr, bc(den), ALU.mult))
            pg = pr.rearrange("p h (g j) -> p h g j", g=4)
            pairs = tmp
            tg = None
            for n, (i, j) in enumerate(((0, 1), (0, 2), (0, 3), (1, 2), (1, 3), (2, 3))):
                dst = gs if n == 0 else gp
                u = dv([t, tg], lambda e: e.tensor_tensor(dst, pg[:, :, :, i], pg[:, :, :, j], ALU.add))
                tg = u if n == 0 else dv([u], lambda e: e.tensor_tensor(gs, gs, gp, ALU.max))

            def first_max(val, n, best, onehot, toks):
                prio = pri[:, 16 - n:16]
                a = dv(toks, lambda e: e.tensor_reduce(best, val, AX, ALU.max))
                a = dv([a], lambda e: e.tensor_tensor(onehot, val, bc(best, n), ALU.is_ge))
                a = dv([a, tp], lambda e: e.tensor_tensor(
                    onehot, onehot, prio.unsqueeze(1).to_broadcast([128, 2, n]), ALU.mult))
                b = dv([a], lambda e: e.tensor_reduce(sm[:, 380:382], onehot, AX, ALU.max))
                return dv([b], lambda e: e.tensor_tensor(onehot, onehot, bc(sm[:, 380:382], n), ALU.is_equal))

            tg = first_max(gs, 4, mx, gp, [tg])
            og4 = oh.rearrange("p h (g j) -> p h g j", g=4)
            tt4 = tmp.rearrange("p h (g j) -> p h g j", g=4)
            gb = gp.unsqueeze(3).to_broadcast([128, 2, 4, 4])
            a = dv([tg], lambda e: e.tensor_tensor(og4, pg, gb, ALU.mult))
            b = dv([tg], lambda e: e.tensor_scalar(gs, gp, -1.0, None, ALU.add))
            gb2 = gs.unsqueeze(3).to_broadcast([128, 2, 4, 4])
            a = dv([a, b], lambda e: e.tensor_tensor(tt4, og4, gb2, ALU.add))
            a = first_max(tmp, 16, p1, m1, [a])
            a = dv([a], lambda e: e.scalar_tensor_tensor(out=tmp, in0=m1, scalar=-4.0, in1=tmp,
                                                         op0=ALU.mult, op1=ALU.add))
            a = first_max(tmp, 16, p2, m2, [a])
            b = dv([a], lambda e: e.tensor_tensor(den, p1, p2, ALU.add))
            b = dv([b], lambda e: e.reciprocal(den, den))
            b1 = dv([b], lambda e: e.tensor_tensor(p1, p1, den, ALU.mult))
            b2 = dv([b1], lambda e: e.tensor_tensor(p2, p2, den, ALU.mult))
            a = dv([a], lambda e: e.tensor_tensor(M, m1, m2, ALU.add))
            b1 = dv([b1, b2], lambda e: e.tensor_tensor(m1, m1, bc(p1), ALU.mult))
            b2 = dv([b2], lambda e: e.tensor_tensor(m2, m2, bc(p2), ALU.mult))
            tgate = dv([b1, b2], lambda e: e.tensor_tensor(gate, m1, m2, ALU.add))
            for h in range(2):
                if h == 1:
                    PE.go([k_ones], lambda e: e.matmul(PS[:, 4, 16:32], ones[:, 0:128], M[:, 0, :],
                                                       start=True, stop=False))
                t = PE.do([a, k_upper, free[4]], lambda e: e.matmul(
                    PS[:, 4, h * 16:h * 16 + 16], upper[:, :], M[:, h, :], start=(h == 0), stop=True))
            PE.go([k_ones], lambda e: e.matmul(PS[:, 4, 32:48], ones[:, 0:128], M[:, 0, :], start=True, stop=False))
            t = PE.do([], lambda e: e.matmul(PS[:, 4, 32:48], ones[:, 0:128], M[:, 1, :], start=False, stop=True))
            a = dv([t], lambda e: e.tensor_reduce(fl, PS[:, 4, 32:48], AX, ALU.max))
            tfl = dv([a], lambda e: e.tensor_scalar(it[:, 0:1], fl, float(CAP), None, ALU.is_gt))
            p = dv([t], lambda e: e.tensor_copy(pos, PS[:, 4, 0:32].rearrange("p (h e) -> p h e", h=2)))
            free[4] = [a, p]
            b = dv([p], lambda e: e.tensor_scalar(og, pos, float(CAP), None, ALU.is_ge))
            tog = dv([b, tgate], lambda e: e.tensor_tensor(og, og, gate, ALU.mult))
            b = dv([p], lambda e: e.tensor_scalar(pos, pos, 1.0, None, ALU.add))
            b = dv([b], lambda e: e.tensor_tensor(pos, pos, M, ALU.mult))
            b = dv([b], lambda e: e.tensor_scalar(pos, pos, -1.0, None, ALU.add))
            ts = []
            for h in range(2):
                s = dv([b, k_iota, x_tok], lambda e: e.tensor_tensor(
                    S[:, h, :].rearrange("p (e s) -> p e s", e=16),
                    iota64[:, :].unsqueeze(1).to_broadcast([128, 16, 64]),
                    pos[:, h, :].unsqueeze(2).to_broadcast([128, 16, 64]), ALU.is_equal))
                ts.append(s)

            def gates():
                out = []
                for h in range(2):
                    for i in range(2):
                        for o in range(2):
                            v = (lambda ap, m: ap.rearrange("p (q m s) -> p q m s", q=8, m=2)[:, :, m, :])
                            ga = gate[:, h, :].rearrange("p (q m) -> p q m", m=2)[:, :, o]
                            out.append(dv([ts, tgate], lambda e: e.tensor_tensor(
                                v(Gs[i][:, h, :], o ^ i), v(S[:, h, :], o),
                                ga.unsqueeze(2).to_broadcast([128, 8, 64]), ALU.mult)))
                return out

            xg_tok, xg_free = [None, None], [None, None]
            gt_tok, gt_free = [None, None], [None, None]
            y_free = [None]

            def gather(q):
                i = q % 2
                got = []
                for half in range(2):
                    b = 6 + half
                    for k4 in range(4):
                        k = 4 * half + k4
                        for h in range(2):
                            t = PE.do([ts, x_tok, free[b] if k4 == 0 else None], lambda e: e.matmul(
                                PS[:, b, k4 * 128:k4 * 128 + 128], X[:, h, k * 128:k * 128 + 128],
                                S[:, h, q * 128:q * 128 + 128], start=(h == 0), stop=(h == 1)))
                    src = PS[:, b, :].rearrange("p (k s) -> p k s", k=4)
                    dst = xg[i][:, 4 * half:4 * half + 4, :]
                    if half:
                        free[b] = DV.do([t, xg_free[i]], lambda e: e.tensor_copy(dst, src))
                    else:
                        free[b] = AC.do([t, xg_free[i]], lambda e: e.activation(dst, src, ACT.Copy))
                    got.append(free[b])
                xg_tok[i] = got

            def turn_gates(q):
                i = q % 2
                for h in range(2):
                    for s in range(2):
                        a = (2 * h + s) * 128
                        t = PE.do([gs_tok, free[6]], lambda e: e.transpose(
                            PS[:, 6, a:a + 128], Gs[s][:, h, q * 128:q * 128 + 128], ident[:, :]))
                src = PS[:, 6, :].rearrange("p (h s t) -> p h s t", h=2, s=2)
                free[6] = AC.do([t, gt_free[i]], lambda e: e.activation(Gt[i], src, ACT.Copy))
                gt_tok[i] = free[6]

            def product(name, bank, lhs, lhs_tok, swap):
                for c in range(4):
                    w, w_ok = W.take(name)
                    for kk in range(2):
                        k = 2 * c + kk
                        for half in range(2):
                            a = kk * 1024 + (half ^ swap) * 512
                            f = (lambda e: e.matmul(PS[64 * half:64 * half + 64, bank, :], lhs(k), w[:, a:a + 512],
                                                    start=(k == 0), stop=(k == 7)))
                            wt = [w_ok, lhs_tok, free[bank] if c == 0 else None] if (kk, half) == (0, 0) else []
                            if (kk, half) == (1, 1):
                                t = PE.do(wt, f)
                            else:
                                PE.go(wt, f)
                    W.give(t)
                return t

            def combine(q, y_tok):
                i = q % 2
                for h in range(2):
                    for d in range(2):
                        b = 2 * h + d
                        t = PE.do([y_tok, gt_tok[i], free[b] if q == 0 else None], lambda e: e.matmul(
                            PS[:, b, :], Gt[i][:, h, d, :], Y[d], start=(q == 0), stop=(q == 7)))
                y_free[0] = t
                gt_free[i] = t

            gather(0)
            gs_tok = gates()
            y_tok = []
            h_free = [None, None]
            hh_free = None
            for ex in range(E):
                q, o, i = ex // 2, ex % 2, ex % 2
                xx, xk = xg[q % 2], xg_tok[q % 2]
                lhs = (lambda k: xx[:, k, o * 64:o * 64 + 64])
                t1 = product(f"w1{layer}", 4, lhs, xk, 0)
                a = AC.do([t1], lambda e: e.activation(th, PS[:, 4, :], ACT.Tanh, scale=0.5))
                s = DV.do([a], lambda e: e.scalar_tensor_tensor(
                    out=sl, in0=th, scalar=1.0, in1=PS[:, 4, :], op0=ALU.add, op1=ALU.mult))
                free[4] = s
                t3 = product(f"w3{layer}", 5, lhs, xk, 0)
                if o == 1:
                    xg_free[q % 2] = t3
                hd = DV.do([t3, s, hh_free], lambda e: e.scalar_tensor_tensor(
                    out=hh, in0=sl, scalar=0.5, in1=PS[:, 5, :], op0=ALU.mult, op1=ALU.mult))
                free[5] = hd
                if o == 0 and q > 0:
                    combine(q - 1, y_tok)
                if o == 0:
                    turn_gates(q)
                    y_tok = []
                if o == 1 and q < 7:
                    gather(q + 1)
                for j in range(4):
                    t = PE.do([hd, free[6] if j == 0 else None], lambda e: e.transpose(
                        PS[:, 6, j * 128:j * 128 + 128], hh[:, j * 128:j * 128 + 128], ident[:, :]))
                hh_free = t
                free[6] = AC.do([t, h_free[i]], lambda e: e.activation(hT[i], PS[:, 6, :], ACT.Copy))
                ty = product(f"w2{layer}", 7, (lambda k: hT[i][:, (k % 4) * 128 + (k // 4) * 64:
                                                              (k % 4) * 128 + (k // 4) * 64 + 64]), free[6], o)
                h_free[i] = ty
                e0 = AC.do([ty, y_free[0]], lambda e: e.activation(Y[o][0:64, :], PS[0:64, 7, :], ACT.Copy))
                e1 = DV.do([ty, y_free[0]], lambda e: e.tensor_copy(Y[1 - o][64:128, :], PS[64:128, 7, :]))
                free[7] = [e0, e1]
                y_tok += [e0, e1]
            combine(7, y_tok)
            tz = (PE.sem, PE.n)
            zt = []
            ev = add_residual(X, x_tok, ALPHA, Z, None)
            for h in range(2):
                for d in range(2):
                    free[2 * h + d] = ev(h, d, PS[:, 2 * h + d, :], tz)
                    zt.append(free[2 * h + d])

            everyone = (AC, DV, PL, SP, PE)
            for en in everyone:
                en.wait([zt, tfl, tog])
            flag = nc.values_load(it[0:1, 0:1], min_val=0, max_val=1)
            with nc.If(flag > 0):
                nc.all_engine_barrier()
                with nc.Fori(0, E) as e_i:
                    overflow(layer, og, e_i)
                    nc.all_engine_barrier(sems_to_clear=over_range)
                    nc.all_engine_barrier()
            return zt

        over = [sem(f"s_o{i}") for i in range(5)]
        nums = sorted(s.num for s in over)
        assert nums == list(range(nums[0], nums[0] + 5))
        over_range = range(nums[0], nums[0] + 5)

        def overflow(layer, og, e_i):
            oPE, oAC, oDV, oPL = (Eng(x.e, s) for x, s in zip((PE, AC, DV, PL), over))
            s_w = over[4]
            hid = F[:, 0:2048].rearrange("p (k t) -> p k t", k=8)
            wb = F[:, 2048:4096]
            th = F[:, 4096:4608]
            H = F[:, 4608:6656].rearrange("p (h n) -> p h n", h=2)
            oge = sm[:, 382:384]
            tg = oDV.do([], lambda e: e.tensor_copy(oge, og[:, :, bass.ds(e_i, 1)]))
            n, w_free = 0, None
            sp = Eng(SP.e, s_w)

            def dense(w, bank, lhs, lhs_tok, bank_tok):
                nonlocal n, w_free
                for c in range(4):
                    sp.wait([w_free])
                    sp.e.dma_start(wb, A[w][layer, bass.ds(e_i, 1), c].rearrange("a p n -> (a p) n"))\
                        .then_inc(s_w, 16)
                    n += 1
                    for kk in range(2):
                        k = 2 * c + kk
                        for h in range(2):
                            for d in range(2):
                                t = oPE.do([(s_w, 16 * n), lhs_tok, bank_tok if k == 0 else None],
                                           lambda e: e.matmul(
                                    PS[:, bank + 2 * h + d, :], lhs[:, k, h * 128:h * 128 + 128],
                                    wb[:, kk * 1024 + d * 512:kk * 1024 + d * 512 + 512],
                                    start=(k == 0), stop=(k == 7)))
                    w_free = t
                return t

            t1 = dense("w1", 0, XT, None, None)
            t3 = dense("w3", 4, XT, None, None)
            hd = None
            for h in range(2):
                for d in range(2):
                    b, dst = 2 * h + d, H[:, h, d * 512:d * 512 + 512]
                    a = oAC.do([t1, hd], lambda e: e.activation(th, PS[:, b, :], ACT.Tanh, scale=0.5))
                    s = oDV.do([a], lambda e: e.scalar_tensor_tensor(
                        out=dst, in0=th, scalar=1.0, in1=PS[:, b, :], op0=ALU.add, op1=ALU.mult))
                    hd = oDV.do([t3, s], lambda e: e.scalar_tensor_tensor(
                        out=dst, in0=dst, scalar=0.5, in1=PS[:, 4 + b, :], op0=ALU.mult, op1=ALU.mult))
            got = []
            for q in range(4):
                for j in range(2):
                    k = 2 * q + j
                    for h in range(2):
                        t = oPE.do([hd], lambda e: e.transpose(
                            PS[:, q, j * 256 + h * 128:j * 256 + h * 128 + 128],
                            H[:, h, k * 128:k * 128 + 128], ident[:, :]))
                got.append(oAC.do([t], lambda e: e.activation(
                    hid[:, 2 * q:2 * q + 2, :], PS[:, q, :].rearrange("p (k t) -> p k t", k=2), ACT.Copy)))
            t = dense("w2", 4, hid, got, hd)
            for h in range(2):
                for d in range(2):
                    z = Z[:, h, d * 512:d * 512 + 512]
                    oDV.do([t, tg], lambda e: e.scalar_tensor_tensor(
                        out=z, in0=PS[:, 4 + 2 * h + d, :], scalar=oge[:, h:h + 1], in1=z,
                        op0=ALU.mult, op1=ALU.add))

        def attention_a(xt_ok, x_free):
            qT = fv(2048, 8)
            kT = fv(4096, 8)
            v = F[:, 6144:8192].rearrange("p (h d) -> p h d", h=2)
            s_sb = [F[:, 8192 + i * 384:8576 + i * 384] for i in range(2)]
            p_sb = [F[:, 8960 + i * 384:9344 + i * 384] for i in range(2)]
            pt = [F[:, 9728 + i * 384:10112 + i * 384] for i in range(2)]
            zf, ab, c, nc_, lf = (F[0:16, 10496 + i * 256:10752 + i * 256] for i in range(5))
            cq = sm[:, 0:32].rearrange("p (b h) -> p b h", b=2)
            wf = col("wf").rearrange("p (k n) -> p k n", k=8)
            for k in range(8):
                t = PE.do([xt_ok, free[7]], lambda e: e.matmul(
                    PS[0:16, 7, 0:256], wf[:, k, :], XT[:, k, :], start=(k == 0), stop=(k == 7)))
            a = DV.do([t, bf_ok], lambda e: e.tensor_scalar(zf, PS[0:16, 7, 0:256], bft[:, 0:1], None, ALU.add))
            free[7] = a
            b = AC.do([a], lambda e: e.activation(ab, zf, ACT.Abs))
            b = AC.do([b], lambda e: e.activation(ab, ab, ACT.Exp, scale=-1.0))
            b = DV.do([b], lambda e: e.tensor_scalar(ab, ab, 1.0, None, ALU.add))
            b = AC.do([b], lambda e: e.activation(ab, ab, ACT.Ln))
            b = DV.do([b], lambda e: e.scalar_tensor_tensor(out=lf, in0=zf, scalar=0.0, in1=ab,
                                                            op0=ALU.min, op1=ALU.subtract))
            tc_ = DV.do([b, k_ones], lambda e: e.tensor_tensor_scan(c, ones[0:16, :], lf, 0.0, ALU.mult, ALU.add))
            tn = DV.do([tc_], lambda e: e.tensor_scalar(nc_, c, -1.0, None, ALU.mult))
            for h in range(2):
                t = PE.do([tc_, free[7]], lambda e: e.transpose(
                    PS[:, 7, h * 16:h * 16 + 16], c[:, h * 128:h * 128 + 128], ident[0:16, 0:16]))
            tq = DV.do([t], lambda e: e.tensor_copy(cq, PS[:, 7, 0:32].rearrange("p (b h) -> p b h", b=2)))
            free[7] = tq
            tok = {}

            def evac(c_, ps, t):
                if c_ < 4:
                    tok["q", c_] = DV.do([t], lambda e: e.tensor_scalar(
                        qT[:, 2 * c_:2 * c_ + 2, :], ps, 0.125, None, ALU.mult))
                    return tok["q", c_]
                i = c_ - 4
                tok["k", i] = AC.do([t], lambda e: e.activation(kT[:, 2 * i:2 * i + 2, :], ps, ACT.Copy))
                return tok["k", i]

            proj_features("aw_in", 8, XT, xt_ok, evac, [0, 1, 2, 3, 4, 5])

            def evac_v(c_, ps, t):
                en = AC if c_ % 2 else DV
                dst = v[:, :, c_ * 256:c_ * 256 + 256]
                if c_ % 2:
                    tok["v", c_] = AC.do([t], lambda e: e.activation(dst, ps, ACT.Copy))
                else:
                    tok["v", c_] = DV.do([t], lambda e: e.tensor_copy(dst, ps))
                return tok["v", c_]

            proj_cols("aw_in", 4, XT, xt_ok, evac_v, [0, 1, 2, 3])
            st = {}
            gt = [None] * 8

            def scores(h):
                i, r = h % 2, slice(64 * (h % 2), 64 * (h % 2) + 64)
                b = i
                w = [tok["q", h // 4], tok["k", h // 4], free[b]]
                PE.go(w, lambda e: e.matmul(PS[:, b, 0:128], qT[r, h // 2, 0:128], kT[r, h // 2, 0:128],
                                            start=True, stop=False))
                PE.go([k_ident, tn], lambda e: e.matmul(PS[:, b, 0:128], ident[0:16, h:h + 1].to_broadcast([16, 128]), nc_[:, 0:128],
                                                     start=False, stop=True))
                PE.go([], lambda e: e.matmul(PS[:, b, 128:384], qT[r, h // 2, 128:256], kT[r, h // 2, :],
                                             start=True, stop=False))
                t = PE.do([], lambda e: e.matmul(PS[:, b, 128:384], ident[0:16, h:h + 1].to_broadcast([16, 128]), nc_, start=False, stop=True))
                s, p = s_sb[i], p_sb[i]
                sc = sm[:, 64 + 16 * i:80 + 16 * i]
                a0 = DV.do([t, tq, k_cmask, st.get(("e", h - 2))], lambda e: e.scalar_tensor_tensor(
                    out=s[:, 0:128], in0=PS[:, b, 0:128], scalar=cq[:, 0, h:h + 1], in1=cmask[:, 128:256],
                    op0=ALU.add, op1=ALU.add))
                a1 = DV.do([], lambda e: e.scalar_tensor_tensor(
                    out=s[:, 128:384], in0=PS[:, b, 128:384], scalar=cq[:, 1, h:h + 1], in1=cmask[:, :],
                    op0=ALU.add, op1=ALU.add))
                free[b] = a1
                m0 = DV.do([a0], lambda e: e.tensor_reduce(sc[:, 0:1], s[:, 0:128], AX, ALU.max))
                m1 = DV.do([a1], lambda e: e.tensor_reduce(sc[:, 1:2], s[:, 128:384], AX, ALU.max))
                ng = DV.do([m0, m1], lambda e: e.tensor_scalar(sc[:, 2:4], sc[:, 0:2], -1.0, None, ALU.mult))
                e0 = AC.do([ng, st.get(("t", h - 2))], lambda e: e.activation(
                    p[:, 0:128], s[:, 0:128], ACT.Exp, bias=sc[:, 2:3], accum_out=sc[:, 4:5]))
                e1 = AC.do([], lambda e: e.activation(
                    p[:, 128:384], s[:, 128:384], ACT.Exp, bias=sc[:, 3:4], accum_out=sc[:, 5:6]))
                st["e", h] = e1
                rc = DV.do([e0, e1], lambda e: e.reciprocal(sc[:, 6:8], sc[:, 4:6]))
                n0 = DV.do([rc], lambda e: e.tensor_scalar(p[:, 0:128], p[:, 0:128], sc[:, 6:7], None, ALU.mult))
                n1 = DV.do([rc], lambda e: e.tensor_scalar(p[:, 128:384], p[:, 128:384], sc[:, 7:8], None, ALU.mult))
                st["p", h] = [n0, n1]

            def turn(h):
                i, b = h % 2, 2 + h % 2
                for n in range(3):
                    t = PE.do([st["p", h], free[b] if n == 0 else None], lambda e: e.transpose(
                        PS[:, b, n * 128:n * 128 + 128], p_sb[i][:, n * 128:n * 128 + 128], ident[:, :]))
                st["t", h] = t
                free[b] = AC.do([t, st.get(("o", h - 2))], lambda e: e.activation(pt[i], PS[:, b, 0:384], ACT.Copy))
                st["pt", h] = free[b]

            def values(h):
                i, b = h % 2, 4 + (h // 2) % 2
                r = slice(64 * i, 64 * i + 64)
                PE.go([st["pt", h], [tok["v", n] for n in range(4)], free[b] if i == 0 else None],
                      lambda e: e.matmul(PS[r, b, 0:256], v[:, 0, h * 64:h * 64 + 64], pt[i][:, 0:256],
                                         start=True, stop=False))
                t = PE.do([], lambda e: e.matmul(PS[r, b, 128:256], v[:, 1, h * 64:h * 64 + 64],
                                                 pt[i][:, 256:384], start=False, stop=True))
                st["o", h] = t
                if i:
                    free[b] = AC.do([t, x_free], lambda e: e.activation(GT[:, h // 2, :], PS[:, b, 0:256], ACT.Copy))
                    gt[h // 2] = free[b]

            for i in range(18):
                if i < 16:
                    scores(i)
                if 1 <= i <= 16:
                    turn(i - 1)
                if i >= 2:
                    values(i - 2)
            return gt

        def ffn(layer, xt_ok, gt_free):
            G = fv(0, 22)
            acc = [[F[:, 5632 + (2 * i + s) * 512:6144 + (2 * i + s) * 512].rearrange("p (k t) -> p k t", k=2)
                    for s in range(2)] for i in range(2)]
            th = [F[:, 7680 + i * 512:8192 + i * 512].rearrange("p (k t) -> p k t", k=2) for i in range(2)]
            cw = col(f"fcw{layer}").rearrange("p (c k) -> p c k", c=44)
            cb = col(f"fcb{layer}")
            gt = [None] * 22
            done = {}
            st = {}

            def evac(n, ps, t):
                pair, side = n // 2, n % 2
                i = pair % 2
                dst = acc[i][side]
                tt = []
                first = (22 if side == 0 else 0) + 2 * pair
                for j in range(2):
                    ch = first + j
                    a = AC.do([t, c_ok, st.get(pair - 2), gt_free], lambda e: e.activation(
                        dst[:, j, :], ps[:, j, :], ACT.Identity, scale=cw[:, ch, 2:3], bias=cb[:, ch:ch + 1]))
                for j in range(2):
                    ch = first + j
                    b = DV.do([a], lambda e: e.scalar_tensor_tensor(
                        out=dst[:, j, 1:256], in0=ps[:, j, 0:255], scalar=cw[:, ch, 1:2],
                        in1=dst[:, j, 1:256], op0=ALU.mult, op1=ALU.add))
                    b = DV.do([b], lambda e: e.scalar_tensor_tensor(
                        out=dst[:, j, 2:256], in0=ps[:, j, 0:254], scalar=cw[:, ch, 0:1],
                        in1=dst[:, j, 2:256], op0=ALU.mult, op1=ALU.add))
                    tt.append(b)
                if side == 0:
                    a = AC.do([tt], lambda e: e.activation(th[i], dst, ACT.Tanh, scale=0.5))
                    done[pair] = PL.do([a], lambda e: e.tensor_scalar(th[i], th[i], 0.5, 0.5, ALU.mult, ALU.add))
                    done[pair] = PL.do([done[pair]], lambda e: e.tensor_tensor(dst, dst, th[i], ALU.mult))
                else:
                    g = DV.do([tt, done[pair], gt_free], lambda e: e.tensor_tensor(
                        G[:, 2 * pair:2 * pair + 2, :], acc[i][0], dst, ALU.mult))
                    gt[2 * pair] = gt[2 * pair + 1] = g
                    st[pair] = g
                return tt

            proj_features(f"up{layer}", 22, XT, xt_ok, evac, [4, 5, 6, 7])
            proj_out(f"down{layer}", 22, G, gt, add_residual(X, None, 1.0, X, None))
            return [free[b] for b in range(4)]

        def attention_b(x_tok):
            XT2 = fv(0, 8)
            kT = fv(2048, 12)
            v = F[:, 5120:8192].rearrange("p (h d) -> p h d", h=2)
            qT = fv(8192, 12)
            p_sb = [F[:, 11264 + i * 384:11648 + i * 384] for i in range(6)]
            n_ok = rms_scale(X, x_tok, Z, None)
            g0, g1 = col("kvg"), col("mixg1")

            def evac2(q, ps, t):
                tt = []
                for j in range(2):
                    k = 2 * q + j
                    tt.append(AC.do([t, x_tok, c_ok], lambda e: e.activation(
                        XT[:, k, :], ps[:, j, :], ACT.Copy, scale=g0[:, k:k + 1])))
                for j in range(2):
                    k = 2 * q + j
                    tt.append(DV.do([t, x_tok, c_ok, tt[1]], lambda e: e.tensor_scalar(
                        XT2[:, k, :], ps[:, j, :], g1[:, k:k + 1], None, ALU.mult)))
                return tt

            xt_ok = to_features(Z, n_ok, evac2)
            dist = Z[:, 0, 0:768].rearrange("p (g n) -> p g n", g=3)
            di = Z[:, 0, 768:1024].bitcast(I32)
            dm = Z[:, 1, 768:1024]
            pt = [Z[:, 1, i * 384:i * 384 + 384] for i in range(2)]
            t = PL.do([xt_ok], lambda e: e.iota(di, pattern=[[-1, 256]], base=128, channel_multiplier=1))
            t0 = DV.do([t], lambda e: e.tensor_copy(dm, di))
            dd = []
            for g, mask in ((1, 3), (2, 15)):
                a = DV.do([t, dd], lambda e: e.tensor_scalar(
                    sm[:, 0:256].bitcast(I32), di, mask, None, ALU.bitwise_and))
                a = DV.do([a], lambda e: e.tensor_scalar(
                    dist[:, g, :], sm[:, 0:256].bitcast(I32), 0.0, -NEG, ALU.is_gt, ALU.mult))
                dd.append(DV.do([a, t0], lambda e: e.tensor_tensor(dist[:, g, :], dist[:, g, :], dm, ALU.add)))
            d0 = PL.do([t0], lambda e: e.affine_select(
                out=dist[:, 0, :], in_=dm, compare_op=ALU.is_ge, fill=-NEG, base=0,
                pattern=[[1, 256]], channel_multiplier=-1))
            dist_ok = []
            for g in range(3):
                dist_ok.append(PL.do([d0, dd], lambda e: e.affine_select(
                    out=dist[:, g, :], in_=dist[:, g, :], compare_op=ALU.is_ge, fill=-NEG, base=128,
                    pattern=[[-1, 256]], channel_multiplier=1)))
            tok = {}

            def evac_k(c, ps, t):
                if c % 2:
                    tok["k", c] = DV.do([t], lambda e: e.tensor_copy(kT[:, 2 * c:2 * c + 2, :], ps))
                else:
                    tok["k", c] = AC.do([t], lambda e: e.activation(kT[:, 2 * c:2 * c + 2, :], ps, ACT.Copy))
                return tok["k", c]

            def evac_v(c, ps, t):
                dst = v[:, :, c * 256:c * 256 + 256]
                if c % 2:
                    tok["v", c] = DV.do([t], lambda e: e.tensor_copy(dst, ps))
                else:
                    tok["v", c] = AC.do([t], lambda e: e.activation(dst, ps, ACT.Copy))
                return tok["v", c]

            def evac_q(c, ps, t):
                tok["q", c] = DV.do([t], lambda e: e.tensor_scalar(
                    qT[:, 2 * c:2 * c + 2, :], ps, 0.125, None, ALU.mult))
                return tok["q", c]

            proj_features("wkv", 6, XT, xt_ok, evac_k, [0, 1, 2, 3])
            proj_cols("wkv", 6, XT, xt_ok, evac_v, [4, 5, 6, 7])
            proj_features("bwq", 6, XT2, xt_ok, evac_q, [0, 1, 2, 3])
            st = {}
            gt = [None] * 4

            def stat(h, i):
                a = 256 + 64 * (h % 2) + 6 * i
                return sm[:, a:a + 6]

            def scores(n):
                h, g, b = n // 3, n % 3, n % 2
                tile, r = 4 * g + h // 2, slice(64 * (h % 2), 64 * (h % 2) + 64)
                s, slope = p_sb[n % 6], 2.0 ** (-8.0 * (8 * g + h + 1) / 24)
                w = [tok["q", tile // 2], tok["k", tile // 2], free[b]]
                PE.go(w, lambda e: e.matmul(PS[:, b, 0:128], qT[r, tile, 0:128], kT[r, tile, 0:128],
                                            start=True, stop=True))
                t = PE.do([], lambda e: e.matmul(PS[:, b, 128:384], qT[r, tile, 128:256], kT[r, tile, :],
                                                 start=True, stop=True))
                prev = st.get(("t", n - 6))
                a0 = DV.do([t, dist_ok, prev, st.get(("c", h - 2))], lambda e: e.scalar_tensor_tensor(
                    out=s[:, 0:128], in0=dist[:, g, 128:256], scalar=-slope, in1=PS[:, b, 0:128],
                    op0=ALU.mult, op1=ALU.add))
                a1 = DV.do([], lambda e: e.scalar_tensor_tensor(
                    out=s[:, 128:384], in0=dist[:, g, :], scalar=-slope, in1=PS[:, b, 128:384],
                    op0=ALU.mult, op1=ALU.add))
                free[b] = a1
                mx, ng, ls = stat(h, 0), stat(h, 1), stat(h, 2)
                i = 2 * g
                m0 = DV.do([a0], lambda e: e.tensor_reduce(mx[:, i:i + 1], s[:, 0:128], AX, ALU.max))
                m1 = DV.do([a1], lambda e: e.tensor_reduce(mx[:, i + 1:i + 2], s[:, 128:384], AX, ALU.max))
                nn = DV.do([m0, m1], lambda e: e.tensor_scalar(ng[:, i:i + 2], mx[:, i:i + 2], -1.0, None, ALU.mult))
                AC.do([nn], lambda e: e.activation(
                    s[:, 0:128], s[:, 0:128], ACT.Exp, bias=ng[:, i:i + 1], accum_out=ls[:, i:i + 1]))
                st["e", n] = AC.do([], lambda e: e.activation(
                    s[:, 128:384], s[:, 128:384], ACT.Exp, bias=ng[:, i + 1:i + 2], accum_out=ls[:, i + 1:i + 2]))

            def weigh(h):
                mx, ls, lse, cf, il = stat(h, 0), stat(h, 2), stat(h, 3), stat(h, 4), stat(h, 5)
                tm = stat(h, 6)
                by_q = (lambda ap: ap.rearrange("p (g q) -> p q g", q=2))
                over_g = (lambda ap: ap.unsqueeze(1).to_broadcast([128, 3, 2]))
                as_g = (lambda ap: ap.rearrange("p (g q) -> p g q", q=2))
                e = [st["e", 3 * h + g] for g in range(3)]
                a = AC.do([e, st.get(("c", h - 2))], lambda e: e.activation(lse, ls, ACT.Ln))
                a = DV.do([a], lambda e: e.tensor_tensor(lse, lse, mx, ALU.add))
                a = DV.do([a], lambda e: e.tensor_reduce(tm[:, 0:2], by_q(lse), AX, ALU.max))
                a = DV.do([a], lambda e: e.tensor_tensor(as_g(lse), as_g(lse), over_g(tm[:, 0:2]), ALU.subtract))
                a = AC.do([a], lambda e: e.activation(cf, lse, ACT.Exp))
                b = DV.do([a], lambda e: e.tensor_reduce(tm[:, 2:4], by_q(cf), AX, ALU.add))
                c = DV.do([b], lambda e: e.tensor_tensor(as_g(il), as_g(ls), over_g(tm[:, 2:4]), ALU.mult))
                c = DV.do([c], lambda e: e.reciprocal(il, il))
                c = DV.do([c], lambda e: e.tensor_tensor(cf, cf, il, ALU.mult))
                st["c", h] = c
                for g in range(3):
                    p, n = p_sb[(3 * h + g) % 6], 3 * h + g
                    n0 = DV.do([c], lambda e: e.tensor_scalar(
                        p[:, 0:128], p[:, 0:128], cf[:, 2 * g:2 * g + 1], None, ALU.mult))
                    n1 = DV.do([c], lambda e: e.tensor_scalar(
                        p[:, 128:384], p[:, 128:384], cf[:, 2 * g + 1:2 * g + 2], None, ALU.mult))
                    st["p", n] = [n0, n1]

            def turn(n):
                i, b = n % 2, 2 + n % 2
                for m in range(3):
                    t = PE.do([st["p", n], free[b] if m == 0 else None], lambda e: e.transpose(
                        PS[:, b, m * 128:m * 128 + 128], p_sb[n % 6][:, m * 128:m * 128 + 128], ident[:, :]))
                st["t", n] = t
                free[b] = AC.do([t, st.get(("o", n - 2)), xt_ok], lambda e: e.activation(
                    pt[i], PS[:, b, 0:384], ACT.Copy))
                st["pt", n] = free[b]

            def values(n):
                h, g, i = n // 3, n % 3, n % 2
                b = 4 + (h // 2) % 2
                r = slice(64 * (h % 2), 64 * (h % 2) + 64)
                c0 = g * 512 + h * 64
                vt = [tok["v", m] for m in range(6)]
                PE.go([st["pt", n], vt, free[b] if (h % 2, g) == (0, 0) else None],
                      lambda e: e.matmul(PS[r, b, 0:256], v[:, 0, c0:c0 + 64], pt[i][:, 0:256],
                                         start=(g == 0), stop=False))
                t = PE.do([], lambda e: e.matmul(PS[r, b, 128:256], v[:, 1, c0:c0 + 64],
                                                 pt[i][:, 256:384], start=False, stop=(g == 2)))
                st["o", n] = t
                if (h % 2, g) == (1, 2):
                    free[b] = AC.do([t], lambda e: e.activation(GT[:, h // 2, :], PS[:, b, 0:256], ACT.Copy))
                    gt[h // 2] = free[b]

            for i in range(24 + 5):
                if i < 24:
                    scores(i)
                    if i % 3 == 2:
                        weigh(i // 3)
                if 4 <= i < 28:
                    turn(i - 4)
                if i >= 5:
                    values(i - 5)
            return gt

        def banks():
            return [free[b] for b in range(4)]

        def second_block(x_tok):
            for layer in range(2):
                if layer == 0:
                    n_ok = rms_scale(X, x_tok, Z, x_tok)
                    xt_ok = to_features(Z, n_ok, scaled_xt(XT, "mixg0", n_ok))
                    gt = attention_a(xt_ok, None)
                    proj_out("aw_out", 8, GT, gt, add_residual(X, x_tok, 1.0, X, None))
                else:
                    gt = attention_b(x_tok)
                    proj_out("bw_out", 4, GT, gt, add_residual(X, x_tok, 1.0, X, None))
                x_tok = banks()
                if dbg == f"att{layer}":
                    return x_tok
                n_ok = rms_scale(X, x_tok, Z, x_tok)
                xt_ok = to_features(Z, n_ok, scaled_xt(XT, f"ffng{layer}", n_ok))
                ffn(layer, xt_ok, xt_ok)
                x_tok = banks()
                if dbg == f"ffn{layer}":
                    return x_tok
            n_ok = rms_scale(X, x_tok, Z, x_tok)
            gr, g_ok = row("final")
            return [(DV if h else PL).do([n_ok, g_ok], lambda e: e.tensor_tensor(
                X[:, h, :], Z[:, h, :], gr, ALU.mult)) for h in range(2)]

        def first_block():
            gt = even_mixer()
            want_row("ln1_g0")
            want_row("ln1_b0")
            proj_out("ew_out", 8, GT, gt, add_residual(X, x_ok, ALPHA, Z, None))
            zt = banks()
            for layer in range(2):
                x1 = layer_norm(Z, zt, f"ln1_g{layer}", f"ln1_b{layer}", X, zt)
                want_row(f"ln2_g{layer}")
                want_row(f"ln2_b{layer}")
                xt_ok = to_features(X, x1, copy_xt(XT, x1))
                if dbg == f"x1_{layer}":
                    return x1
                zt = moe(layer, x1, xt_ok)
                x2 = layer_norm(Z, zt, f"ln2_g{layer}", f"ln2_b{layer}", X, zt)
                if dbg == f"x2_{layer}":
                    return x2
                if layer == 0:
                    want_row("ln1_g1")
                    want_row("ln1_b1")
                    xt_ok = to_features(X, x2, copy_xt(XT, x2))
                    gt = odd_mixer(xt_ok)
                    proj_out("ow_out", 8, GT, gt, add_residual(X, x2, ALPHA, Z, x2))
                    zt = banks()
            want_row("final")
            return x2

        if dbg and dbg.startswith(("att", "ffn", "all")):
            W.used = 0
            x2 = x_ok
            want_row("final")
            fin = second_block(x_ok)
        else:
            fin = first_block()
            if not dbg:
                fin = second_block(fin)
        SP.wait([fin])
        if dbg:
            for n in range(min(2, rows_used[0])):
                SP.e.wait_ge(s_row[n], 16 * ((rows_used[0] - n + 1) // 2))
            for n in range(RING):
                SP.e.wait_ge(ring_sems[n], 16 * ((min(W.used + RING, len(plan)) + RING - 1 - n) // RING))
        SP.e.dma_start(out.rearrange("(h p) d -> p h d", p=128), X[:, :, :]).then_inc(s_out, 16)
        SP.e.wait_ge(s_out, 16)


def _cols(w):
    k, n = w.shape
    return w.reshape(k // 128, 128, n // 256, 256).transpose(2, 1, 0, 3).reshape(n // 256, 128, -1)


def _rows(w):
    k, n = w.shape
    return w.reshape(k // 256, 2, 128, n).transpose(0, 2, 1, 3).reshape(k // 256, 128, 2 * n)


def _feat(v):
    v = v.reshape(-1, v.shape[-1])
    return v.reshape(v.shape[0], -1, 128).transpose(2, 1, 0).reshape(128, -1)


def layout(i):
    c = np.ascontiguousarray
    a = {}
    a["x"] = i["x"][0]
    parts = {
        "a_dw": _feat(i["even_a_dw"][0]), "a_dw_b": _feat(i["even_a_dw_b"]), "a_ln_g": _feat(i["even_a_ln_g"]),
        "a_ln_b": _feat(i["even_a_ln_b"]), "b_dw": _feat(i["even_b_dw"][0]), "c_dw": _feat(i["odd_c_dw"][0]),
        "c_dw_b": _feat(i["odd_c_dw_b"]), "bga": _feat(i["odd_b_gate_a"].reshape(1, -1)),
        "bgx": _feat(i["odd_b_gate_x"].reshape(1, -1)), "lam": _feat(i["odd_lam"]),
        "mixg0": _feat(i["mix_norm_g_2"][0:1]), "mixg1": _feat(i["mix_norm_g_2"][1:2]),
        "kvg": _feat(i["kv_norm_g_2"].reshape(1, -1)),
        "ffng0": _feat(i["ffn_norm_g_2"][0:1]), "ffng1": _feat(i["ffn_norm_g_2"][1:2]),
        "fcw0": _feat(i["ffn_conv_w_2"][0]), "fcw1": _feat(i["ffn_conv_w_2"][1]),
        "fcb0": _feat(i["ffn_conv_b_2"][0:1]), "fcb1": _feat(i["ffn_conv_b_2"][1:2]),
        "wr": i["w_router"].reshape(8, 128, 16).transpose(1, 0, 2).reshape(128, 128),
        "wf": i["a_w_in_2"][0][:, 3072:].reshape(8, 128, 16).transpose(1, 0, 2).reshape(128, 128),
    }
    for n, (at, w) in COLS.items():
        assert parts[n].shape == (128, w), n
    a["cols"] = c(np.concatenate([parts[n] for n in COLS], axis=1))
    a["b_router_rows"] = c(np.broadcast_to(i["b_router"], (128, 16)))
    a["a_b_f"] = c(i["a_b_f_2"].reshape(16, 1))
    a["rows"] = c(np.stack([i["ln1_g"][0], i["ln1_b"][0], i["ln2_g"][0], i["ln2_b"][0], i["ln1_g"][1],
                            i["ln1_b"][1], i["ln2_g"][1], i["ln2_b"][1], i["final_norm_g_2"]]))
    a["even_w_in"] = c(_cols(i["even_w_in"][0]))
    a["even_w_out"] = c(_rows(i["even_w_out"][0]))
    a["odd_w_in"] = c(_cols(i["odd_w_in"][0]))
    a["odd_w_out"] = c(_rows(i["odd_w_out"][0]))
    g = np.stack([i["odd_w_gate_a"][0], i["odd_w_gate_x"][0]])
    a["odd_gates"] = c(g.reshape(2, 4, 2, 128, 256).transpose(0, 3, 1, 2, 4).reshape(2, 128, 2048))
    for k, n in (("w1", "moe_w1"), ("w3", "moe_w3"), ("w2", "moe_w2")):
        w = i[n]
        a[k] = c(w.reshape(2, 16, 4, 2, 128, 1024).transpose(0, 1, 2, 4, 3, 5).reshape(2, 16, 4, 128, 2048))
    a["a_w_in"] = c(_cols(i["a_w_in_2"][0][:, :3072]))
    a["a_w_out"] = c(_rows(i["a_w_out_2"][0]))
    a["w_kv"] = c(_cols(i["w_kv_2"]))
    a["b_w_q"] = c(_cols(i["b_w_q_2"][0]))
    a["b_w_out"] = c(_rows(i["b_w_out_2"][0]))
    up = [_cols(i["ffn_w_up_2"][n]) for n in range(2)]
    order = [x for p in range(11) for x in (11 + p, p)]
    a["ffn_up"] = c(np.stack([u[order] for u in up]))
    a["ffn_down"] = c(np.stack([_rows(i["ffn_w_down_2"][n]) for n in range(2)]))
    return a


def build(nc, shapes, dbg=None):
    A = {n: nc.dram_tensor(f"in_{n}", s, F32, kind="ExternalInput").ap() for n, s in shapes.items()}
    out = nc.dram_tensor("out_y", (T, D), F32, kind="ExternalOutput").ap()
    program(nc, A, out, dbg)


def kernel(**inputs):
    import concourse.bacc as _bacc
    from concourse.bass_utils import run_bass_kernel_spmd as _run

    arrays = layout({k: np.asarray(v) for k, v in inputs.items()})
    nc = _bacc.Bacc("TRN2", target_bir_lowering=False, num_devices=1)
    build(nc, {n: v.shape for n, v in arrays.items()})
    r = _run(nc, [{f"in_{n}": v for n, v in arrays.items()}], core_ids=[0])
    return r.results[0]["out_y"].reshape(1, T, D)
```

```python
from contextlib import ExitStack
import math

import numpy as np

import concourse.bass as bass
from concourse import mybir

F32 = mybir.dt.float32
F32R = mybir.dt.float32r
I32 = mybir.dt.int32
ALU = mybir.AluOpType
ACT = mybir.ActivationFunctionType
AX = mybir.AxisListType.X

T, D, NT, KD = 256, 1024, 2, 8
E, CAP = 16, 64
ALPHA = 4.0 ** 0.25
LN_EPS, RMS_EPS = 1e-5, 1e-6
RING = 9
PIECE, NPIECE = 512, 4
LAG = 5
CH = 2048
NEG = -1e30

COLS = {}
_at = 0
for _n, _w in (("a_dw", 4 * 31), ("a_dw_b", 4), ("a_ln_g", 4), ("a_ln_b", 4), ("b_dw", 4 * 3),
               ("c_dw", 8 * 4), ("c_dw_b", 8), ("bga", 8), ("bgx", 8), ("lam", 8),
               ("mixg0", 8), ("mixg1", 8), ("kvg", 8), ("ffng0", 8), ("ffng1", 8),
               ("fcw0", 44 * 3), ("fcw1", 44 * 3), ("fcb0", 44), ("fcb1", 44),
               ("lng0", 8), ("lnb0", 8), ("lng1", 8), ("lnb1", 8), ("lng2", 8), ("lnb2", 8), ("wr", 8 * 16), ("wf", 8 * 16)):
    COLS[_n] = (_at, _w)
    _at += _w
NCOLS = _at
ROWS = ("ln2_g1", "ln2_b1", "final")


class Eng:

    def __init__(self, engine, sem):
        self.e, self.sem, self.n, self.seen = engine, sem, 0, {}

    def wait(self, toks):
        for t in toks:
            if t is None:
                continue
            if isinstance(t, list):
                self.wait(t)
                continue
            sem, val = t
            if self.seen.get(sem.name, 0) < val:
                self.e.wait_ge(sem, val)
                self.seen[sem.name] = val

    def do(self, toks, fn):
        self.wait(toks)
        fn(self.e).then_inc(self.sem, 1)
        self.n += 1
        return (self.sem, self.n)

    def go(self, toks, fn):
        self.wait(toks)
        fn(self.e)


class Stream:

    def __init__(self, sp, ring, sems, plan):
        self.sp, self.ring, self.sems, self.plan = sp, ring, sems, plan
        self.used = 0
        for n in range(RING):
            self.load(n, None)

    def load(self, n, freed):
        if n < len(self.plan):
            s = n % RING
            self.sp.wait([freed])
            src = self.plan[n][1]
            self.sp.e.dma_start(self.ring[:, s, 0:src.shape[-1]], src).then_inc(self.sems[s], 16)

    def take(self, name):
        n = self.used
        assert self.plan[n][0] == name, (self.plan[n][0], name)
        self.used += 1
        return self.ring[:, n % RING, :], (self.sems[n % RING], 16 * (n // RING + 1))

    def give(self, tok):
        self.load(self.used - 1 + RING, tok)


def program(nc, A, out, dbg=None):
    ctx = ExitStack()
    with ctx:
        def sb(name, shape, dt=F32):
            return ctx.enter_context(nc.sbuf_tensor(name, shape, dt))

        def sem(name):
            return ctx.enter_context(nc.semaphore(name))

        PE = Eng(nc.tensor, sem("s_pe"))
        AC = Eng(nc.scalar, sem("s_act"))
        DV = Eng(nc.vector, sem("s_dve"))
        PL = Eng(nc.gpsimd, sem("s_pool"))
        SP = Eng(nc.sync, sem("s_sp"))
        ring_sems = [sem(f"s_w{i}") for i in range(RING)]
        s_c, s_x, s_br, s_bf, s_out = sem("s_c"), sem("s_x"), sem("s_br"), sem("s_bf"), sem("s_out")
        s_row = [sem("s_row0"), sem("s_row1")]

        ring = sb("ring", [128, RING, CH])
        PS = ctx.enter_context(nc.psum_tensor("PS", [128, 8, 512], F32))
        cols = sb("cols", [128, NCOLS])
        X = sb("X", [128, NT, D])
        Z = sb("Z", [128, NT, D])
        XT = sb("XT", [128, KD, T])
        rowbuf = sb("rowbuf", [128, 2, D])
        F = sb("F", [128, 14080])
        GT = F[:, 0:2048].rearrange("p (k t) -> p k t", k=8)
        ident = sb("ident", [128, 128])
        ones = sb("ones", [128, 256])
        mean512 = sb("mean512", [128, 128])
        upper = sb("upper", [128, 128])
        iota64 = sb("iota64", [128, 64])
        cmask = sb("cmask", [128, 256])
        mhalf = sb("mhalf", [128, 2])
        brt = sb("brt", [128, 16])
        bft = sb("bft", [16, 1])
        wh = sb("wh", [128, NPIECE, PIECE], F32R)
        wl = sb("wl", [128, NPIECE, PIECE], F32R)
        xh = sb("xh", [128, KD, T], F32R)
        xl = sb("xl", [128, KD, T], F32R)
        nc2 = sb("nc2", [128, 2, 384], F32R)
        nch, ncl = nc2[:, 0, :], nc2[:, 1, :]
        wfh = sb("wfh", [128, 128], F32R)
        wfl = sb("wfl", [128, 128], F32R)
        identr = sb("identr", [128, 16], F32R)
        sm = sb("sm", [128, 512])
        it = sb("it", [128, 8], I32)

        def col(name):
            a, w = COLS[name]
            return cols[:, a:a + w]

        def fv(a, k, t=T):
            return F[:, a:a + k * t].rearrange("p (k t) -> p k t", k=k)

        AC.e.dma_start(X[:, :, :], A["x"].rearrange("(h p) d -> p h d", p=128)).then_inc(s_x, 16)
        AC.e.dma_start(cols[:, :], A["cols"]).then_inc(s_c, 16)
        AC.e.dma_start(brt[:, :], A["b_router_rows"]).then_inc(s_br, 16)
        AC.e.dma_start(bft[:, :], A["a_b_f"]).then_inc(s_bf, 16)
        c_ok, x_ok, br_ok, bf_ok = (s_c, 16), (s_x, 16), (s_br, 16), (s_bf, 16)

        t0 = PL.do([], lambda e: e.memset(ident[:, :], 0.0))
        k_ident = PL.do([t0], lambda e: e.affine_select(
            out=ident[:, :], in_=ident[:, :], compare_op=ALU.not_equal, fill=1.0, base=0,
            pattern=[[-1, 128]], channel_multiplier=1))
        k_identr = PL.do([k_ident], lambda e: e.tensor_copy(identr[:, :], ident[:, 0:16]))
        k_ones = PL.do([], lambda e: e.memset(ones[:, :], 1.0))
        k_mean = PL.do([], lambda e: e.memset(mean512[:, :], 1.0 / 512))
        k_mhalf = PL.do([], lambda e: e.memset(mhalf[:, :], -0.5))
        t0 = PL.do([], lambda e: e.memset(upper[:, :], 1.0))
        k_upper = PL.do([t0], lambda e: e.affine_select(
            out=upper[:, :], in_=upper[:, :], compare_op=ALU.is_gt, fill=0.0, base=0,
            pattern=[[1, 128]], channel_multiplier=-1))
        k_iota = PL.do([], lambda e: e.iota(iota64[:, :], pattern=[[1, 64]], base=1, channel_multiplier=0,
                                            allow_small_or_imprecise_dtypes=True))
        t0 = PL.do([], lambda e: e.memset(cmask[:, :], 0.0))
        k_cmask = PL.do([t0], lambda e: e.affine_select(
            out=cmask[:, :], in_=cmask[:, :], compare_op=ALU.is_ge, fill=NEG, base=128,
            pattern=[[-1, 256]], channel_multiplier=1))
        plan = []

        def add(name, ap, order, split=True):
            for c in order:
                plan.append((name, ap[c], split))

        def add_moe(layer):
            for e in range(E):
                for w in ("w1", "w3", "w2"):
                    add(f"{w}{layer}", A[w][layer, e], range(4), False)

        add("ew_in", A["even_w_in"], [2, 3, 0, 1, 6, 7, 8, 9, 4, 5])
        add("ew_out", A["even_w_out"], range(4))
        add_moe(0)
        add("ow_in", A["odd_w_in"], [4, 5, 6, 7, 0, 1, 2, 3])
        add("gates", A["odd_gates"], range(2), False)
        add("ow_out", A["odd_w_out"], range(4))
        add_moe(1)
        add("aq_in", A["a_w_in"], range(8))
        add("av_in", A["a_w_v"], range(4))
        add("aw_out", A["a_w_out"], range(4))
        add("up0", A["ffn_up"][0], range(22))
        add("down0", A["ffn_down"][0], range(11))
        add("wk", A["w_k"], range(6))
        add("wv", A["w_v"], range(6))
        add("bwq", A["b_w_q"], range(6))
        add("bw_out", A["b_w_out"], range(2))
        add("up1", A["ffn_up"][1], range(22))
        add("down1", A["ffn_down"][1], range(11))
        if dbg and dbg.startswith(("att", "ffn", "all")):
            plan = plan[[n for n, _, _ in plan].index("aq_in"):]
        W = Stream(SP, ring, ring_sems, plan)

        free = [None] * 8
        rows_used = [0]
        row_free = [None, None]
        loaded = {}

        def want_row(name):
            n = rows_used[0]
            rows_used[0] += 1
            AC.wait([row_free[n % 2]])
            AC.e.dma_start(rowbuf[:, n % 2, :], A["rows"][ROWS.index(name), :].partition_broadcast(128)).then_inc(s_row[n % 2], 16)
            loaded[name] = (n % 2, (s_row[n % 2], 16 * (n // 2 + 1)))

        def row(name):
            return rowbuf[:, loaded[name][0], :], loaded[name][1]

        def row_done(name, toks):
            row_free[loaded[name][0]] = toks

        def f32(ap):
            return ap.bitcast(F32)

        pieces = []
        piece_free = [None] * NPIECE
        state = {"issued": 0, "at": CH, "chunk": None}

        def dense_next():
            return W.used < len(plan) and plan[W.used][2]

        def ahead():
            while len(pieces) < NPIECE and (state["at"] < CH or dense_next()):
                if state["at"] == CH:
                    state["name"] = plan[W.used][0]
                    state["chunk"] = W.take(state["name"])
                    state["at"] = 0
                w, w_ok = state["chunk"]
                src = w[:, state["at"]:state["at"] + PIECE]
                i = state["issued"] % NPIECE
                state["issued"] += 1
                state["at"] += PIECE
                a = AC.do([w_ok, piece_free[i]], lambda e: e.activation(wh[:, i, :], src, ACT.Copy))
                b = DV.do([a], lambda e: e.tensor_tensor(wl[:, i, :], src, f32(wh[:, i, :]), ALU.subtract))
                if state["at"] == CH:
                    W.give(b)
                pieces.append((state["name"], i, b))

        def piece(name, n=0):
            got, i, tok = pieces[n]
            assert got == name, (got, name)
            return wh[:, i, :], wl[:, i, :], tok

        def piece_done(tok):
            piece_free[pieces.pop(0)[1]] = tok
            ahead()

        def mm3(out, lt, rt, toks, first, last, mark):
            PE.go(toks, lambda e: e.matmul(out, lt[1], rt[0], start=first, stop=False))
            PE.go([], lambda e: e.matmul(out, lt[0], rt[1], start=False, stop=False))
            f = (lambda e: e.matmul(out, lt[0], rt[0], start=False, stop=last))
            return PE.do([], f) if mark else PE.go([], f)

        x_free = [None] * 4

        def split_x(q, src, src_tok):
            s = q % 4
            d = slice(2 * s, 2 * s + 2)
            a = AC.do([src_tok, x_free[s]], lambda e: e.activation(xh[:, d, :], src, ACT.Copy))
            return DV.do([a], lambda e: e.tensor_tensor(xl[:, d, :], src, f32(xh[:, d, :]), ALU.subtract))

        def to_features(src, src_toks, evac, first=0, by=None):
            toks = []
            for h in range(2):
                for q in range(4):
                    b = first + q
                    for j in range(2):
                        k = 2 * q + j
                        w = [src_toks[h], k_ident, free[b]]
                        o = PS[:, b, j * 256 + h * 128:j * 256 + h * 128 + 128]
                        s = src[:, h, k * 128:k * 128 + 128]
                        if by:
                            f = (lambda e: e.matmul(o, s, by[h], start=True, stop=True))
                        else:
                            f = (lambda e: e.transpose(o, s, ident[:, :]))
                        if (h, j) == (1, 1):
                            t = PE.do(w, f)
                        else:
                            PE.go(w, f)
                    if h:
                        free[b] = evac(q, PS[:, b, :].rearrange("p (k t) -> p k t", k=2), t)
                        toks.append(free[b])
            return toks

        def to_tokens(src, src_toks, dst, dst_free):
            toks = []
            for h in range(2):
                for d in range(2):
                    b = 2 * h + d
                    for kk in range(4):
                        k = 4 * d + kk
                        t = PE.do([src_toks[k // 2], free[b] if kk == 0 else None], lambda e: e.transpose(
                            PS[:, b, kk * 128:kk * 128 + 128], src[:, k, h * 128:h * 128 + 128], ident[:, :]))
                    free[b] = AC.do([t, dst_free], lambda e: e.activation(
                        dst[:, h, d * 512:d * 512 + 512], PS[:, b, :], ACT.Copy))
                    toks.append(free[b])
            return toks

        def proj_features(name, n, xt_toks, evac, banks):
            for c in range(n):
                b = banks[c % len(banks)]
                for j in range(2):
                    for k in range(8):
                        if k % 4 == 0:
                            h, l, w_ok = piece(name)
                        a = (k % 4) * 128
                        t = mm3(PS[:, b, j * 256:j * 256 + 256], (h[:, a:a + 128], l[:, a:a + 128]),
                                (xh[:, k, :], xl[:, k, :]),
                                [xt_toks[k // 2], w_ok, free[b] if (j, k) == (0, 0) else None],
                                k == 0, k == 7, k % 4 == 3)
                        if k % 4 == 3:
                            piece_done(t)
                free[b] = evac(c, PS[:, b, :].rearrange("p (k t) -> p k t", k=2), t)
            x_free[:] = [t] * 4

        def proj_cols(name, n, xt_toks, evac, banks):
            for c in range(n):
                for k in range(8):
                    h, l, w_ok = piece(name)
                    for m in range(2):
                        b, x = banks[(2 * c + m) % len(banks)], slice(m * 128, m * 128 + 128)
                        t = mm3(PS[:, b, :], (xh[:, k, x], xl[:, k, x]), (h, l),
                                [xt_toks[k // 2], w_ok, free[b] if k == 0 else None], k == 0, k == 7, m == 1)
                    piece_done(t)
                for m in range(2):
                    b = banks[(2 * c + m) % len(banks)]
                    free[b] = evac(c, m, PS[:, b, :], t)
            x_free[:] = [t] * 4

        def proj_out(name, nk, gt, gt_toks, evac):
            nq = nk // 2
            toks = {}

            def split(q):
                if q < nq:
                    toks[q] = split_x(q, gt[:, 2 * q:2 * q + 2, :], [gt_toks[2 * q], gt_toks[2 * q + 1]])

            for q in range(3):
                split(q)
            for q in range(nq - 1):
                for kk in range(2):
                    k = 2 * q + kk
                    s = k % 8
                    for d in range(2):
                        h, l, w_ok = piece(name)
                        for m in range(2):
                            b, x = 2 * m + d, slice(m * 128, m * 128 + 128)
                            t = mm3(PS[:, b, :], (xh[:, s, x], xl[:, s, x]), (h, l),
                                    [toks[q], w_ok, free[b] if k == 0 else None], k == 0, False, m == 1)
                        piece_done(t)
                x_free[q % 4] = t
                split(q + 3)
            for m in range(2):
                x = slice(m * 128, m * 128 + 128)
                for kk in range(2):
                    s = (nk - 2 + kk) % 8
                    for d in range(2):
                        h, l, w_ok = piece(name, 2 * kk + d)
                        t = mm3(PS[:, 2 * m + d, :], (xh[:, s, x], xl[:, s, x]), (h, l),
                                [toks[nq - 1], w_ok], False, kk == 1, kk == 1)
                        if kk:
                            free[2 * m + d] = evac(m, d, PS[:, 2 * m + d, :], t)
            x_free[(nq - 1) % 4] = t
            for _ in range(4):
                piece_done(t)

        def rstd(var, eps, h, toks):
            a = DV.do(toks, lambda e: e.tensor_scalar(sm[:, 490 + h:491 + h], var, eps, None, ALU.add))
            return PL.do([a, k_mhalf], lambda e: e.tensor_tensor(
                sm[:, 500 + h:501 + h], sm[:, 490 + h:491 + h], mhalf[:, 0:1], ALU.pow))

        def moments(src, src_toks, h):
            st = sm[:, 400 + 12 * h:412 + 12 * h].rearrange("p (d s) -> p d s", d=2)
            mv = sm[:, 424 + 2 * h:426 + 2 * h]
            tt = [DV.do([src_toks], lambda e: e.bn_stats(st[:, d, :], src[:, h, d * 512:d * 512 + 512]))
                  for d in range(2)]
            a = DV.do(tt, lambda e: e.bn_aggr(mv, st))
            return mv[:, 0:1], sm[:, 500 + h:501 + h], [a, rstd(mv[:, 1:2], LN_EPS, h, [a])]

        def layer_norm(zt, n, halves):
            g, b = col(f"lng{n}"), col(f"lnb{n}")
            done = []
            for h in range(2):
                mean, r, ok = moments(Z, zt[2 * h:2 * h + 2] if halves else zt, h)
                done.append(DV.do([ok], lambda e: e.tensor_scalar(
                    Z[:, h, :], Z[:, h, :], mean, r, ALU.subtract, ALU.mult)))

            def evac(q, ps, t):
                tt = []
                for k in (2 * q, 2 * q + 1):
                    if q % 2:
                        tt.append(DV.do([t, c_ok], lambda e: e.tensor_scalar(
                            XT[:, k, :], ps[:, k % 2, :], g[:, k:k + 1], b[:, k:k + 1], ALU.mult, ALU.add)))
                    else:
                        tt.append(AC.do([t, c_ok], lambda e: e.activation(
                            XT[:, k, :], ps[:, k % 2, :], ACT.Identity, scale=g[:, k:k + 1], bias=b[:, k:k + 1])))
                return tt

            return to_features(Z, done, evac, first=4)

        def rms_features(src, src_toks, evac):
            done = []
            for h in range(2):
                s = AC.do([src_toks[2 * h:2 * h + 2]], lambda e: e.activation(
                    Z[:, h, :], src[:, h, :], ACT.Square, scale=1.0 / 32, accum_out=sm[:, 430 + h:431 + h]))
                r = rstd(sm[:, 430 + h:431 + h], RMS_EPS, h, [s])
                done.append(DV.do([r], lambda e: e.tensor_scalar(
                    Z[:, h, 0:128], ident[:, :], sm[:, 500 + h:501 + h], None, ALU.mult)))
            return to_features(src, done, evac, first=4, by=[Z[:, 0, 0:128], Z[:, 1, 0:128]])

        def split_xt(gname=None):
            g = gname and col(gname)

            def evac(q, ps, t):
                d = slice(2 * q, 2 * q + 2)
                if g is None:
                    a = AC.do([t, x_free[q]], lambda e: e.activation(xh[:, d, :], ps, ACT.Copy))
                    return DV.do([a], lambda e: e.tensor_tensor(xl[:, d, :], ps, f32(xh[:, d, :]), ALU.subtract))
                for k in (2 * q, 2 * q + 1):
                    a = AC.do([t, x_free[q], c_ok], lambda e: e.activation(
                        xh[:, k, :], ps[:, k % 2, :], ACT.Copy, scale=g[:, k:k + 1]))
                for k in (2 * q, 2 * q + 1):
                    b = DV.do([a], lambda e: e.scalar_tensor_tensor(
                        out=xl[:, k, :], in0=ps[:, k % 2, :], scalar=g[:, k:k + 1], in1=f32(xh[:, k, :]),
                        op0=ALU.mult, op1=ALU.subtract))
                return b
            return evac

        def even_mixer():
            ahead()
            xt_ok = to_features(X, [x_ok, x_ok], split_xt())
            aP = F[:, 2048:2048 + 4 * 286].rearrange("p (k t) -> p k t", k=4)
            bP = F[:, 3200:3200 + 4 * 258].rearrange("p (k t) -> p k t", k=4)
            sg = fv(4300, 4)
            acc = fv(5400, 4)
            bc = fv(6500, 4)
            bacc = fv(7600, 4)
            sq = fv(8700, 4)
            rs = F[:, 9800:10056]
            gh, bh = sm[:, 0:4], sm[:, 4:8]
            z1 = DV.do([], lambda e: e.memset(aP[:, :, 0:30], 0.0))
            z2 = DV.do([], lambda e: e.memset(bP[:, :, 0:2], 0.0))
            h1 = DV.do([c_ok], lambda e: e.tensor_scalar(gh, col("a_ln_g"), 0.5, None, ALU.mult))
            h2 = DV.do([c_ok], lambda e: e.tensor_scalar(bh, col("a_ln_b"), 0.5, None, ALU.mult))
            tok = {}
            aw = col("a_dw").rearrange("p (c k) -> p c k", c=4)
            last = [None] * 4
            steps = [(k, c) for half in range(2) for k in range(31) for c in (2 * half, 2 * half + 1)]

            def convolve(n):
                for _ in range(min(n, len(steps))):
                    k, c = steps.pop(0)
                    src, wk = aP[:, c, k:k + 256], aw[:, c, k:k + 1]
                    if k == 0:
                        last[c] = DV.do([tok["a", c // 2], z1, c_ok], lambda e: e.tensor_scalar(
                            acc[:, c, :], src, wk, None, ALU.mult))
                    else:
                        last[c] = DV.do([last[c]], lambda e: e.scalar_tensor_tensor(
                            out=acc[:, c, :], in0=src, scalar=wk, in1=acc[:, c, :],
                            op0=ALU.mult, op1=ALU.add))

            def evac(c, ps, t):
                i = 2 * (c % 2)
                if c < 2:
                    tok["g", c] = AC.do([t], lambda e: e.activation(sg[:, i:i + 2, :], ps, ACT.Tanh, scale=0.5))
                    return tok["g", c]
                if c < 4:
                    tok["a", c - 2] = DV.do([t, tok["g", c - 2]], lambda e: e.scalar_tensor_tensor(
                        out=aP[:, i:i + 2, 30:286], in0=sg[:, i:i + 2, :], scalar=1.0, in1=ps,
                        op0=ALU.add, op1=ALU.mult))
                    return tok["a", c - 2]
                convolve(20)
                if c < 6:
                    tok["c", c - 4] = AC.do([t], lambda e: e.activation(bc[:, i:i + 2, :], ps, ACT.Copy))
                    return tok["c", c - 4]
                if c < 8:
                    tok["x", c - 6] = DV.do([t, tok["c", c - 6]], lambda e: e.tensor_tensor(
                        bP[:, i:i + 2, 2:258], bc[:, i:i + 2, :], ps, ALU.mult))
                    return tok["x", c - 6]
                tok["b", c - 8] = AC.do([t, tok["x", c - 8]], lambda e: e.activation(
                    bc[:, i:i + 2, :], ps, ACT.Copy))
                return tok["b", c - 8]

            proj_features("ew_in", 10, xt_ok, evac, list(range(8)))
            convolve(len(steps))
            bw = col("b_dw").rearrange("p (c k) -> p c k", c=4)
            blast = [None] * 4
            for k in range(3):
                for c in range(4):
                    src, wk = bP[:, c, k:k + 256], bw[:, c, k:k + 1]
                    if k == 0:
                        blast[c] = DV.do([tok["x", c // 2], z2, c_ok], lambda e: e.tensor_scalar(
                            bacc[:, c, :], src, wk, None, ALU.mult))
                    else:
                        blast[c] = DV.do([blast[c]], lambda e: e.scalar_tensor_tensor(
                            out=bacc[:, c, :], in0=src, scalar=wk, in1=bacc[:, c, :],
                            op0=ALU.mult, op1=ALU.add))
            gt = [None] * 8
            for i in range(2):
                t = DV.do([blast, tok["b", i]], lambda e: e.tensor_tensor(
                    GT[:, 4 + 2 * i:6 + 2 * i, :], bacc[:, 2 * i:2 * i + 2, :], bc[:, 2 * i:2 * i + 2, :], ALU.mult))
                gt[4 + 2 * i] = gt[5 + 2 * i] = t
            for c in range(4):
                last[c] = DV.do([last[c], c_ok], lambda e: e.tensor_scalar(
                    acc[:, c, :], acc[:, c, :], 0.5, col("a_dw_b")[:, c:c + 1], ALU.mult, ALU.add))
            for c in range(4):
                m = PE.do([last[c], k_mean, free[0]], lambda e: e.matmul(
                    PS[:, 0, 0:256], mean512[:, :], acc[:, c, :], start=(c == 0), stop=(c == 3)))
            d = DV.do([m], lambda e: e.tensor_tensor(
                acc, acc, PS[:, 0, 0:256].unsqueeze(1).to_broadcast([128, 4, 256]), ALU.subtract))
            free[0] = d
            s = AC.do([d], lambda e: e.activation(sq, acc, ACT.Square))
            for c in range(4):
                m = PE.do([s, free[1]], lambda e: e.matmul(
                    PS[:, 1, 0:256], mean512[:, :], sq[:, c, :], start=(c == 0), stop=(c == 3)))
            v = DV.do([m], lambda e: e.tensor_scalar(rs, PS[:, 1, 0:256], LN_EPS, None, ALU.add))
            free[1] = v
            r = AC.do([v], lambda e: e.activation(rs, rs, ACT.Sqrt))
            r = DV.do([r], lambda e: e.reciprocal(rs, rs))
            d = DV.do([r, d, s], lambda e: e.tensor_tensor(
                acc, acc, rs.unsqueeze(1).to_broadcast([128, 4, 256]), ALU.mult))
            for c in range(4):
                y = DV.do([d, h1, h2], lambda e: e.tensor_scalar(
                    acc[:, c, :], acc[:, c, :], gh[:, c:c + 1], bh[:, c:c + 1], ALU.mult, ALU.add))
                th = AC.do([y, m], lambda e: e.activation(sq[:, c, :], acc[:, c, :], ACT.Tanh))
                gt[c] = DV.do([th], lambda e: e.scalar_tensor_tensor(
                    out=GT[:, c, :], in0=sq[:, c, :], scalar=1.0, in1=acc[:, c, :],
                    op0=ALU.add, op1=ALU.mult))
            return gt

        def add_residual(x, x_tok, scale, dst, dst_free):
            def evac(h, d, ps, t):
                sl = slice(d * 512, d * 512 + 512)
                if scale == 1.0:
                    return DV.do([t, x_tok, dst_free], lambda e: e.tensor_tensor(
                        dst[:, h, sl], x[:, h, sl], ps, ALU.add))
                return DV.do([t, x_tok, dst_free], lambda e: e.scalar_tensor_tensor(
                    out=dst[:, h, sl], in0=x[:, h, sl], scalar=scale, in1=ps, op0=ALU.mult, op1=ALU.add))
            return evac

        def odd_mixer(xt_ok, tokens):
            xP = F[:, 2048:2048 + 8 * 259].rearrange("p (k t) -> p k t", k=8)
            y = fv(4128, 8)
            xc = fv(6176, 8)
            r = fv(8224, 8)
            ig = fv(10272, 8)
            sp = [sm[:, i * 8:i * 8 + 8] for i in range(6)]
            hb = sm[:, 48:64]
            lam = col("lam")
            t = AC.do([c_ok], lambda e: e.activation(sp[0], lam, ACT.Abs))
            t = AC.do([t], lambda e: e.activation(sp[1], sp[0], ACT.Exp, scale=-1.0))
            u = DV.do([t], lambda e: e.tensor_scalar(sp[2], sp[1], 1.0, None, ALU.add))
            t = AC.do([u], lambda e: e.activation(sp[3], sp[2], ACT.Ln))
            t = AC.do([t], lambda e: e.activation(sp[4], sp[3], ACT.Tanh, scale=0.5))
            v = DV.do([t], lambda e: e.tensor_scalar(sp[5], sp[4], -1.0, 1.0, ALU.mult, ALU.add))
            v = DV.do([v], lambda e: e.reciprocal(sp[5], sp[5]))
            v = DV.do([v], lambda e: e.scalar_tensor_tensor(out=sp[4], in0=sp[4], scalar=2.0, in1=sp[5],
                                                            op0=ALU.mult, op1=ALU.mult))
            v = DV.do([v], lambda e: e.tensor_tensor(sp[4], sp[4], sp[1], ALU.subtract))
            u = DV.do([v], lambda e: e.reciprocal(sp[2], sp[2]))
            v = DV.do([u], lambda e: e.tensor_tensor(sp[4], sp[4], sp[2], ALU.mult))
            v = DV.do([v], lambda e: e.tensor_tensor(sp[3], sp[3], sp[4], ALU.subtract))
            u = DV.do([c_ok], lambda e: e.tensor_scalar(sp[0], lam, -1.0, 0.0, ALU.mult, ALU.max))
            v = DV.do([v, u], lambda e: e.tensor_tensor(sp[3], sp[3], sp[0], ALU.add))
            sp2 = sp[1]
            v_sp = DV.do([v], lambda e: e.tensor_scalar(sp2, sp[3], 2.0, None, ALU.mult))
            v_hb = DV.do([c_ok], lambda e: e.tensor_scalar(
                hb, cols[:, COLS["bga"][0]:COLS["bga"][0] + 16], 0.5, None, ALU.mult))
            z1 = DV.do([xt_ok], lambda e: e.memset(xP[:, :, 0:3], 0.0))
            tok = {}

            def evac(c, ps, t):
                if c < 4:
                    tok["x", c] = AC.do([t, xt_ok], lambda e: e.activation(xP[:, 2 * c:2 * c + 2, 3:259], ps, ACT.Copy))
                    return tok["x", c]
                i = 2 * (c - 4)
                tok["y", c - 4] = AC.do([t], lambda e: e.activation(y[:, i:i + 2, :], ps, ACT.Copy))
                return tok["y", c - 4]

            proj_features("ow_in", 8, xt_ok, evac, list(range(8)))
            cw = col("c_dw").rearrange("p (c k) -> p c k", c=8)
            cb = col("c_dw_b")
            last = [None] * 8
            for k in range(4):
                for c in range(8):
                    src, wk = xP[:, c, k:k + 256], cw[:, c, k:k + 1]
                    if k == 0:
                        last[c] = DV.do([tok["x", c // 2], z1, c_ok], lambda e: e.tensor_scalar(
                            xc[:, c, :], src, wk, cb[:, c:c + 1], ALU.mult, ALU.add))
                    else:
                        last[c] = DV.do([last[c]], lambda e: e.scalar_tensor_tensor(
                            out=xc[:, c, :], in0=src, scalar=wk, in1=xc[:, c, :], op0=ALU.mult, op1=ALU.add))
            for g, dst in ((0, r), (1, ig)):
                w, w_ok = W.take("gates")
                wv = w.rearrange("p (h k n) -> p h k n", h=4, k=2)
                for h in range(4):
                    b = h + 4 * g
                    for j in range(2):
                        for k in range(2):
                            t = PE.do([w_ok, last[2 * h + k], free[b] if j == 0 else None], lambda e: e.matmul(
                                PS[:, b, j * 256:j * 256 + 256], wv[:, h, k, j * 128:j * 128 + 128],
                                xc[:, 2 * h + k, :], start=(k == 0), stop=(k == 1)))
                    for j in range(2):
                        c = 2 * h + j
                        tok[g, c] = AC.do([t, v_hb], lambda e: e.activation(
                            dst[:, c, :], PS[:, b, j * 256:j * 256 + 256], ACT.Tanh, scale=0.5,
                            bias=hb[:, 8 * g + c:8 * g + c + 1]))
                    free[b] = tok[g, c]
                W.give(t)
            Tt = fv(2048, 8)
            gt = [None] * 8
            r1 = DV.do([tok[0, 7]], lambda e: e.tensor_scalar(r, r, 1.0, None, ALU.add))
            bx = DV.do([tok[1, 7], last], lambda e: e.scalar_tensor_tensor(
                out=xc, in0=ig, scalar=1.0, in1=xc, op0=ALU.add, op1=ALU.mult))
            tt = [AC.do([r1, v_sp, last], lambda e: e.activation(
                Tt[:, c, :], r[:, c, :], ACT.Tanh, scale=sp2[:, c:c + 1])) for c in range(8)]
            ri = DV.do([tt], lambda e: e.tensor_scalar(r, Tt, 1.0, None, ALU.add))
            ri = DV.do([ri], lambda e: e.reciprocal(r, r))
            yt = [tok["y", i] for i in range(4)]
            g1 = AC.do([yt, bx], lambda e: e.activation(ig, y, ACT.Square))
            g2 = DV.do([g1], lambda e: e.tensor_scalar(ig, ig, 0.044715, 1.0, ALU.mult, ALU.add))
            g3 = DV.do([g2], lambda e: e.tensor_tensor(ig, ig, y, ALU.mult))
            g4 = AC.do([g3], lambda e: e.activation(ig, ig, ACT.Tanh, scale=math.sqrt(2.0 / math.pi)))
            g5 = DV.do([g4], lambda e: e.scalar_tensor_tensor(
                out=y, in0=ig, scalar=1.0, in1=y, op0=ALU.add, op1=ALU.mult))
            sq = AC.do([tt, g4, g5], lambda e: e.activation(ig, Tt, ACT.Sqrt))
            b1 = DV.do([sq, ri, bx], lambda e: e.tensor_tensor(xc, xc, ig, ALU.mult))
            b2 = DV.do([b1], lambda e: e.tensor_tensor(xc, xc, r, ALU.mult))
            a1 = DV.do([sq], lambda e: e.tensor_scalar(Tt, Tt, -1.0, 1.0, ALU.mult, ALU.add))
            a2 = DV.do([a1, ri], lambda e: e.tensor_tensor(Tt, Tt, r, ALU.mult))
            for c in range(8):
                s = DV.do([a2, b2], lambda e: e.tensor_tensor_scan(
                    ig[:, c, :], Tt[:, c, :], xc[:, c, :], 0.0, ALU.mult, ALU.add))
                gt[c] = DV.do([s, g5], lambda e: e.scalar_tensor_tensor(
                    out=GT[:, c, :], in0=y[:, c, :], scalar=0.5, in1=ig[:, c, :], op0=ALU.mult, op1=ALU.mult))
            x2 = tokens()
            ahead()
            return gt, x2

        def moe(layer, xt_ok, x_free):
            S = F[:, 0:2048].rearrange("p (h n) -> p h n", h=2)
            Gs = [F[:, 2048 + i * 2048:4096 + i * 2048].rearrange("p (h n) -> p h n", h=2) for i in range(2)]
            Gt = [F[:, 6144 + i * 512:6656 + i * 512].rearrange("p (h s t) -> p h s t", h=2, s=2)
                  for i in range(2)]
            xg = [F[:, 7168 + i * 1024:8192 + i * 1024].rearrange("p (k s) -> p k s", k=8) for i in range(2)]
            th, sl, hh = (F[:, 9216 + i * 512:9728 + i * 512] for i in range(3))
            hT = [F[:, 10752 + i * 512:11264 + i * 512] for i in range(2)]
            Y = [F[:, 11776 + i * 512:12288 + i * 512] for i in range(2)]

            def v2(a, n=16):
                return sm[:, a:a + 2 * n].rearrange("p (h e) -> p h e", h=2)

            wr = col("wr").rearrange("p (k e) -> p k e", k=8)
            for h in range(2):
                PE.go([br_ok, k_ident, free[3]], lambda e: e.matmul(
                    PS[:, 3, h * 16:h * 16 + 16], ident[:, :], brt[:, :], start=True, stop=False))
                for k in range(8):
                    t = PE.do([xt_ok[k // 2], c_ok], lambda e: e.matmul(
                        PS[:, 3, h * 16:h * 16 + 16], XT[:, k, h * 128:h * 128 + 128], wr[:, k, :],
                        start=False, stop=(k == 7)))
            lg, pr, oh, tmp, m1, m2 = v2(0), v2(32), v2(64), v2(96), v2(128), v2(160)
            M, pos, gate, og = v2(192), v2(224), v2(256), v2(288)
            mx = sm[:, 320:322]
            gs = sm[:, 324:332].rearrange("p (h g) -> p h g", h=2)
            gp = sm[:, 332:340].rearrange("p (h g) -> p h g", h=2)
            p1, p2, den = sm[:, 340:342], sm[:, 342:344], sm[:, 344:346]
            pri = sm[:, 346:362]
            cnt = sm[:, 362:378]
            fl = sm[:, 378:379]

            def dv(toks, fn):
                return DV.do(toks, fn)

            def bc(ap, n=16):
                return ap.unsqueeze(2).to_broadcast([128, 2, n])

            tp = PL.do([k_iota], lambda e: e.tensor_scalar(pri, iota64[:, 0:16], -1.0, 17.0, ALU.mult, ALU.add))
            L = PS[:, 3, 0:32].rearrange("p (h e) -> p h e", h=2)
            t = dv([t], lambda e: e.tensor_reduce(mx, L, AX, ALU.max))
            free[3] = t = dv([t], lambda e: e.tensor_tensor(lg, L, bc(mx), ALU.subtract))
            tex = t = AC.do([t], lambda e: e.activation(pr, lg, ACT.Exp))
            x_tok = to_tokens(XT, xt_ok, X, x_free)
            pq = pr.rearrange("p h (g i j) -> p (h g i) j", g=4, i=2)
            hi, su = tmp[:, 0, :], tmp[:, 1, :]
            u = dv([t], lambda e: e.tensor_tensor(hi, pq[:, :, 0], pq[:, :, 1], ALU.max))
            v = dv([t], lambda e: e.tensor_tensor(su, pq[:, :, 0], pq[:, :, 1], ALU.add))
            h2 = hi.rearrange("p (n i) -> p n i", i=2)
            s2 = su.rearrange("p (n i) -> p n i", i=2)
            u = dv([u], lambda e: e.tensor_tensor(sm[:, 324:332], h2[:, :, 0], h2[:, :, 1], ALU.add))
            v = dv([v], lambda e: e.tensor_tensor(sm[:, 332:340], s2[:, :, 0], s2[:, :, 1], ALU.max))
            tg = dv([u, v], lambda e: e.tensor_tensor(sm[:, 324:332], sm[:, 324:332], sm[:, 332:340], ALU.max))

            def first_max(val, prio, best, onehot, n, toks):
                a = dv(toks, lambda e: e.tensor_reduce(best, val, AX, ALU.max))
                a = dv([a], lambda e: e.tensor_tensor(onehot, val, bc(best, n), ALU.is_ge))
                a = dv([a], lambda e: e.tensor_tensor(onehot, onehot, prio, ALU.mult))
                b = dv([a], lambda e: e.tensor_reduce(sm[:, 380:382], onehot, AX, ALU.max))
                return dv([b], lambda e: e.tensor_tensor(onehot, onehot, bc(sm[:, 380:382], n), ALU.is_equal))

            tg = first_max(gs, pri[:, 12:16].unsqueeze(1).to_broadcast([128, 2, 4]), mx, gp, 4, [tg, tp])
            gb = gp.unsqueeze(3).to_broadcast([128, 2, 4, 4])
            pm = oh
            b = dv([tg], lambda e: e.tensor_tensor(
                pm.rearrange("p h (g j) -> p h g j", g=4),
                pri.rearrange("p (g j) -> p g j", g=4).unsqueeze(1).to_broadcast([128, 2, 4, 4]), gb, ALU.mult))
            a = dv([tg], lambda e: e.tensor_tensor(
                tmp.rearrange("p h (g j) -> p h g j", g=4), pr.rearrange("p h (g j) -> p h g j", g=4), gb, ALU.mult))
            a = first_max(tmp, pm, p1, m1, 16, [a, b])
            a = dv([a], lambda e: e.scalar_tensor_tensor(out=tmp, in0=m1, scalar=-4.0, in1=tmp,
                                                         op0=ALU.mult, op1=ALU.add))
            am = first_max(tmp, pm, p2, m2, 16, [a])
            a = dv([am], lambda e: e.tensor_tensor(M, m1, m2, ALU.add))
            for h in range(2):
                if h == 1:
                    PE.go([k_ones], lambda e: e.matmul(PS[:, 4, 16:32], ones[:, 0:128], M[:, 0, :],
                                                       start=True, stop=False))
                t = PE.do([a, k_upper, free[4]], lambda e: e.matmul(
                    PS[:, 4, h * 16:h * 16 + 16], upper[:, :], M[:, h, :], start=(h == 0), stop=True))
            PE.go([k_ones, free[5]], lambda e: e.matmul(PS[:, 5, 0:16], ones[:, 0:128], M[:, 0, :], start=True, stop=False))
            tc = PE.do([], lambda e: e.matmul(PS[:, 5, 0:16], ones[:, 0:128], M[:, 1, :], start=False, stop=True))
            free[4] = p = dv([t], lambda e: e.scalar_tensor_tensor(
                out=pos, in0=PS[:, 4, 0:32].rearrange("p (h e) -> p h e", h=2), scalar=1.0, in1=M,
                op0=ALU.add, op1=ALU.mult))
            ts = []
            S4 = S.rearrange("p h (e s) -> p h e s", e=16)
            for e0, e1 in ((0, 2), (2, 16)):
                ts.append(dv([p, k_iota, x_free], lambda e: e.tensor_tensor(
                    S4[:, :, e0:e1, :],
                    iota64[:, :].unsqueeze(1).unsqueeze(1).to_broadcast([128, 2, e1 - e0, 64]),
                    pos[:, :, e0:e1].unsqueeze(3).to_broadcast([128, 2, e1 - e0, 64]), ALU.is_equal)))

            def gates():
                d = dv([tex], lambda e: e.tensor_reduce(den, pr, AX, ALU.add))
                d = dv([d], lambda e: e.reciprocal(den, den))
                a = dv([d, am], lambda e: e.tensor_tensor(p1, p1, den, ALU.mult))
                b = dv([d, am], lambda e: e.tensor_tensor(p2, p2, den, ALU.mult))
                b = dv([a, b], lambda e: e.tensor_tensor(den, p1, p2, ALU.add))
                b = dv([b], lambda e: e.reciprocal(den, den))
                b1 = dv([b], lambda e: e.tensor_tensor(p1, p1, den, ALU.mult))
                b2 = dv([b], lambda e: e.tensor_tensor(p2, p2, den, ALU.mult))
                b1 = dv([b1], lambda e: e.tensor_tensor(m1, m1, bc(p1), ALU.mult))
                b2 = dv([b2], lambda e: e.tensor_tensor(m2, m2, bc(p2), ALU.mult))
                tgate = dv([b1, b2], lambda e: e.tensor_tensor(gate, m1, m2, ALU.add))
                out = []
                for h in range(2):
                    for i in range(2):
                        for o in range(2):
                            v = (lambda ap, m: ap.rearrange("p (q m s) -> p q m s", q=8, m=2)[:, :, m, :])
                            ga = gate[:, h, :].rearrange("p (q m) -> p q m", m=2)[:, :, o]
                            out.append(dv([ts, tgate], lambda e: e.tensor_tensor(
                                v(Gs[i][:, h, :], o ^ i), v(S[:, h, :], o),
                                ga.unsqueeze(2).to_broadcast([128, 8, 64]), ALU.mult)))
                a = dv([tc], lambda e: e.tensor_reduce(fl, PS[:, 5, 0:16], AX, ALU.max))
                free[5] = a
                tfl = dv([a], lambda e: e.tensor_scalar(it[:, 0:1], fl, float(CAP), None, ALU.is_gt))
                b = dv([p], lambda e: e.tensor_scalar(og, pos, float(CAP), None, ALU.is_gt))
                return out, tfl, dv([b, tgate], lambda e: e.tensor_tensor(og, og, gate, ALU.mult))

            xg_tok, xg_free = [None, None], [None, None]
            gt_tok, gt_free = [None, None], [None, None]
            y_free = [None]

            def gather(q):
                i = q % 2
                got = []
                for half in range(2):
                    b = 6 + half
                    for k4 in range(4):
                        k = 4 * half + k4
                        for h in range(2):
                            t = PE.do([ts[min(q, 1)], x_tok, free[b] if k4 == 0 else None], lambda e: e.matmul(
                                PS[:, b, k4 * 128:k4 * 128 + 128], X[:, h, k * 128:k * 128 + 128],
                                S[:, h, q * 128:q * 128 + 128], start=(h == 0), stop=(h == 1)))
                    src = PS[:, b, :].rearrange("p (k s) -> p k s", k=4)
                    dst = xg[i][:, 4 * half:4 * half + 4, :]
                    if half:
                        free[b] = DV.do([t, xg_free[i]], lambda e: e.tensor_copy(dst, src))
                    else:
                        free[b] = AC.do([t, xg_free[i]], lambda e: e.activation(dst, src, ACT.Copy))
                    got.append(free[b])
                xg_tok[i] = got

            def turn_gates(q):
                i = q % 2
                for h in range(2):
                    for s in range(2):
                        a = (2 * h + s) * 128
                        t = PE.do([gs_tok, free[6]], lambda e: e.transpose(
                            PS[:, 6, a:a + 128], Gs[s][:, h, q * 128:q * 128 + 128], ident[:, :]))
                src = PS[:, 6, :].rearrange("p (h s t) -> p h s t", h=2, s=2)
                free[6] = AC.do([t, gt_free[i]], lambda e: e.activation(Gt[i], src, ACT.Copy))
                gt_tok[i] = free[6]

            def product(name, bank, lhs, lhs_tok, swap):
                for c in range(4):
                    w, w_ok = W.take(name)
                    for kk in range(2):
                        k = 2 * c + kk
                        for half in range(2):
                            a = kk * 1024 + (half ^ swap) * 512
                            f = (lambda e: e.matmul(PS[64 * half:64 * half + 64, bank, :], lhs(k), w[:, a:a + 512],
                                                    start=(k == 0), stop=(k == 7)))
                            wt = [w_ok, lhs_tok, free[bank] if c == 0 else None] if (kk, half) == (0, 0) else []
                            if (kk, half) == (1, 1):
                                t = PE.do(wt, f)
                            else:
                                PE.go(wt, f)
                    W.give(t)
                return t

            z_tok = [None] * 4

            def combine(q, y_tok):
                i = q % 2
                for h in range(2):
                    for d in range(2):
                        b = 2 * h + d
                        t = PE.do([y_tok, gt_tok[i], free[b] if q == 0 else None], lambda e: e.matmul(
                            PS[:, b, :], Gt[i][:, h, d, :], Y[d], start=(q == 0), stop=(q == 7)))
                        z_tok[b] = t
                y_free[0] = t
                gt_free[i] = t

            gather(0)
            gs_tok, tfl, tog = gates()
            y_tok = []
            h_free = [None, None]
            hh_free = None
            for ex in range(E):
                q, o, i = ex // 2, ex % 2, ex % 2
                xx, xk = xg[q % 2], xg_tok[q % 2]
                lhs = (lambda k: xx[:, k, o * 64:o * 64 + 64])
                t1 = product(f"w1{layer}", 4, lhs, xk, 0)
                a = AC.do([t1], lambda e: e.activation(th, PS[:, 4, :], ACT.Tanh, scale=0.5))
                s = DV.do([a], lambda e: e.scalar_tensor_tensor(
                    out=sl, in0=th, scalar=1.0, in1=PS[:, 4, :], op0=ALU.add, op1=ALU.mult))
                free[4] = s
                t3 = product(f"w3{layer}", 5, lhs, xk, 0)
                if o == 1:
                    xg_free[q % 2] = t3
                hd = DV.do([t3, s, hh_free], lambda e: e.scalar_tensor_tensor(
                    out=hh, in0=sl, scalar=0.5, in1=PS[:, 5, :], op0=ALU.mult, op1=ALU.mult))
                free[5] = hd
                if ex == 9:
                    for en in (AC, DV, PL, SP, PE):
                        en.wait([tfl])
                    flag = nc.values_load(it[0:1, 0:1], min_val=0, max_val=1)
                if o == 0 and q > 0:
                    combine(q - 1, y_tok)
                if o == 0:
                    turn_gates(q)
                    y_tok = []
                if o == 1 and q < 7:
                    gather(q + 1)
                for j in range(4):
                    t = PE.do([hd, free[6] if j == 0 else None], lambda e: e.transpose(
                        PS[:, 6, j * 128:j * 128 + 128], hh[:, j * 128:j * 128 + 128], ident[:, :]))
                hh_free = t
                free[6] = AC.do([t, h_free[i]], lambda e: e.activation(hT[i], PS[:, 6, :], ACT.Copy))
                ty = product(f"w2{layer}", 7, (lambda k: hT[i][:, (k % 4) * 128 + (k // 4) * 64:
                                                              (k % 4) * 128 + (k // 4) * 64 + 64]), free[6], o)
                h_free[i] = ty
                e0 = AC.do([ty, y_free[0]], lambda e: e.activation(Y[o][0:64, :], PS[0:64, 7, :], ACT.Copy))
                e1 = DV.do([ty, y_free[0]], lambda e: e.tensor_copy(Y[1 - o][64:128, :], PS[64:128, 7, :]))
                free[7] = [e0, e1]
                y_tok += [e0, e1]
            combine(7, y_tok)
            zt = []
            ev = add_residual(X, x_tok, ALPHA, Z, None)
            for h in range(2):
                for d in range(2):
                    free[2 * h + d] = ev(h, d, PS[:, 2 * h + d, :], z_tok[2 * h + d])
                    zt.append(free[2 * h + d])

            with nc.If(flag > 0):
                for en in (AC, DV, PL, SP, PE):
                    for other in (AC, DV, PL, PE):
                        en.e.wait_ge(other.sem, other.n)
                nc.all_engine_barrier()
                with nc.Fori(0, E) as e_i:
                    overflow(layer, og, e_i)
                    nc.all_engine_barrier(sems_to_clear=over_range)
                    nc.all_engine_barrier()
            return zt

        over = [sem(f"s_o{i}") for i in range(5)]
        nums = sorted(s.num for s in over)
        assert nums == list(range(nums[0], nums[0] + 5))
        over_range = range(nums[0], nums[0] + 5)

        def overflow(layer, og, e_i):
            oPE, oAC, oDV, oPL = (Eng(x.e, s) for x, s in zip((PE, AC, DV, PL), over))
            s_w = over[4]
            hid = F[:, 0:2048].rearrange("p (k t) -> p k t", k=8)
            wb = F[:, 2048:4096]
            th = F[:, 4096:4608]
            H = F[:, 4608:6656].rearrange("p (h n) -> p h n", h=2)
            oge = sm[:, 382:384]
            tg = oDV.do([], lambda e: e.tensor_copy(oge, og[:, :, bass.ds(e_i, 1)]))
            n, w_free = 0, None
            sp = Eng(SP.e, s_w)

            def dense(w, bank, lhs, lhs_tok, bank_tok):
                nonlocal n, w_free
                for c in range(4):
                    sp.wait([w_free])
                    sp.e.dma_start(wb, A[w][layer, bass.ds(e_i, 1), c].rearrange("a p n -> (a p) n"))\
                        .then_inc(s_w, 16)
                    n += 1
                    for kk in range(2):
                        k = 2 * c + kk
                        for h in range(2):
                            for d in range(2):
                                t = oPE.do([(s_w, 16 * n), lhs_tok, bank_tok if k == 0 else None],
                                           lambda e: e.matmul(
                                    PS[:, bank + 2 * h + d, :], lhs[:, k, h * 128:h * 128 + 128],
                                    wb[:, kk * 1024 + d * 512:kk * 1024 + d * 512 + 512],
                                    start=(k == 0), stop=(k == 7)))
                    w_free = t
                return t

            t1 = dense("w1", 0, XT, None, None)
            t3 = dense("w3", 4, XT, None, None)
            hd = None
            for h in range(2):
                for d in range(2):
                    b, dst = 2 * h + d, H[:, h, d * 512:d * 512 + 512]
                    a = oAC.do([t1, hd], lambda e: e.activation(th, PS[:, b, :], ACT.Tanh, scale=0.5))
                    s = oDV.do([a], lambda e: e.scalar_tensor_tensor(
                        out=dst, in0=th, scalar=1.0, in1=PS[:, b, :], op0=ALU.add, op1=ALU.mult))
                    hd = oDV.do([t3, s], lambda e: e.scalar_tensor_tensor(
                        out=dst, in0=dst, scalar=0.5, in1=PS[:, 4 + b, :], op0=ALU.mult, op1=ALU.mult))
            got = []
            for q in range(4):
                for j in range(2):
                    k = 2 * q + j
                    for h in range(2):
                        t = oPE.do([hd], lambda e: e.transpose(
                            PS[:, q, j * 256 + h * 128:j * 256 + h * 128 + 128],
                            H[:, h, k * 128:k * 128 + 128], ident[:, :]))
                got.append(oAC.do([t], lambda e: e.activation(
                    hid[:, 2 * q:2 * q + 2, :], PS[:, q, :].rearrange("p (k t) -> p k t", k=2), ACT.Copy)))
            t = dense("w2", 4, hid, got, hd)
            for h in range(2):
                for d in range(2):
                    z = Z[:, h, d * 512:d * 512 + 512]
                    oDV.do([t, tg], lambda e: e.scalar_tensor_tensor(
                        out=z, in0=PS[:, 4 + 2 * h + d, :], scalar=oge[:, h:h + 1], in1=z,
                        op0=ALU.mult, op1=ALU.add))

        def attention_a(xt_ok, x_free):
            qT = fv(2048, 8)
            kT = fv(4096, 8)
            v = F[:, 6144:8192].rearrange("p (h d) -> p h d", h=2)
            p_sb = [F[:, 8192 + i * 384:8576 + i * 384] for i in range(4)]
            dg = F[:, 12800:13312].rearrange("p (i b q) -> p i b q", i=2, b=2)
            pt = [F[:, 9728 + i * 384:10112 + i * 384] for i in range(2)]
            zf, ab, c, lf = (F[0:16, 10496 + i * 256:10752 + i * 256] for i in range(4))
            pads = [F[:, 11776 + i * 256:12032 + i * 256] for i in range(4)]
            n0 = PL.do([], lambda e: e.memset(f32(nch), 0.0))
            n0 = PL.do([], lambda e: e.memset(f32(ncl), 0.0))
            pad0 = [PL.do([xt_ok], lambda e: e.memset(F[:, 11776:12800], 0.0))] * 4
            cq = sm[:, 0:32].rearrange("p (b h) -> p b h", b=2)
            wf = col("wf")
            a = AC.do([c_ok], lambda e: e.activation(wfh[:, :], wf, ACT.Copy))
            wf_ok = DV.do([a], lambda e: e.tensor_tensor(wfl[:, :], wf, f32(wfh[:, :]), ALU.subtract))
            for k in range(8):
                t = mm3(PS[0:16, 7, 0:256], (wfh[:, k * 16:k * 16 + 16], wfl[:, k * 16:k * 16 + 16]),
                        (xh[:, k, :], xl[:, k, :]), [xt_ok[k // 2], wf_ok, free[7]], k == 0, k == 7, True)
            a = DV.do([t, bf_ok], lambda e: e.tensor_scalar(zf, PS[0:16, 7, 0:256], bft[:, 0:1], None, ALU.add))
            free[7] = a
            b = AC.do([a], lambda e: e.activation(ab, zf, ACT.Abs))
            b = AC.do([b], lambda e: e.activation(ab, ab, ACT.Exp, scale=-1.0))
            b = DV.do([b], lambda e: e.tensor_scalar(ab, ab, 1.0, None, ALU.add))
            b = AC.do([b], lambda e: e.activation(ab, ab, ACT.Ln))
            b = DV.do([b], lambda e: e.scalar_tensor_tensor(out=lf, in0=zf, scalar=0.0, in1=ab,
                                                            op0=ALU.min, op1=ALU.subtract))
            tc_ = DV.do([b, k_ones], lambda e: e.tensor_tensor_scan(c, ones[0:16, :], lf, 0.0, ALU.mult, ALU.add))
            nc3 = nch[0:16, :]
            n1 = DV.do([tc_, n0], lambda e: e.tensor_scalar(nc3[:, 0:128], c[:, 0:128], -1.0, None, ALU.mult))
            n2 = DV.do([tc_, n0], lambda e: e.tensor_scalar(nc3[:, 128:384], c, -1.0, None, ALU.mult))
            n3 = DV.do([n1, n2], lambda e: e.scalar_tensor_tensor(
                out=ncl[0:16, 128:384], in0=c, scalar=-1.0, in1=f32(nc3[:, 128:384]), op0=ALU.mult, op1=ALU.subtract))
            tn = DV.do([n3], lambda e: e.tensor_copy(ncl[0:16, 0:128], f32(ncl[0:16, 128:256])))
            for h in range(2):
                t = PE.do([tc_, free[7]], lambda e: e.transpose(
                    PS[:, 7, h * 16:h * 16 + 16], c[:, h * 128:h * 128 + 128], ident[0:16, 0:16]))
            tq = DV.do([t], lambda e: e.tensor_copy(cq, PS[:, 7, 0:32].rearrange("p (b h) -> p b h", b=2)))
            free[7] = tq
            tok = {}

            def evac(c_, ps, t):
                if c_ < 4:
                    tok["q", c_] = DV.do([t], lambda e: e.tensor_scalar(
                        qT[:, 2 * c_:2 * c_ + 2, :], ps, 0.125, None, ALU.mult))
                    return tok["q", c_]
                i = c_ - 4
                tok["k", i] = AC.do([t], lambda e: e.activation(kT[:, 2 * i:2 * i + 2, :], ps, ACT.Copy))
                return tok["k", i]

            proj_features("aq_in", 8, xt_ok, evac, [0, 1, 2, 3, 4, 5])

            def evac_v(c_, m, ps, t):
                dst = v[:, m, c_ * 512:c_ * 512 + 512]
                if m:
                    tok["v", c_, m] = AC.do([t], lambda e: e.activation(dst, ps, ACT.Copy))
                else:
                    tok["v", c_, m] = DV.do([t], lambda e: e.tensor_copy(dst, ps))
                return tok["v", c_, m]

            proj_cols("av_in", 2, xt_ok, evac_v, [0, 1, 2, 3])
            st = {}
            gt = [None] * 8

            def pad(h):
                r = slice(64 * (h % 2), 64 * (h % 2) + 64)
                st["pad", h] = PL.do([tok["q", h // 4], pad0, st.get(("s", h - 4))], lambda e: e.tensor_copy(
                    pads[h % 4][r, :], qT[r, h // 2, :]))

            def scores(h):
                i = h % 2
                b = i
                w = [st["pad", h], tok["k", h // 4], free[b]]
                q = pads[h % 4]
                sel = identr[:, h:h + 1].to_broadcast([128, 128])
                PE.go([w, tn, k_identr], lambda e: e.matmul(PS[:, b, 0:384], sel, nch, start=True, stop=False))
                PE.go([], lambda e: e.matmul(PS[:, b, 0:384], sel, ncl, start=False, stop=False))
                PE.go([], lambda e: e.matmul(PS[:, b, 0:128], q[:, 0:128], kT[:, h // 2, 0:128],
                                             start=False, stop=False))
                t = PE.do([], lambda e: e.matmul(PS[:, b, 128:384], q[:, 128:256], kT[:, h // 2, :],
                                                 start=False, stop=True))
                st["s", h] = t
                s = p_sb[h % 4]
                sc = sm[:, 64 + 16 * (h % 4):80 + 16 * (h % 4)]
                a0 = DV.do([t, tq, k_cmask, st.get(("t", h - 4))], lambda e: e.scalar_tensor_tensor(
                    out=s[:, 0:128], in0=PS[:, b, 0:128], scalar=cq[:, 0, h:h + 1], in1=cmask[:, 128:256],
                    op0=ALU.add, op1=ALU.add))
                a1 = DV.do([], lambda e: e.scalar_tensor_tensor(
                    out=s[:, 128:384], in0=PS[:, b, 128:384], scalar=cq[:, 1, h:h + 1], in1=cmask[:, :],
                    op0=ALU.add, op1=ALU.add))
                free[b] = a1
                m0 = DV.do([a0], lambda e: e.tensor_reduce(sc[:, 0:1], s[:, 0:128], AX, ALU.max))
                m1 = DV.do([a1], lambda e: e.tensor_reduce(sc[:, 1:2], s[:, 128:384], AX, ALU.max))
                ng = DV.do([m0, m1], lambda e: e.tensor_scalar(sc[:, 2:4], sc[:, 0:2], -1.0, None, ALU.mult))
                AC.go([ng], lambda e: e.activation(
                    s[:, 0:128], s[:, 0:128], ACT.Exp, bias=sc[:, 2:3], accum_out=sc[:, 4:5]))
                st["e", h] = AC.do([], lambda e: e.activation(
                    s[:, 128:384], s[:, 128:384], ACT.Exp, bias=sc[:, 3:4], accum_out=sc[:, 5:6]))

            def invert(h):
                sc = sm[:, 64 + 16 * (h % 4):80 + 16 * (h % 4)]
                rc = DV.do([st["e", h]], lambda e: e.reciprocal(sc[:, 6:8], sc[:, 4:6]))
                for b in range(2):
                    d = DV.do([rc, st.get(("t", h - 2))], lambda e: e.tensor_scalar(
                        dg[:, h % 2, b, :], ident[:, :], sc[:, 6 + b:7 + b], None, ALU.mult))
                st["d", h] = d

            def turn(h):
                i, b = h % 2, 2 + h % 2
                for n in range(3):
                    t = PE.do([st["d", h], free[b] if n == 0 else None], lambda e: e.matmul(
                        PS[:, b, n * 128:n * 128 + 128], p_sb[h % 4][:, n * 128:n * 128 + 128],
                        dg[:, i, 1 if n else 0, :], start=True, stop=True))
                st["t", h] = t
                free[b] = AC.do([t, st.get(("o", h - 2))], lambda e: e.activation(pt[i], PS[:, b, 0:384], ACT.Copy))
                st["pt", h] = free[b]

            def values(h):
                i, b = h % 2, 4 + (h // 2) % 2
                r = slice(64 * i, 64 * i + 64)
                PE.go([st["pt", h], [tok["v", n, m] for n in range(2) for m in range(2)], free[b] if i == 0 else None],
                      lambda e: e.matmul(PS[r, b, 0:256], v[:, 0, h * 64:h * 64 + 64], pt[i][:, 0:256],
                                         start=True, stop=False))
                t = PE.do([], lambda e: e.matmul(PS[r, b, 128:256], v[:, 1, h * 64:h * 64 + 64],
                                                 pt[i][:, 256:384], start=False, stop=True))
                st["o", h] = t
                if i:
                    free[b] = AC.do([t, x_free], lambda e: e.activation(GT[:, h // 2, :], PS[:, b, 0:256], ACT.Copy))
                    gt[h // 2] = free[b]

            pad(0)
            pad(1)
            for i in range(19):
                if i < 16:
                    scores(i)
                if i < 14:
                    pad(i + 2)
                if 1 <= i <= 16:
                    invert(i - 1)
                if 2 <= i <= 17:
                    turn(i - 2)
                if i >= 3:
                    values(i - 3)
            return gt

        def ffn(layer, xt_ok, gt_free):
            G = fv(0, 22)
            acc = [[F[:, 5632 + (2 * i + s) * 512:6144 + (2 * i + s) * 512].rearrange("p (k t) -> p k t", k=2)
                    for s in range(2)] for i in range(2)]
            th = [F[:, 7680 + i * 512:8192 + i * 512].rearrange("p (k t) -> p k t", k=2) for i in range(2)]
            cw = col(f"fcw{layer}").rearrange("p (c k) -> p c k", c=44)
            cb = col(f"fcb{layer}")
            gt = [None] * 22
            done = {}
            st = {}

            def evac(n, ps, t):
                pair, side = n // 2, n % 2
                i = pair % 2
                dst = acc[i][side]
                tt = []
                first = (22 if side == 0 else 0) + 2 * pair
                for j in range(2):
                    ch = first + j
                    a = AC.do([t, c_ok, st.get(pair - 2), gt_free], lambda e: e.activation(
                        dst[:, j, :], ps[:, j, :], ACT.Identity, scale=cw[:, ch, 2:3], bias=cb[:, ch:ch + 1]))
                for j in range(2):
                    ch = first + j
                    b = DV.do([a], lambda e: e.scalar_tensor_tensor(
                        out=dst[:, j, 1:256], in0=ps[:, j, 0:255], scalar=cw[:, ch, 1:2],
                        in1=dst[:, j, 1:256], op0=ALU.mult, op1=ALU.add))
                    b = DV.do([b], lambda e: e.scalar_tensor_tensor(
                        out=dst[:, j, 2:256], in0=ps[:, j, 0:254], scalar=cw[:, ch, 0:1],
                        in1=dst[:, j, 2:256], op0=ALU.mult, op1=ALU.add))
                    tt.append(b)
                if side == 0:
                    a = AC.do([tt], lambda e: e.activation(th[i], dst, ACT.Tanh, scale=0.5))
                    done[pair] = PL.do([a], lambda e: e.tensor_scalar(th[i], th[i], 0.5, 0.5, ALU.mult, ALU.add))
                    done[pair] = PL.do([done[pair]], lambda e: e.tensor_tensor(dst, dst, th[i], ALU.mult))
                else:
                    g = DV.do([tt, done[pair], gt_free], lambda e: e.tensor_tensor(
                        G[:, 2 * pair:2 * pair + 2, :], acc[i][0], dst, ALU.mult))
                    gt[2 * pair] = gt[2 * pair + 1] = g
                    st[pair] = g
                return tt

            proj_features(f"up{layer}", 22, xt_ok, evac, [4, 5, 6, 7])
            proj_out(f"down{layer}", 22, G, gt, add_residual(X, None, 1.0, X, None))
            return [free[b] for b in range(4)]

        def attention_b(x_tok):
            kT = fv(2048, 12)
            v = F[:, 5120:8192].rearrange("p (h d) -> p h d", h=2)
            qT = fv(8192, 12)
            pads = [F[:, 1024 + i * 256:1280 + i * 256] for i in range(4)]
            pad0 = PL.do([x_tok], lambda e: e.memset(F[:, 1024:2048], 0.0))
            XF = XT[:, :, :].rearrange("p k t -> p (k t)")
            S3 = [a.rearrange("p (g n) -> p g n", g=3) for a in (
                F[:, 11264:12416], F[:, 12416:13568], XF[:, 0:1152])]
            dg = XF[:, 1152:1664].rearrange("p (i b q) -> p i b q", i=2, b=2)
            g1 = col("mixg1")

            kv_split = split_xt("kvg")
            xt_ok, xt2_ok = [], []

            def evac2(q, ps, t):
                a = kv_split(q, ps, t)
                xt_ok.append(a)
                for k in (2 * q, 2 * q + 1):
                    b = AC.do([a], lambda e: e.activation(XT[:, k, :], ps[:, k % 2, :], ACT.Copy, scale=g1[:, k:k + 1]))
                xt2_ok.append(b)
                return b

            rms_features(X, x_tok, evac2)
            ZF = Z[:, :, :].rearrange("p h d -> p (h d)")
            dist = ZF[:, 0:1152].rearrange("p (g n) -> p g n", g=3)
            pt = [ZF[:, 1152 + i * 384:1536 + i * 384] for i in range(2)]
            di, dx = F[:, 11264:11520].bitcast(I32), F[:, 11520:11776].bitcast(I32)
            t = PL.do([xt2_ok], lambda e: e.iota(di, pattern=[[-1, 256]], base=128, channel_multiplier=1))
            t0 = DV.do([t], lambda e: e.tensor_copy(dist[:, 0, 128:384], di))
            dd = [t0]
            for g, mask in ((1, 3), (2, 15)):
                a = DV.do([t, dd], lambda e: e.tensor_scalar(dx, di, mask, None, ALU.bitwise_and))
                a = DV.do([a], lambda e: e.tensor_scalar(dist[:, g, 128:384], dx, 0.0, -NEG, ALU.is_gt, ALU.mult))
                dd.append(DV.do([a, t0], lambda e: e.tensor_tensor(
                    dist[:, g, 128:384], dist[:, g, 128:384], dist[:, 0, 128:384], ALU.add)))
            d0 = PL.do([dd], lambda e: e.affine_select(
                out=dist[:, 0, 128:384], in_=dist[:, 0, 128:384], compare_op=ALU.is_ge, fill=-NEG, base=0,
                pattern=[[1, 256]], channel_multiplier=-1))
            dl = []
            for g in range(3):
                dl.append(PL.do([d0, dd], lambda e: e.affine_select(
                    out=dist[:, g, 128:384], in_=dist[:, g, 128:384], compare_op=ALU.is_ge, fill=-NEG,
                    base=128, pattern=[[-1, 256]], channel_multiplier=1)))
            dist_ok = DV.do([dl], lambda e: e.tensor_copy(dist[:, :, 0:128], dist[:, :, 256:384]))
            tok = {}

            def evac_k(c, ps, t):
                if c % 2:
                    tok["k", c] = DV.do([t], lambda e: e.tensor_copy(kT[:, 2 * c:2 * c + 2, :], ps))
                else:
                    tok["k", c] = AC.do([t], lambda e: e.activation(kT[:, 2 * c:2 * c + 2, :], ps, ACT.Copy))
                return tok["k", c]

            def evac_v(c, m, ps, t):
                dst = v[:, m, c * 512:c * 512 + 512]
                if m:
                    tok["v", c, m] = DV.do([t], lambda e: e.tensor_copy(dst, ps))
                else:
                    tok["v", c, m] = AC.do([t], lambda e: e.activation(dst, ps, ACT.Copy))
                return tok["v", c, m]

            def evac_q(c, ps, t):
                tok["q", c] = DV.do([t], lambda e: e.tensor_scalar(
                    qT[:, 2 * c:2 * c + 2, :], ps, 0.125, None, ALU.mult))
                return tok["q", c]

            proj_features("wk", 6, xt_ok, evac_k, [0, 1, 2, 3])
            proj_cols("wv", 3, xt_ok, evac_v, [4, 5, 6, 7])
            q_ok = [split_x(q, XT[:, 2 * q:2 * q + 2, :], xt2_ok[q]) for q in range(4)]
            proj_features("bwq", 6, q_ok, evac_q, [0, 1, 2, 3])
            st = {}
            gt = [None] * 4

            def pad(n):
                h, g, m = n // 3, n % 3, st.get("pads", 0)
                r, tile = slice(64 * (h % 2), 64 * (h % 2) + 64), 4 * g + h // 2
                i = 2 * (h % 2) + n % 2
                st["pad", n] = PL.do([tok["q", tile // 2], pad0, st.get(("last", i))], lambda e: e.tensor_copy(
                    pads[i][r, :], qT[r, tile, :]))

            def scores(n):
                h, g, b = n // 3, n % 3, n % 4
                i = 2 * (h % 2) + n % 2
                tile, q = 4 * g + h // 2, pads[i]
                s, slope = S3[h % 3][:, g, :], 2.0 ** (-8.0 * (8 * g + h + 1) / 24)
                w = [st["pad", n], tok["k", tile // 2], free[b]]
                PE.go(w, lambda e: e.matmul(PS[:, b, 0:128], q[:, 0:128], kT[:, tile, 0:128],
                                            start=True, stop=True))
                t = PE.do([], lambda e: e.matmul(PS[:, b, 128:384], q[:, 128:256], kT[:, tile, :],
                                                 start=True, stop=True))
                st["last", i] = t
                free[b] = DV.do([t, dist_ok, st.get(("t", n - 9)), q_ok], lambda e: e.scalar_tensor_tensor(
                    out=s, in0=dist[:, g, :], scalar=-slope, in1=PS[:, b, 0:384], op0=ALU.mult, op1=ALU.add))
                st["a", n] = free[b]

            def soften(h):
                s = S3[h % 3]
                sc = sm[:, 256 + 8 * (h % 3):264 + 8 * (h % 3)]
                a = [st["a", 3 * h + g] for g in range(3)]
                m0 = DV.do([a, st.get(("d", h - 3))], lambda e: e.tensor_reduce(
                    sc[:, 0:1], s[:, :, 0:128], mybir.AxisListType.XY, ALU.max))
                m1 = DV.do([], lambda e: e.tensor_reduce(
                    sc[:, 1:2], s[:, :, 128:384], mybir.AxisListType.XY, ALU.max))
                ng = DV.do([m0, m1], lambda e: e.tensor_scalar(sc[:, 2:4], sc[:, 0:2], -1.0, None, ALU.mult))
                AC.go([ng], lambda e: e.activation(
                    s[:, :, 0:128], s[:, :, 0:128], ACT.Exp, bias=sc[:, 2:3], accum_out=sc[:, 4:5]))
                st["e", h] = AC.do([], lambda e: e.activation(
                    s[:, :, 128:384], s[:, :, 128:384], ACT.Exp, bias=sc[:, 3:4], accum_out=sc[:, 5:6]))

            def invert(h):
                sc = sm[:, 256 + 8 * (h % 3):264 + 8 * (h % 3)]
                rc = DV.do([st["e", h]], lambda e: e.reciprocal(sc[:, 6:8], sc[:, 4:6]))
                for b in range(2):
                    d = DV.do([rc, st.get(("t", 3 * (h - 2) + 2))], lambda e: e.tensor_scalar(
                        dg[:, h % 2, b, :], ident[:, :], sc[:, 6 + b:7 + b], None, ALU.mult))
                st["d", h] = d

            def turn(n):
                i, b, h = n % 2, 4 + n % 2, n // 3
                s = S3[h % 3][:, n % 3, :]
                for m in range(3):
                    t = PE.do([st["d", h], free[b] if m == 0 else None], lambda e: e.matmul(
                        PS[:, b, m * 128:m * 128 + 128], s[:, m * 128:m * 128 + 128],
                        dg[:, h % 2, 1 if m else 0, :], start=True, stop=True))
                st["t", n] = t
                free[b] = AC.do([t, st.get(("o", n - 2)), xt2_ok], lambda e: e.activation(
                    pt[i], PS[:, b, 0:384], ACT.Copy))
                st["pt", n] = free[b]

            def values(n):
                h, g, i = n // 3, n % 3, n % 2
                b = 6 + (h // 2) % 2
                r = slice(64 * (h % 2), 64 * (h % 2) + 64)
                c0 = g * 512 + h * 64
                vt = [tok["v", c, m] for c in range(3) for m in range(2)]
                PE.go([st["pt", n], vt, free[b] if (h % 2, g) == (0, 0) else None],
                      lambda e: e.matmul(PS[r, b, 0:256], v[:, 0, c0:c0 + 64], pt[i][:, 0:256],
                                         start=(g == 0), stop=False))
                t = PE.do([], lambda e: e.matmul(PS[r, b, 128:256], v[:, 1, c0:c0 + 64],
                                                 pt[i][:, 256:384], start=False, stop=(g == 2)))
                st["o", n] = t
                if (h % 2, g) == (1, 2):
                    free[b] = DV.do([t], lambda e: e.tensor_copy(GT[:, h // 2, :], PS[:, b, 0:256]))
                    gt[h // 2] = free[b]

            pad(0)
            pad(1)
            for i in range(24 + LAG + 1):
                if i < 24:
                    scores(i)
                if i < 22:
                    pad(i + 2)
                if i < 24:
                    if i % 3 == 2:
                        soften(i // 3)
                if i >= 4 and i % 3 == 1 and i // 3 <= 8:
                    invert(i // 3 - 1)
                if LAG <= i < 24 + LAG:
                    turn(i - LAG)
                if i > LAG:
                    values(i - LAG - 1)
            return gt

        def banks():
            return [free[b] for b in range(4)]

        def second_block(x_tok):
            for layer in range(2):
                if layer == 0:
                    ahead()
                    xt_ok = rms_features(X, x_tok, split_xt("mixg0"))
                    gt = attention_a(xt_ok, None)
                    proj_out("aw_out", 8, GT, gt, add_residual(X, x_tok, 1.0, X, None))
                else:
                    gt = attention_b(x_tok)
                    proj_out("bw_out", 4, GT, gt, add_residual(X, x_tok, 1.0, X, None))
                x_tok = banks()
                if dbg == f"att{layer}":
                    return x_tok
                xt_ok = rms_features(X, x_tok, split_xt(f"ffng{layer}"))
                ffn(layer, xt_ok, xt_ok)
                x_tok = banks()
                if dbg == f"ffn{layer}":
                    return x_tok
            gr, g_ok = row("final")
            done = []
            for h in range(2):
                s = AC.do([x_tok[2 * h:2 * h + 2]], lambda e: e.activation(
                    Z[:, h, :], X[:, h, :], ACT.Square, scale=1.0 / 32, accum_out=sm[:, 430 + h:431 + h]))
                r = rstd(sm[:, 430 + h:431 + h], RMS_EPS, h, [s])
                done.append(DV.do([r, g_ok], lambda e: e.scalar_tensor_tensor(
                    out=X[:, h, :], in0=X[:, h, :], scalar=sm[:, 500 + h:501 + h], in1=gr,
                    op0=ALU.mult, op1=ALU.mult)))
            return done

        def first_block():
            gt = even_mixer()
            proj_out("ew_out", 8, GT, gt, add_residual(X, x_ok, ALPHA, Z, None))
            zt = banks()
            for layer in range(2):
                xt_ok = layer_norm(zt, 2 * layer, True)
                if dbg == f"x1_{layer}":
                    return to_tokens(XT, xt_ok, X, zt)
                zt = moe(layer, xt_ok, zt)
                if layer == 0:
                    ahead()
                    xt_ok = layer_norm(zt, 1, False)
                    if dbg == f"x2_{layer}":
                        return to_tokens(XT, xt_ok, X, zt)
                    sp = [split_x(q, XT[:, 2 * q:2 * q + 2, :], xt_ok[q]) for q in range(4)]
                    gt, x2 = odd_mixer(sp, lambda: to_tokens(XT, xt_ok, X, zt))
                    proj_out("ow_out", 8, GT, gt, add_residual(X, x2, ALPHA, Z, x2))
                    zt = banks()
            want_row("ln2_g1")
            want_row("ln2_b1")
            (gr, g_ok), (br, b_ok) = row("ln2_g1"), row("ln2_b1")
            done = []
            for h in range(2):
                mean, r, ok = moments(Z, zt, h)
                a = DV.do([ok, zt, g_ok], lambda e: e.scalar_tensor_tensor(
                    out=X[:, h, :], in0=Z[:, h, :], scalar=mean, in1=gr, op0=ALU.subtract, op1=ALU.mult))
                a = DV.do([a, b_ok], lambda e: e.scalar_tensor_tensor(
                    out=X[:, h, :], in0=X[:, h, :], scalar=r, in1=br, op0=ALU.mult, op1=ALU.add))
                done += [a, a]
            row_done("ln2_g1", done)
            row_done("ln2_b1", done)
            want_row("final")
            return done

        if dbg and dbg.startswith(("att", "ffn", "all")):
            W.used = 0
            want_row("final")
            fin = second_block([x_ok] * 4)
        else:
            fin = first_block()
            if not dbg:
                fin = second_block(fin)
        SP.wait([fin])
        if dbg:
            SP.e.wait_ge(s_br, 16)
            SP.e.wait_ge(s_bf, 16)
            for n in range(min(2, rows_used[0])):
                SP.e.wait_ge(s_row[n], 16 * ((rows_used[0] - n + 1) // 2))
            for n in range(RING):
                SP.e.wait_ge(ring_sems[n], 16 * ((min(W.used + RING, len(plan)) + RING - 1 - n) // RING))
        SP.e.dma_start(out.rearrange("(h p) d -> p h d", p=128), X[:, :, :]).then_inc(s_out, 16)
        SP.e.wait_ge(s_out, 16)


def _cols(w):
    k, n = w.shape
    return w.reshape(k // 128, 128, n // 256, 2, 128).transpose(2, 1, 3, 0, 4).reshape(n // 256, 128, -1)


def _blocks(w):
    k, n = w.shape
    return w.reshape(k // 512, 4, 128, n // 512, 512).transpose(3, 0, 2, 1, 4).reshape(k // 512 * (n // 512), 128, -1)


def _rows(w):
    k, n = w.shape
    return w.reshape(k // 256, 2, 128, n).transpose(0, 2, 1, 3).reshape(k // 256, 128, 2 * n)


def _feat(v):
    v = v.reshape(-1, v.shape[-1])
    return v.reshape(v.shape[0], -1, 128).transpose(2, 1, 0).reshape(128, -1)


def layout(i):
    c = np.ascontiguousarray
    a = {}
    a["x"] = i["x"][0]
    parts = {
        "a_dw": _feat(i["even_a_dw"][0]), "a_dw_b": _feat(i["even_a_dw_b"]), "a_ln_g": _feat(i["even_a_ln_g"]),
        "a_ln_b": _feat(i["even_a_ln_b"]), "b_dw": _feat(i["even_b_dw"][0]), "c_dw": _feat(i["odd_c_dw"][0]),
        "c_dw_b": _feat(i["odd_c_dw_b"]), "bga": _feat(i["odd_b_gate_a"].reshape(1, -1)),
        "bgx": _feat(i["odd_b_gate_x"].reshape(1, -1)), "lam": _feat(i["odd_lam"]),
        "mixg0": _feat(i["mix_norm_g_2"][0:1]), "mixg1": _feat(i["mix_norm_g_2"][1:2]),
        "kvg": _feat(i["kv_norm_g_2"].reshape(1, -1)),
        "ffng0": _feat(i["ffn_norm_g_2"][0:1]), "ffng1": _feat(i["ffn_norm_g_2"][1:2]),
        "fcw0": _feat(i["ffn_conv_w_2"][0]), "fcw1": _feat(i["ffn_conv_w_2"][1]),
        "fcb0": _feat(i["ffn_conv_b_2"][0:1]), "fcb1": _feat(i["ffn_conv_b_2"][1:2]),
        "lng0": _feat(i["ln1_g"][0:1]), "lnb0": _feat(i["ln1_b"][0:1]),
        "lng1": _feat(i["ln2_g"][0:1]), "lnb1": _feat(i["ln2_b"][0:1]),
        "lng2": _feat(i["ln1_g"][1:2]), "lnb2": _feat(i["ln1_b"][1:2]),
        "wr": i["w_router"].reshape(8, 128, 16).transpose(1, 0, 2).reshape(128, 128),
        "wf": i["a_w_in_2"][0][:, 3072:].reshape(8, 128, 16).transpose(1, 0, 2).reshape(128, 128),
    }
    for n, (at, w) in COLS.items():
        assert parts[n].shape == (128, w), n
    a["cols"] = c(np.concatenate([parts[n] for n in COLS], axis=1))
    a["b_router_rows"] = c(np.broadcast_to(i["b_router"], (128, 16)))
    a["a_b_f"] = c(i["a_b_f_2"].reshape(16, 1))
    a["rows"] = c(np.stack([i["ln2_g"][1], i["ln2_b"][1], i["final_norm_g_2"]]))
    a["even_w_in"] = c(_cols(i["even_w_in"][0]))
    a["even_w_out"] = c(_rows(i["even_w_out"][0]))
    a["odd_w_in"] = c(_cols(i["odd_w_in"][0]))
    a["odd_w_out"] = c(_rows(i["odd_w_out"][0]))
    g = np.stack([i["odd_w_gate_a"][0], i["odd_w_gate_x"][0]])
    a["odd_gates"] = c(g.reshape(2, 4, 2, 128, 256).transpose(0, 3, 1, 2, 4).reshape(2, 128, 2048))
    for k, n in (("w1", "moe_w1"), ("w3", "moe_w3"), ("w2", "moe_w2")):
        w = i[n]
        a[k] = c(w.reshape(2, 16, 4, 2, 128, 1024).transpose(0, 1, 2, 4, 3, 5).reshape(2, 16, 4, 128, 2048))
    a["a_w_in"] = c(_cols(i["a_w_in_2"][0][:, :2048]))
    a["a_w_v"] = c(_blocks(i["a_w_in_2"][0][:, 2048:3072]))
    a["a_w_out"] = c(_rows(i["a_w_out_2"][0]))
    a["w_k"] = c(_cols(i["w_kv_2"][:, :1536]))
    a["w_v"] = c(_blocks(i["w_kv_2"][:, 1536:]))
    a["b_w_q"] = c(_cols(i["b_w_q_2"][0]))
    a["b_w_out"] = c(_rows(i["b_w_out_2"][0]))
    up = [_cols(i["ffn_w_up_2"][n]) for n in range(2)]
    order = [x for p in range(11) for x in (11 + p, p)]
    a["ffn_up"] = c(np.stack([u[order] for u in up]))
    a["ffn_down"] = c(np.stack([_rows(i["ffn_w_down_2"][n]) for n in range(2)]))
    return a


def build(nc, shapes, dbg=None):
    A = {n: nc.dram_tensor(f"in_{n}", s, F32, kind="ExternalInput").ap() for n, s in shapes.items()}
    out = nc.dram_tensor("out_y", (T, D), F32, kind="ExternalOutput").ap()
    program(nc, A, out, dbg)


def kernel(**inputs):
    import concourse.bacc as _bacc
    from concourse.bass_utils import run_bass_kernel_spmd as _run

    arrays = layout({k: np.asarray(v) for k, v in inputs.items()})
    nc = _bacc.Bacc("TRN2", target_bir_lowering=False, num_devices=1)
    build(nc, {n: v.shape for n, v in arrays.items()})
    r = _run(nc, [{f"in_{n}": v for n, v in arrays.items()}], core_ids=[0])
    return r.results[0]["out_y"].reshape(1, T, D)
```

```python
from contextlib import ExitStack
import math

import numpy as np

import concourse.bass as bass
from concourse import mybir

F32 = mybir.dt.float32
F32R = mybir.dt.float32r
I32 = mybir.dt.int32
ALU = mybir.AluOpType
ACT = mybir.ActivationFunctionType
AX = mybir.AxisListType.X

T, D, NT, KD = 256, 1024, 2, 8
E, CAP = 16, 64
ALPHA = 4.0 ** 0.25
LN_EPS, RMS_EPS = 1e-5, 1e-6
RING = 10
PIECE, NPIECE = 512, 4
PE_TAPS = 12
INV, LAG = 5, 5
CH = 2048
NEG = -1e30

COLS = {}
_at = 0
for _n, _w in (("a_dw", 4 * 31), ("a_dw_b", 4), ("a_ln_g", 4), ("a_ln_b", 4), ("b_dw", 4 * 3),
               ("c_dw", 8 * 4), ("c_dw_b", 8), ("bga", 8), ("bgx", 8), ("lam", 8),
               ("mixg0", 8), ("mixg1", 8), ("kvg", 8), ("ffng0", 8), ("ffng1", 8),
               ("fcw0", 44 * 3), ("fcw1", 44 * 3), ("fcb0", 44), ("fcb1", 44),
               ("lng0", 8), ("lnb0", 8), ("lng1", 8), ("lnb1", 8), ("lng2", 8), ("lnb2", 8), ("wr", 8 * 16), ("wf", 8 * 16)):
    COLS[_n] = (_at, _w)
    _at += _w
NCOLS = _at
ROWS = ("ln2_g1", "ln2_b1", "final")


class Eng:

    def __init__(self, engine, sem):
        self.e, self.sem, self.n, self.seen = engine, sem, 0, {}

    def wait(self, toks):
        for t in toks:
            if t is None:
                continue
            if isinstance(t, list):
                self.wait(t)
                continue
            sem, val = t
            if self.seen.get(sem.name, 0) < val:
                self.e.wait_ge(sem, val)
                self.seen[sem.name] = val

    def do(self, toks, fn):
        self.wait(toks)
        fn(self.e).then_inc(self.sem, 1)
        self.n += 1
        return (self.sem, self.n)

    def go(self, toks, fn):
        self.wait(toks)
        fn(self.e)


class Stream:

    def __init__(self, sp, ring, sems, plan):
        self.sp, self.ring, self.sems, self.plan = sp, ring, sems, plan
        self.used = 0
        for n in range(RING):
            self.load(n, None)

    def load(self, n, freed):
        if n < len(self.plan):
            s = n % RING
            self.sp.wait([freed])
            src = self.plan[n][1]
            self.sp.e.dma_start(self.ring[:, s, 0:src.shape[-1]], src).then_inc(self.sems[s], 16)

    def take(self, name):
        n = self.used
        assert self.plan[n][0] == name, (self.plan[n][0], name)
        self.used += 1
        return self.ring[:, n % RING, :], (self.sems[n % RING], 16 * (n // RING + 1))

    def give_of(self, n, tok):
        self.load(n + RING, tok)

    def give(self, tok):
        self.load(self.used - 1 + RING, tok)


def program(nc, A, out, dbg=None):
    ctx = ExitStack()
    with ctx:
        def sb(name, shape, dt=F32):
            return ctx.enter_context(nc.sbuf_tensor(name, shape, dt))

        def sem(name):
            return ctx.enter_context(nc.semaphore(name))

        PE = Eng(nc.tensor, sem("s_pe"))
        AC = Eng(nc.scalar, sem("s_act"))
        DV = Eng(nc.vector, sem("s_dve"))
        PL = Eng(nc.gpsimd, sem("s_pool"))
        SP = Eng(nc.sync, sem("s_sp"))
        ring_sems = [sem(f"s_w{i}") for i in range(RING)]
        s_c, s_x, s_br, s_bf, s_out = sem("s_c"), sem("s_x"), sem("s_br"), sem("s_bf"), sem("s_out")
        s_row = sem("s_row")

        ring = sb("ring", [128, RING, CH])
        PS = ctx.enter_context(nc.psum_tensor("PS", [128, 8, 512], F32))
        cols = sb("cols", [128, NCOLS])
        X = sb("X", [128, NT, D])
        Z = sb("Z", [128, NT, D])
        XT = sb("XT", [128, KD, T])
        F = sb("F", [128, 13568])
        GT = F[:, 0:2048].rearrange("p (k t) -> p k t", k=8)
        ident = sb("ident", [128, 128])
        ones = sb("ones", [128, 256])
        mean512 = sb("mean512", [128, 128])
        upper = sb("upper", [128, 128])
        iota64 = sb("iota64", [128, 64])
        cmask = sb("cmask", [128, 256])
        mhalf = sb("mhalf", [128, 2])
        brt = sb("brt", [16, 1])
        lgT = sb("lgT", [16, 256])
        bft = sb("bft", [16, 1])
        wh = sb("wh", [128, NPIECE, PIECE], F32R)
        wl = sb("wl", [128, NPIECE, PIECE], F32R)
        xh = sb("xh", [128, KD, T], F32R)
        xl = sb("xl", [128, KD, T], F32R)
        nc2 = sb("nc2", [128, 2, 384], F32R)
        nch, ncl = nc2[:, 0, :], nc2[:, 1, :]
        wfh = sb("wfh", [128, 128], F32R)
        wfl = sb("wfl", [128, 128], F32R)
        identr = sb("identr", [128, 16], F32R)
        sm = sb("sm", [128, 640])
        it = sb("it", [128, 8], I32)

        def col(name):
            a, w = COLS[name]
            return cols[:, a:a + w]

        def fv(a, k, t=T):
            return F[:, a:a + k * t].rearrange("p (k t) -> p k t", k=k)

        AC.e.dma_start(X[:, :, :], A["x"].rearrange("(h p) d -> p h d", p=128)).then_inc(s_x, 16)
        AC.e.dma_start(cols[:, :], A["cols"]).then_inc(s_c, 16)
        AC.e.dma_start(brt[:, :], A["b_router"]).then_inc(s_br, 16)
        AC.e.dma_start(bft[:, :], A["a_b_f"]).then_inc(s_bf, 16)
        c_ok, x_ok, br_ok, bf_ok = (s_c, 16), (s_x, 16), (s_br, 16), (s_bf, 16)

        t0 = PL.do([], lambda e: e.memset(ident[:, :], 0.0))
        k_ident = PL.do([t0], lambda e: e.affine_select(
            out=ident[:, :], in_=ident[:, :], compare_op=ALU.not_equal, fill=1.0, base=0,
            pattern=[[-1, 128]], channel_multiplier=1))
        k_identr = PL.do([k_ident], lambda e: e.tensor_copy(identr[:, :], ident[:, 0:16]))
        k_ones = PL.do([], lambda e: e.memset(ones[:, :], 1.0))
        k_mean = PL.do([], lambda e: e.memset(mean512[:, :], 1.0 / 512))
        k_mhalf = PL.do([], lambda e: e.memset(mhalf[:, :], -0.5))
        t0 = PL.do([], lambda e: e.memset(upper[:, :], 1.0))
        k_upper = PL.do([t0], lambda e: e.affine_select(
            out=upper[:, :], in_=upper[:, :], compare_op=ALU.is_gt, fill=0.0, base=0,
            pattern=[[1, 128]], channel_multiplier=-1))
        k_iota = PL.do([], lambda e: e.iota(iota64[:, :], pattern=[[1, 64]], base=1, channel_multiplier=0,
                                            allow_small_or_imprecise_dtypes=True))
        t0 = PL.do([], lambda e: e.memset(cmask[:, :], 0.0))
        k_cmask = PL.do([t0], lambda e: e.affine_select(
            out=cmask[:, :], in_=cmask[:, :], compare_op=ALU.is_ge, fill=NEG, base=128,
            pattern=[[-1, 256]], channel_multiplier=1))
        plan = []

        def add(name, ap, order, split=True):
            for c in order:
                plan.append((name, ap[c], split))

        def add_moe(layer):
            for e in range(E):
                for w in ("w1", "w3", "w2"):
                    add(f"{w}{layer}", A[w][layer, e], range(4), False)

        add("ew_in", A["even_w_in"], [2, 3, 0, 1, 6, 7, 8, 9, 4, 5])
        add("ew_out", A["even_w_out"], [2, 3, 0, 1])
        add_moe(0)
        add("ow_in", A["odd_w_in"], [4, 5, 6, 7, 0, 1])
        add("gates", A["odd_gates"], range(2), False)
        add("ow_in", A["odd_w_in"], [2, 3])
        add("ow_out", A["odd_w_out"], range(4))
        add_moe(1)
        add("aq_in", A["a_w_in"], range(8))
        add("av_in", A["a_w_v"], range(4))
        add("aw_out", A["a_w_out"], range(4))
        add("up0", A["ffn_up"][0], range(22))
        add("down0", A["ffn_down"][0], range(11))
        add("wk", A["w_k"], range(6))
        add("wv", A["w_v"], range(6))
        add("bwq", A["b_w_q"], range(6))
        add("bw_out", A["b_w_out"], range(2))
        add("up1", A["ffn_up"][1], range(22))
        add("down1", A["ffn_down"][1], range(11))
        if dbg and dbg.startswith(("att", "ffn", "all")):
            plan = plan[[n for n, _, _ in plan].index("aq_in"):]
        W = Stream(SP, ring, ring_sems, plan)

        free = [None] * 8
        rows2 = F[:, 0:2048].rearrange("p (r d) -> p r d", r=2)
        rows_ok = (s_row, 32)
        row_loads = []

        def load_rows(free_tok):
            AC.wait([free_tok])
            for r in range(2):
                AC.e.dma_start(rows2[:, r, :], A["rows"][r, :].partition_broadcast(128)).then_inc(s_row, 16)
                row_loads.append(r)

        def f32(ap):
            return ap.bitcast(F32)

        pieces = []
        piece_free = [None] * NPIECE
        state = {"issued": 0, "at": CH, "chunk": None}

        def dense_next():
            return W.used < len(plan) and plan[W.used][2]

        def ahead(upto=NPIECE):
            while len(pieces) < min(upto, NPIECE) and (state["at"] < CH or dense_next()):
                if state["at"] == CH:
                    state["name"] = plan[W.used][0]
                    state["chunk"] = W.take(state["name"])
                    state["at"] = 0
                w, w_ok = state["chunk"]
                src = w[:, state["at"]:state["at"] + PIECE]
                i = state["issued"] % NPIECE
                state["issued"] += 1
                state["at"] += PIECE
                a = AC.do([w_ok, piece_free[i]], lambda e: e.activation(wh[:, i, :], src, ACT.Copy))
                b = DV.do([a], lambda e: e.tensor_tensor(wl[:, i, :], src, f32(wh[:, i, :]), ALU.subtract))
                if state["at"] == CH:
                    W.give(b)
                pieces.append((state["name"], i, b))

        def piece(name, n=0):
            got, i, tok = pieces[n]
            assert got == name, (got, name)
            return wh[:, i, :], wl[:, i, :], tok

        def piece_done(tok):
            piece_free[pieces.pop(0)[1]] = tok
            ahead()

        def mm3(out, lt, rt, toks, first, last, mark):
            PE.go(toks, lambda e: e.matmul(out, lt[1], rt[0], start=first, stop=False))
            PE.go([], lambda e: e.matmul(out, lt[0], rt[1], start=False, stop=False))
            f = (lambda e: e.matmul(out, lt[0], rt[0], start=False, stop=last))
            return PE.do([], f) if mark else PE.go([], f)

        x_free = [None] * 4

        def split_xg(q, src, g, src_tok):
            for k in (2 * q, 2 * q + 1):
                a = AC.do([src_tok, x_free[q], c_ok], lambda e: e.activation(
                    xh[:, k, :], src[:, k % 2, :], ACT.Copy, scale=g[:, k:k + 1]))
            for k in (2 * q, 2 * q + 1):
                b = DV.do([a], lambda e: e.scalar_tensor_tensor(
                    out=xl[:, k, :], in0=src[:, k % 2, :], scalar=g[:, k:k + 1], in1=f32(xh[:, k, :]),
                    op0=ALU.mult, op1=ALU.subtract))
            return b

        def split_x(q, src, src_tok):
            s = q % 4
            d = slice(2 * s, 2 * s + 2)
            a = AC.do([src_tok, x_free[s]], lambda e: e.activation(xh[:, d, :], src, ACT.Copy))
            return DV.do([a], lambda e: e.tensor_tensor(xl[:, d, :], src, f32(xh[:, d, :]), ALU.subtract))

        def to_features(src, src_toks, evac, first=0, by=None):
            toks = []
            for h in range(2):
                for q in range(4):
                    b = first + q
                    for j in range(2):
                        k = 2 * q + j
                        w = [src_toks[h], k_ident, free[b]]
                        o = PS[:, b, j * 256 + h * 128:j * 256 + h * 128 + 128]
                        s = src[:, h, k * 128:k * 128 + 128]
                        if by:
                            f = (lambda e: e.matmul(o, s, by[h], start=True, stop=True))
                        else:
                            f = (lambda e: e.transpose(o, s, ident[:, :]))
                        if (h, j) == (1, 1):
                            t = PE.do(w, f)
                        else:
                            PE.go(w, f)
                    if h:
                        if q == 0:
                            ahead(2)
                        free[b] = evac(q, PS[:, b, :].rearrange("p (k t) -> p k t", k=2), t)
                        toks.append(free[b])
            ahead()
            return toks

        def to_tokens(src, src_toks, dst, dst_free):
            toks = []
            for h in range(2):
                for d in range(2):
                    b = 2 * h + d
                    for kk in range(4):
                        k = 4 * d + kk
                        t = PE.do([src_toks[k // 2], free[b] if kk == 0 else None], lambda e: e.transpose(
                            PS[:, b, kk * 128:kk * 128 + 128], src[:, k, h * 128:h * 128 + 128], ident[:, :]))
                    free[b] = AC.do([t, dst_free], lambda e: e.activation(
                        dst[:, h, d * 512:d * 512 + 512], PS[:, b, :], ACT.Copy))
                    toks.append(free[b])
            return toks

        deferred = []

        def defer(n, fn):
            deferred.append([n, fn])

        def run_deferred(all_of_it=False):
            for d in deferred:
                d[0] -= 1
            while deferred and (all_of_it or deferred[0][0] <= 0):
                deferred.pop(0)[1]()

        def proj_features(name, n, xt_toks, evac, banks, start=0, between=None, flush=True):
            for c in range(start, start + n):
                b = banks[c % len(banks)]
                for j in range(2):
                    for k in range(8):
                        if k % 4 == 0:
                            h, l, w_ok = piece(name)
                        a = (k % 4) * 128
                        t = mm3(PS[:, b, j * 256:j * 256 + 256], (h[:, a:a + 128], l[:, a:a + 128]),
                                (xh[:, k, :], xl[:, k, :]),
                                [xt_toks[k // 2], w_ok, free[b] if (j, k) == (0, 0) else None],
                                k == 0, k == 7, k % 4 == 3)
                        if k % 4 == 3:
                            piece_done(t)
                            run_deferred()
                            if between:
                                between(c)
                evac(c, b, PS[:, b, :].rearrange("p (k t) -> p k t", k=2), t)
            x_free[:] = [t] * 4
            if flush:
                run_deferred(True)

        def proj_cols(name, n, xt_toks, evac, banks):
            for c in range(n):
                for k in range(8):
                    h, l, w_ok = piece(name)
                    for m in range(2):
                        b, x = banks[(2 * c + m) % len(banks)], slice(m * 128, m * 128 + 128)
                        t = mm3(PS[:, b, :], (xh[:, k, x], xl[:, k, x]), (h, l),
                                [xt_toks[k // 2], w_ok, free[b] if k == 0 else None], k == 0, k == 7, m == 1)
                    piece_done(t)
                for m in range(2):
                    b = banks[(2 * c + m) % len(banks)]
                    free[b] = evac(c, m, PS[:, b, :], t)
            x_free[:] = [t] * 4

        def proj_out(name, nk, gt, gt_toks, evac, half_done=None):
            for _ in proj_out_steps(name, nk, gt, gt_toks, evac, half_done):
                pass

        def proj_out_steps(name, nk, gt, gt_toks, evac, half_done=None, prime=False):
            nq = nk // 2
            toks = {}

            def split(upto):
                while len(toks) < min(nq, upto) and gt_toks[2 * len(toks) + 1] is not None:
                    q = len(toks)
                    toks[q] = split_x(q, gt[:, 2 * q:2 * q + 2, :], [gt_toks[2 * q], gt_toks[2 * q + 1]])

            if prime:
                split(2)
                yield
            for q in range(nq - 1):
                split(q + 3)
                for kk in range(2):
                    k = 2 * q + kk
                    s = k % 8
                    for d in range(2):
                        h, l, w_ok = piece(name)
                        for m in range(2):
                            b, x = 2 * m + d, slice(m * 128, m * 128 + 128)
                            t = mm3(PS[:, b, :], (xh[:, s, x], xl[:, s, x]), (h, l),
                                    [toks[q], w_ok, free[b] if k == 0 else None], k == 0, False, m == 1)
                        piece_done(t)
                x_free[q % 4] = t
                yield
            split(nq)
            for m in range(2):
                x = slice(m * 128, m * 128 + 128)
                for kk in range(2):
                    s = (nk - 2 + kk) % 8
                    for d in range(2):
                        h, l, w_ok = piece(name, 2 * kk + d)
                        t = mm3(PS[:, 2 * m + d, :], (xh[:, s, x], xl[:, s, x]), (h, l),
                                [toks[nq - 1], w_ok], False, kk == 1, kk == 1)
                        if kk:
                            free[2 * m + d] = evac(m, d, PS[:, 2 * m + d, :], t)
                if half_done:
                    half_done(m, free[2 * m:2 * m + 2])
            x_free[(nq - 1) % 4] = t
            for _ in range(4):
                piece_free[pieces.pop(0)[1]] = t

        def rstd(var, eps, h, toks):
            a = DV.do(toks, lambda e: e.tensor_scalar(sm[:, 490 + h:491 + h], var, eps, None, ALU.add))
            return PL.do([a, k_mhalf], lambda e: e.tensor_tensor(
                sm[:, 500 + h:501 + h], sm[:, 490 + h:491 + h], mhalf[:, 0:1], ALU.pow))

        def moments(src, src_toks, h):
            st = sm[:, 400 + 12 * h:412 + 12 * h].rearrange("p (d s) -> p d s", d=2)
            mv = sm[:, 424 + 2 * h:426 + 2 * h]
            tt = [DV.do([src_toks], lambda e: e.bn_stats(st[:, d, :], src[:, h, d * 512:d * 512 + 512]))
                  for d in range(2)]
            a = DV.do(tt, lambda e: e.bn_aggr(mv, st))
            return mv[:, 0:1], sm[:, 500 + h:501 + h], [a, rstd(mv[:, 1:2], LN_EPS, h, [a])]

        def norm_half(h, toks):
            mean, r, ok = moments(Z, toks, h)
            if h == 0:
                nm = PL.do([ok], lambda e: e.tensor_tensor(sm[:, 504:505], mean, r, ALU.mult))
                nm = PL.do([nm], lambda e: e.tensor_scalar(sm[:, 504:505], sm[:, 504:505], -1.0, None, ALU.mult))
                return AC.do([nm], lambda e: e.activation(
                    Z[:, h, :], Z[:, h, :], ACT.Identity, scale=r, bias=sm[:, 504:505]))
            return DV.do([ok], lambda e: e.tensor_scalar(
                Z[:, h, :], Z[:, h, :], mean, r, ALU.subtract, ALU.mult))

        def normed(n, done):
            g, b = col(f"lng{n}"), col(f"lnb{n}")

            def evac(q, ps, t):
                tt = []
                for k in (2 * q, 2 * q + 1):
                    if q % 2:
                        tt.append(DV.do([t, c_ok], lambda e: e.tensor_scalar(
                            XT[:, k, :], ps[:, k % 2, :], g[:, k:k + 1], b[:, k:k + 1], ALU.mult, ALU.add)))
                    else:
                        tt.append(AC.do([t, c_ok], lambda e: e.activation(
                            XT[:, k, :], ps[:, k % 2, :], ACT.Identity, scale=g[:, k:k + 1], bias=b[:, k:k + 1])))
                return tt

            return to_features(Z, done, evac, first=4)

        def rms_half(h, toks):
            s = AC.do([toks], lambda e: e.activation(
                Z[:, h, :], X[:, h, :], ACT.Square, scale=1.0 / 32, accum_out=sm[:, 430 + h:431 + h]))
            r = rstd(sm[:, 430 + h:431 + h], RMS_EPS, h, [s])
            return DV.do([r], lambda e: e.tensor_scalar(
                Z[:, h, 0:128], ident[:, :], sm[:, 500 + h:501 + h], None, ALU.mult))

        def rms_features(done, evac):
            return to_features(X, done, evac, first=4, by=[Z[:, 0, 0:128], Z[:, 1, 0:128]])

        def split_xt(gname=None):
            g = gname and col(gname)

            def evac(q, ps, t):
                d = slice(2 * q, 2 * q + 2)
                if g is None:
                    a = AC.do([t, x_free[q]], lambda e: e.activation(xh[:, d, :], ps, ACT.Copy))
                    return DV.do([a], lambda e: e.tensor_tensor(xl[:, d, :], ps, f32(xh[:, d, :]), ALU.subtract))
                for k in (2 * q, 2 * q + 1):
                    a = AC.do([t, x_free[q], c_ok], lambda e: e.activation(
                        xh[:, k, :], ps[:, k % 2, :], ACT.Copy, scale=g[:, k:k + 1]))
                for k in (2 * q, 2 * q + 1):
                    b = DV.do([a], lambda e: e.scalar_tensor_tensor(
                        out=xl[:, k, :], in0=ps[:, k % 2, :], scalar=g[:, k:k + 1], in1=f32(xh[:, k, :]),
                        op0=ALU.mult, op1=ALU.subtract))
                return b
            return evac

        def even_mixer(half_done):
            ahead()
            xt_ok = to_features(X, [x_ok, x_ok], split_xt())
            aP = F[:, 2048:2048 + 4 * 286].rearrange("p (k t) -> p k t", k=4)
            bP = F[:, 3200:3200 + 4 * 258].rearrange("p (k t) -> p k t", k=4)
            sg = fv(4300, 4)
            acc = fv(5400, 4)
            bc = fv(6500, 4)
            bacc = fv(7600, 4)
            sq = fv(8700, 4)
            rs = F[:, 9800:10056]
            dgs = [F[:, 10056 + i * 128:10184 + i * 128] for i in range(6)]
            b2 = sm[:, 8:12]
            h0 = DV.do([c_ok], lambda e: e.tensor_scalar(b2, col("a_dw_b"), 2.0, None, ALU.mult))
            gh, bh = sm[:, 0:4], sm[:, 4:8]
            z1 = DV.do([], lambda e: e.memset(aP[:, :, 0:30], 0.0))
            z2 = DV.do([], lambda e: e.memset(bP[:, :, 0:2], 0.0))
            h1 = DV.do([c_ok], lambda e: e.tensor_scalar(gh, col("a_ln_g"), 0.5, None, ALU.mult))
            h2 = DV.do([c_ok], lambda e: e.tensor_scalar(bh, col("a_ln_b"), 0.5, None, ALU.mult))
            tok = {}
            aw = col("a_dw").rearrange("p (c k) -> p c k", c=4)
            last = [None] * 4
            steps = [(k, c) for half in range(2) for k in range(PE_TAPS, 31) for c in (2 * half, 2 * half + 1)]
            pe_steps = [(k, c) for c in range(4) for k in range(PE_TAPS)]
            dg_free = [None] * len(dgs)

            def convolve(n):
                for _ in range(min(n, len(steps))):
                    k, c = steps.pop(0)
                    src, wk = aP[:, c, k:k + 256], aw[:, c, k:k + 1]
                    if k == PE_TAPS:
                        last[c] = DV.do([tok["a", c // 2], z1, h0, c_ok], lambda e: e.tensor_scalar(
                            acc[:, c, :], src, wk, b2[:, c:c + 1], ALU.mult, ALU.add))
                    else:
                        last[c] = DV.do([last[c]], lambda e: e.scalar_tensor_tensor(
                            out=acc[:, c, :], in0=src, scalar=wk, in1=acc[:, c, :],
                            op0=ALU.mult, op1=ALU.add))

            ready = []

            def diagonals(n):
                while len(ready) < n and pe_steps:
                    k, c = pe_steps.pop(0)
                    i = len(pe_steps) % len(dgs)
                    ready.append((k, c, i, AC.do([dg_free[i], k_ident, c_ok], lambda e: e.activation(
                        dgs[i], ident[:, :], ACT.Copy, scale=aw[:, c, k:k + 1]))))

            def convolve_pe(n):
                for _ in range(n):
                    if not ready:
                        return
                    k, c, i, d = ready.pop(0)
                    b, o = 6 + c // 2, (c % 2) * 256
                    dg_free[i] = PE.do([d, tok["a", c // 2], z1], lambda e: e.matmul(
                        PS[:, b, o:o + 256], dgs[i], aP[:, c, k:k + 256], start=(k == 0), stop=(k == PE_TAPS - 1)))
                    tok["pe", c] = dg_free[i]
                    diagonals(4)

            bw = col("b_dw").rearrange("p (c k) -> p c k", c=4)
            blast = [None] * 4
            b_steps = [(k, c) for c in range(4) for k in range(3)]
            gt = [None] * 8

            def convolve_b(n):
                for _ in range(min(n, len(b_steps))):
                    k, c = b_steps.pop(0)
                    src, wk = bP[:, c, k:k + 256], bw[:, c, k:k + 1]
                    if k == 0:
                        blast[c] = AC.do([tok["x", c // 2], z2, c_ok], lambda e: e.activation(
                            bacc[:, c, :], src, ACT.Copy, scale=wk))
                    else:
                        blast[c] = DV.do([blast[c]], lambda e: e.scalar_tensor_tensor(
                            out=bacc[:, c, :], in0=src, scalar=wk, in1=bacc[:, c, :],
                            op0=ALU.mult, op1=ALU.add))

            def between(c):
                if c == 8:
                    convolve_pe(2)
                    convolve_b(4)
                    convolve(1)
                    return
                if c == 3:
                    diagonals(4)
                if c >= 4:
                    convolve_pe(2)
                    convolve(4)

            def evac(c, b, ps, t):
                free[b] = evacuate(c, ps, t)

            def evacuate(c, ps, t):
                i = 2 * (c % 2)
                if c < 2:
                    tok["g", c] = AC.do([t], lambda e: e.activation(sg[:, i:i + 2, :], ps, ACT.Tanh, scale=0.5))
                    return tok["g", c]
                if c < 4:
                    tok["a", c - 2] = DV.do([t, tok["g", c - 2]], lambda e: e.scalar_tensor_tensor(
                        out=aP[:, i:i + 2, 30:286], in0=sg[:, i:i + 2, :], scalar=1.0, in1=ps,
                        op0=ALU.add, op1=ALU.mult))
                    return tok["a", c - 2]
                if c < 6:
                    tok["c", c - 4] = AC.do([t], lambda e: e.activation(bc[:, i:i + 2, :], ps, ACT.Copy))
                    return tok["c", c - 4]
                if c < 8:
                    tok["x", c - 6] = DV.do([t, tok["c", c - 6]], lambda e: e.tensor_tensor(
                        bP[:, i:i + 2, 2:258], bc[:, i:i + 2, :], ps, ALU.mult))
                    return tok["x", c - 6]
                i = 2 * (c - 8)
                gt[i] = gt[i + 1] = DV.do([t, blast], lambda e: e.tensor_tensor(
                    GT[:, i:i + 2, :], bacc[:, i:i + 2, :], ps, ALU.mult))
                return gt[i]

            proj_features("ew_in", 10, xt_ok, evac, list(range(6)), between=between)
            out = proj_out_steps("ew_out", 8, GT, gt, add_residual(X, x_ok, ALPHA, Z, None), half_done)
            convolve_pe(len(pe_steps))
            next(out)
            convolve(len(steps))
            for c in range(4):
                b, o = 6 + c // 2, (c % 2) * 256
                last[c] = DV.do([last[c], tok["pe", 2 * (c // 2) + 1]], lambda e: e.tensor_tensor(
                    acc[:, c, :], acc[:, c, :], PS[:, b, o:o + 256], ALU.add))
                free[b] = last[c]
            for c in range(4):
                m = PE.do([last[c], k_mean, free[4]], lambda e: e.matmul(
                    PS[:, 4, 0:256], mean512[:, :], acc[:, c, :], start=(c == 0), stop=(c == 3)))
            d = DV.do([m], lambda e: e.tensor_tensor(
                acc, acc, PS[:, 4, 0:256].unsqueeze(1).to_broadcast([128, 4, 256]), ALU.subtract))
            free[4] = d
            s = AC.do([d], lambda e: e.activation(sq, acc, ACT.Square))
            var = PS[:, 5, 0:2]
            for h in range(2):
                for c in range(4):
                    m = PE.do([s, free[5]], lambda e: e.matmul(
                        var[:, h:h + 1], sq[:, c, h * 128:h * 128 + 128], mean512[:, 0:1],
                        start=(c == 0), stop=(c == 3)))
            for h in range(2):
                r = rstd(var[:, h:h + 1], 4.0 * LN_EPS, h, [m])
                dg = DV.do([r, s], lambda e: e.tensor_scalar(
                    rs[:, h * 128:h * 128 + 128], ident[:, :], sm[:, 500 + h:501 + h], None, ALU.mult))
            for h in range(2):
                r = PE.do([dg, k_ones, free[5], free[4]], lambda e: e.matmul(
                    PS[:, 4, h * 128:h * 128 + 128], ones[:, 0:128], rs[:, h * 128:h * 128 + 128],
                    start=True, stop=True))
            d = DV.do([r, d, s], lambda e: e.tensor_tensor(
                acc, acc, PS[:, 4, 0:256].unsqueeze(1).to_broadcast([128, 4, 256]), ALU.mult))
            free[4] = free[5] = d
            for c in range(4):
                y = DV.do([d, h1, h2], lambda e: e.tensor_scalar(
                    acc[:, c, :], acc[:, c, :], gh[:, c:c + 1], bh[:, c:c + 1], ALU.mult, ALU.add))
                th = AC.do([y, m], lambda e: e.activation(sq[:, c, :], acc[:, c, :], ACT.Tanh))
                gt[4 + c] = DV.do([th], lambda e: e.scalar_tensor_tensor(
                    out=GT[:, 4 + c, :], in0=sq[:, c, :], scalar=1.0, in1=acc[:, c, :],
                    op0=ALU.add, op1=ALU.mult))
            for _ in out:
                pass

        def add_residual(x, x_tok, scale, dst, dst_free):
            def evac(h, d, ps, t):
                sl = slice(d * 512, d * 512 + 512)
                if scale == 1.0:
                    return DV.do([t, x_tok, dst_free], lambda e: e.tensor_tensor(
                        dst[:, h, sl], x[:, h, sl], ps, ALU.add))
                return DV.do([t, x_tok, dst_free], lambda e: e.scalar_tensor_tensor(
                    out=dst[:, h, sl], in0=x[:, h, sl], scalar=scale, in1=ps, op0=ALU.mult, op1=ALU.add))
            return evac

        odd_const = {}

        def odd_constants():
            sp = [sm[:, 512 + i * 8:520 + i * 8] for i in range(6)]
            hb = sm[:, 560:576]
            lam = col("lam")
            t = AC.do([c_ok], lambda e: e.activation(sp[0], lam, ACT.Abs))
            t = AC.do([t], lambda e: e.activation(sp[1], sp[0], ACT.Exp, scale=-1.0))
            u = DV.do([t], lambda e: e.tensor_scalar(sp[2], sp[1], 1.0, None, ALU.add))
            t = AC.do([u], lambda e: e.activation(sp[3], sp[2], ACT.Ln))
            t = AC.do([t], lambda e: e.activation(sp[4], sp[3], ACT.Tanh, scale=0.5))
            v = DV.do([t], lambda e: e.tensor_scalar(sp[5], sp[4], -1.0, 1.0, ALU.mult, ALU.add))
            v = DV.do([v], lambda e: e.reciprocal(sp[5], sp[5]))
            v = DV.do([v], lambda e: e.scalar_tensor_tensor(out=sp[4], in0=sp[4], scalar=2.0, in1=sp[5],
                                                            op0=ALU.mult, op1=ALU.mult))
            v = DV.do([v], lambda e: e.tensor_tensor(sp[4], sp[4], sp[1], ALU.subtract))
            u = DV.do([v], lambda e: e.reciprocal(sp[2], sp[2]))
            v = DV.do([u], lambda e: e.tensor_tensor(sp[4], sp[4], sp[2], ALU.mult))
            v = DV.do([v], lambda e: e.tensor_tensor(sp[3], sp[3], sp[4], ALU.subtract))
            u = DV.do([c_ok], lambda e: e.tensor_scalar(sp[0], lam, -1.0, 0.0, ALU.mult, ALU.max))
            v = DV.do([v, u], lambda e: e.tensor_tensor(sp[3], sp[3], sp[0], ALU.add))
            sp2 = sp[1]
            v_sp = DV.do([v], lambda e: e.tensor_scalar(sp2, sp[3], 2.0, None, ALU.mult))
            v_hb = DV.do([c_ok], lambda e: e.tensor_scalar(
                hb, cols[:, COLS["bga"][0]:COLS["bga"][0] + 16], 0.5, None, ALU.mult))
            odd_const.update(sp2=sp2, v_sp=v_sp, hb=hb, v_hb=v_hb)

        def odd_mixer(xt_ok, tokens, half_done):
            y, xc, Tt, ig, R = (fv(a, 8) for a in (2048, 4096, 6144, 8192, 10240))
            gq = [F[:, 12288 + i * 512:12800 + i * 512].rearrange("p (k t) -> p k t", k=2) for i in range(2)]
            sp2, v_sp, hb, v_hb = (odd_const[n] for n in ("sp2", "v_sp", "hb", "v_hb"))
            cw = col("c_dw").rearrange("p (c k) -> p c k", c=8)
            cb = col("c_dw_b")
            tok = {}
            two = (lambda ap, h: ap[:, 2 * h:2 * h + 2, :])

            def evac_x(c, bank, ps, t):
                for j in range(2):
                    ch = 2 * c + j
                    a = AC.do([t, c_ok, xt_ok], lambda e: e.activation(
                        xc[:, ch, :], ps[:, j, :], ACT.Identity, scale=cw[:, ch, 3:4], bias=cb[:, ch:ch + 1]))

                def rest():
                    b = [a, a]
                    for k in (2, 1, 0):
                        for j in range(2):
                            ch, n = 2 * c + j, 3 - k
                            b[j] = DV.do([b[j]], lambda e: e.scalar_tensor_tensor(
                                out=xc[:, ch, n:256], in0=ps[:, j, 0:256 - n], scalar=cw[:, ch, k:k + 1],
                                in1=xc[:, ch, n:256], op0=ALU.mult, op1=ALU.add))
                    tok["x", c] = free[bank] = b
                defer(1, rest)

            def evac_y(c, bank, ps, t):
                i = c - 4
                q, yy = gq[i % 2], two(y, i)
                s = AC.do([t, xt_ok], lambda e: e.activation(yy, ps, ACT.Copy))
                g = AC.do([tok.get(("y", i - 2)), xt_ok, s], lambda e: e.activation(q, ps, ACT.Square))

                free[bank] = g
                st = {}

                def first():
                    a = DV.do([g], lambda e: e.tensor_scalar(q, q, 0.044715, 1.0, ALU.mult, ALU.add))
                    st["a"] = DV.do([a], lambda e: e.tensor_tensor(q, q, yy, ALU.mult))

                def second():
                    st["a"] = AC.do([st["a"]], lambda e: e.activation(
                        q, q, ACT.Tanh, scale=math.sqrt(2.0 / math.pi)))

                def third():
                    tok["y", i] = DV.do([st["a"]], lambda e: e.scalar_tensor_tensor(
                        out=yy, in0=q, scalar=1.0, in1=yy, op0=ALU.add, op1=ALU.mult))

                defer(1, first)
                defer(2, second)
                defer(3, third)

            proj_features("ow_in", 4, xt_ok, evac_x, list(range(4)))
            proj_features("ow_in", 2, xt_ok, evac_y, list(range(8)), start=4)
            w = [W.take("gates") for _ in range(2)]
            wv = [ap.rearrange("p (h k n) -> p h k n", h=4, k=2) for ap, _ in w]
            ahead_after = W.used
            ahead()

            def gate(g, h):
                b = 4 * g + h
                for j in range(2):
                    for k in range(2):
                        t = PE.do([w[g][1], tok["x", h], free[b]], lambda e: e.matmul(
                            PS[:, b, j * 256:j * 256 + 256], wv[g][:, h, k, j * 128:j * 128 + 128],
                            xc[:, 2 * h + k, :], start=(k == 0), stop=(k == 1)))
                dst = ig if g else Tt
                for j in range(2):
                    c = 2 * h + j
                    free[b] = AC.do([t, v_hb], lambda e: e.activation(
                        dst[:, c, :], PS[:, b, j * 256:j * 256 + 256], ACT.Tanh, scale=0.5,
                        bias=hb[:, 8 * g + c:8 * g + c + 1]))
                return t

            def decay(i):
                d = slice(4 * i, 4 * i + 4)
                for c in range(4 * i, 4 * i + 4):
                    b = DV.do([free[c // 2], v_sp], lambda e: e.tensor_scalar(
                        Tt[:, c, :], Tt[:, c, :], sp2[:, c:c + 1], sp2[:, c:c + 1], ALU.mult, ALU.add))
                a = AC.do([b], lambda e: e.activation(R[:, d, :], Tt[:, d, :], ACT.Exp, scale=-2.0))
                tok["a", 2 * i] = tok["a", 2 * i + 1] = a

            for h in range(4):
                t0 = gate(0, h)
                if h % 2:
                    decay(h // 2)
            for h in range(4):
                t1 = gate(1, h)
                a = DV.do([free[4 + h], t1], lambda e: e.scalar_tensor_tensor(
                    out=two(xc, h), in0=two(ig, h), scalar=1.0, in1=two(xc, h), op0=ALU.add, op1=ALU.mult))
                tok["b", h] = DV.do([a, tok["a", h]], lambda e: e.scalar_tensor_tensor(
                    out=two(xc, h), in0=two(R, h), scalar=1.0, in1=two(xc, h), op0=ALU.add, op1=ALU.mult))
            W.give_of(ahead_after - 2, t0)
            W.give_of(ahead_after - 1, t1)
            for i in range(2):
                d = slice(4 * i, 4 * i + 4)
                tok["T", i] = AC.do([tok["a", 2 * i]], lambda e: e.activation(Tt[:, d, :], Tt[:, d, :], ACT.Tanh))
            for i in range(2):
                d = slice(4 * i, 4 * i + 4)
                tok["q", 2 * i] = tok["q", 2 * i + 1] = AC.do([tok["T", i]], lambda e: e.activation(
                    Tt[:, d, :], Tt[:, d, :], ACT.Sqrt, scale=0.25))
            gt = [None] * 8

            def recur(h):
                b = DV.do([tok["q", h], tok["b", h]], lambda e: e.tensor_tensor(
                    two(xc, h), two(xc, h), two(Tt, h), ALU.mult))
                for c in (2 * h, 2 * h + 1):
                    s = DV.do([b, tok["a", h]], lambda e: e.tensor_tensor_scan(
                        ig[:, c, :], R[:, c, :], xc[:, c, :], 0.0, ALU.mult, ALU.add))
                tok["h", h] = s

            def join(h):
                t = DV.do([tok["h", h], tok["y", h]], lambda e: e.scalar_tensor_tensor(
                    out=two(GT, h), in0=two(y, h), scalar=0.5, in1=two(ig, h), op0=ALU.mult, op1=ALU.mult))
                gt[2 * h] = gt[2 * h + 1] = t

            proj_features("ow_in", 1, xt_ok, evac_y, list(range(8)), start=6)
            recur(0)
            join(0)
            proj_features("ow_in", 1, xt_ok, evac_y, list(range(8)), start=7, flush=False)
            x2 = [None]
            out = proj_out_steps("ow_out", 8, GT, gt, (lambda *a: add_residual(X, x2[0], ALPHA, Z, x2[0])(*a)),
                                 half_done, True)
            next(out)
            x2[0] = tokens()
            recur(1)
            join(1)
            run_deferred(True)
            next(out)
            for h in (2, 3):
                recur(h)
                join(h)
            for _ in out:
                pass

        def moe(layer, xt_ok, x_free):
            S = F[:, 0:2048].rearrange("p (h n) -> p h n", h=2)
            Gs = [F[:, 2048 + i * 2048:4096 + i * 2048].rearrange("p (h n) -> p h n", h=2) for i in range(2)]
            Gt = [F[:, 6144 + i * 512:6656 + i * 512].rearrange("p (h s t) -> p h s t", h=2, s=2)
                  for i in range(2)]
            xg = [F[:, 7168 + i * 1024:8192 + i * 1024].rearrange("p (k s) -> p k s", k=8) for i in range(2)]
            th, sl, hh = (F[:, 9216 + i * 512:9728 + i * 512] for i in range(3))
            hT = [F[:, 10752 + i * 512:11264 + i * 512] for i in range(2)]
            Y = [F[:, 11776 + i * 512:12288 + i * 512] for i in range(2)]

            def v2(a, n=16):
                return sm[:, a:a + 2 * n].rearrange("p (h e) -> p h e", h=2)

            wr = col("wr").rearrange("p (k e) -> p k e", k=8)
            for k in range(8):
                t = PE.do([xt_ok[k // 2], c_ok, free[3]], lambda e: e.matmul(
                    PS[0:16, 3, 0:256], wr[:, k, :], XT[:, k, :], start=(k == 0), stop=(k == 7)))
            t = DV.do([t, br_ok], lambda e: e.tensor_scalar(
                lgT[:, :], PS[0:16, 3, 0:256], brt[:, 0:1], None, ALU.add))
            for h in range(2):
                t = PE.do([t, k_ident], lambda e: e.transpose(
                    PS[:, 3, h * 16:h * 16 + 16], lgT[:, h * 128:h * 128 + 128], ident[0:16, 0:16]))
            lg, pr, oh, tmp, m1, m2 = v2(0), v2(32), v2(64), v2(96), v2(128), v2(160)
            M, pos, gate, og = v2(192), v2(224), v2(256), v2(288)
            mx = sm[:, 320:322]
            gs = sm[:, 324:332].rearrange("p (h g) -> p h g", h=2)
            gp = sm[:, 332:340].rearrange("p (h g) -> p h g", h=2)
            p1, p2, den = sm[:, 340:342], sm[:, 342:344], sm[:, 344:346]
            pri = sm[:, 346:362]
            fl = sm[:, 378:379]

            def dv(toks, fn):
                return DV.do(toks, fn)

            def bc(ap, n=16):
                return ap.unsqueeze(2).to_broadcast([128, 2, n])

            tp = PL.do([k_iota], lambda e: e.tensor_scalar(pri, iota64[:, 0:16], -1.0, 17.0, ALU.mult, ALU.add))
            L = PS[:, 3, 0:32].rearrange("p (h e) -> p h e", h=2)
            t = dv([t], lambda e: e.tensor_reduce(mx, L, AX, ALU.max))
            free[3] = t = dv([t], lambda e: e.tensor_tensor(lg, L, bc(mx), ALU.subtract))
            tex = t = AC.do([t], lambda e: e.activation(pr, lg, ACT.Exp))
            x_tok = to_tokens(XT, xt_ok, X, x_free)
            pq = pr.rearrange("p h (g i j) -> p (h g i) j", g=4, i=2)
            hi, su = tmp[:, 0, :], tmp[:, 1, :]
            u = dv([t], lambda e: e.tensor_tensor(hi, pq[:, :, 0], pq[:, :, 1], ALU.max))
            v = dv([t], lambda e: e.tensor_tensor(su, pq[:, :, 0], pq[:, :, 1], ALU.add))
            h2 = hi.rearrange("p (n i) -> p n i", i=2)
            s2 = su.rearrange("p (n i) -> p n i", i=2)
            u = dv([u], lambda e: e.tensor_tensor(sm[:, 324:332], h2[:, :, 0], h2[:, :, 1], ALU.add))
            v = dv([v], lambda e: e.tensor_tensor(sm[:, 332:340], s2[:, :, 0], s2[:, :, 1], ALU.max))
            tg = dv([u, v], lambda e: e.tensor_tensor(sm[:, 324:332], sm[:, 324:332], sm[:, 332:340], ALU.max))

            def first_max(val, prio, best, onehot, n, toks):
                a = dv(toks, lambda e: e.tensor_reduce(best, val, AX, ALU.max))
                a = dv([a], lambda e: e.tensor_tensor(onehot, val, bc(best, n), ALU.is_ge))
                a = dv([a], lambda e: e.tensor_tensor(onehot, onehot, prio, ALU.mult))
                b = dv([a], lambda e: e.tensor_reduce(sm[:, 380:382], onehot, AX, ALU.max))
                return dv([b], lambda e: e.tensor_tensor(onehot, onehot, bc(sm[:, 380:382], n), ALU.is_equal))

            tg = first_max(gs, pri[:, 12:16].unsqueeze(1).to_broadcast([128, 2, 4]), mx, gp, 4, [tg, tp])
            gb = gp.unsqueeze(3).to_broadcast([128, 2, 4, 4])
            pm = oh
            b = dv([tg], lambda e: e.tensor_tensor(
                pm.rearrange("p h (g j) -> p h g j", g=4),
                pri.rearrange("p (g j) -> p g j", g=4).unsqueeze(1).to_broadcast([128, 2, 4, 4]), gb, ALU.mult))
            a = dv([tg], lambda e: e.tensor_tensor(
                tmp.rearrange("p h (g j) -> p h g j", g=4), pr.rearrange("p h (g j) -> p h g j", g=4), gb, ALU.mult))
            a = first_max(tmp, pm, p1, m1, 16, [a, b])
            a = dv([a], lambda e: e.scalar_tensor_tensor(out=tmp, in0=m1, scalar=-4.0, in1=tmp,
                                                         op0=ALU.mult, op1=ALU.add))
            am = first_max(tmp, pm, p2, m2, 16, [a])
            a = dv([am], lambda e: e.tensor_tensor(M, m1, m2, ALU.add))
            for h in range(2):
                if h == 1:
                    PE.go([k_ones], lambda e: e.matmul(PS[:, 4, 16:32], ones[:, 0:128], M[:, 0, :],
                                                       start=True, stop=False))
                t = PE.do([a, k_upper, free[4]], lambda e: e.matmul(
                    PS[:, 4, h * 16:h * 16 + 16], upper[:, :], M[:, h, :], start=(h == 0), stop=True))
            PE.go([k_ones, free[5]], lambda e: e.matmul(PS[:, 5, 0:16], ones[:, 0:128], M[:, 0, :], start=True, stop=False))
            tc = PE.do([], lambda e: e.matmul(PS[:, 5, 0:16], ones[:, 0:128], M[:, 1, :], start=False, stop=True))
            free[4] = p = dv([t], lambda e: e.scalar_tensor_tensor(
                out=pos, in0=PS[:, 4, 0:32].rearrange("p (h e) -> p h e", h=2), scalar=1.0, in1=M,
                op0=ALU.add, op1=ALU.mult))
            ts = []
            S4 = S.rearrange("p h (e s) -> p h e s", e=16)
            for e0, e1 in ((0, 2), (2, 16)):
                ts.append(dv([p, k_iota, x_free], lambda e: e.tensor_tensor(
                    S4[:, :, e0:e1, :],
                    iota64[:, :].unsqueeze(1).unsqueeze(1).to_broadcast([128, 2, e1 - e0, 64]),
                    pos[:, :, e0:e1].unsqueeze(3).to_broadcast([128, 2, e1 - e0, 64]), ALU.is_equal)))

            def gates():
                d = dv([tex], lambda e: e.tensor_reduce(den, pr, AX, ALU.add))
                d = dv([d], lambda e: e.reciprocal(den, den))
                a = dv([d, am], lambda e: e.tensor_tensor(p1, p1, den, ALU.mult))
                b = dv([d, am], lambda e: e.tensor_tensor(p2, p2, den, ALU.mult))
                b = dv([a, b], lambda e: e.tensor_tensor(den, p1, p2, ALU.add))
                b = dv([b], lambda e: e.reciprocal(den, den))
                b1 = dv([b], lambda e: e.tensor_tensor(p1, p1, den, ALU.mult))
                b2 = dv([b], lambda e: e.tensor_tensor(p2, p2, den, ALU.mult))
                b1 = dv([b1], lambda e: e.tensor_tensor(m1, m1, bc(p1), ALU.mult))
                b2 = dv([b2], lambda e: e.tensor_tensor(m2, m2, bc(p2), ALU.mult))
                tgate = dv([b1, b2], lambda e: e.tensor_tensor(gate, m1, m2, ALU.add))
                out = []
                for h in range(2):
                    for i in range(2):
                        for o in range(2):
                            v = (lambda ap, m: ap.rearrange("p (q m s) -> p q m s", q=8, m=2)[:, :, m, :])
                            ga = gate[:, h, :].rearrange("p (q m) -> p q m", m=2)[:, :, o]
                            out.append(dv([ts, tgate], lambda e: e.tensor_tensor(
                                v(Gs[i][:, h, :], o ^ i), v(S[:, h, :], o),
                                ga.unsqueeze(2).to_broadcast([128, 8, 64]), ALU.mult)))
                a = dv([tc], lambda e: e.tensor_reduce(fl, PS[:, 5, 0:16], AX, ALU.max))
                free[5] = a
                tfl = dv([a], lambda e: e.tensor_scalar(it[:, 0:1], fl, float(CAP), None, ALU.is_gt))
                b = dv([p], lambda e: e.tensor_scalar(og, pos, float(CAP), None, ALU.is_gt))
                return out, tfl, dv([b, tgate], lambda e: e.tensor_tensor(og, og, gate, ALU.mult))

            xg_tok, xg_free = [None, None], [None, None]
            gt_tok, gt_free = [None, None], [None, None]
            y_free = [None]

            def gather(q, halves=(0, 1)):
                i = q % 2
                if 0 in halves:
                    xg_tok[i] = []
                for half in halves:
                    b = 6 + half
                    for k4 in range(4):
                        k = 4 * half + k4
                        for h in range(2):
                            t = PE.do([ts[min(q, 1)], x_tok, free[b] if k4 == 0 else None], lambda e: e.matmul(
                                PS[:, b, k4 * 128:k4 * 128 + 128], X[:, h, k * 128:k * 128 + 128],
                                S[:, h, q * 128:q * 128 + 128], start=(h == 0), stop=(h == 1)))
                    src = PS[:, b, :].rearrange("p (k s) -> p k s", k=4)
                    dst = xg[i][:, 4 * half:4 * half + 4, :]
                    if half:
                        free[b] = DV.do([t, xg_free[i]], lambda e: e.tensor_copy(dst, src))
                    else:
                        free[b] = AC.do([t, xg_free[i]], lambda e: e.activation(dst, src, ACT.Copy))
                    xg_tok[i].append(free[b])

            def turn_gates(q):
                i = q % 2
                for h in range(2):
                    for s in range(2):
                        a = (2 * h + s) * 128
                        t = PE.do([gs_tok, free[6]], lambda e: e.transpose(
                            PS[:, 6, a:a + 128], Gs[s][:, h, q * 128:q * 128 + 128], ident[:, :]))
                src = PS[:, 6, :].rearrange("p (h s t) -> p h s t", h=2, s=2)
                free[6] = AC.do([t, gt_free[i]], lambda e: e.activation(Gt[i], src, ACT.Copy))
                gt_tok[i] = free[6]

            def product(name, bank, lhs, lhs_tok, swap, halfway=None):
                for c in range(4):
                    if c == 2 and halfway:
                        halfway()
                    w, w_ok = W.take(name)
                    for kk in range(2):
                        k = 2 * c + kk
                        for half in range(2):
                            a = kk * 1024 + (half ^ swap) * 512
                            f = (lambda e: e.matmul(PS[64 * half:64 * half + 64, bank, :], lhs(k), w[:, a:a + 512],
                                                    start=(k == 0), stop=(k == 7)))
                            wt = [w_ok, lhs_tok[c // 2], free[bank] if c == 0 else None] if (kk, half) == (0, 0) else []
                            if (kk, half) == (1, 1):
                                t = PE.do(wt, f)
                            else:
                                PE.go(wt, f)
                    W.give(t)
                return t

            z_tok = [None] * 4

            def combine(q, y_tok):
                i = q % 2
                for h in range(2):
                    for d in range(2):
                        b = 2 * h + d
                        t = PE.do([y_tok, gt_tok[i], free[b] if q == 0 else None], lambda e: e.matmul(
                            PS[:, b, :], Gt[i][:, h, d, :], Y[d], start=(q == 0), stop=(q == 7)))
                        z_tok[b] = t
                y_free[0] = t
                gt_free[i] = t

            gather(0, (0,))
            gs_tok = None
            y_tok = []
            h_free = [None, None]
            hh_free = None
            for ex in range(E):
                q, o, i = ex // 2, ex % 2, ex % 2
                xx, xk = xg[q % 2], xg_tok[q % 2]
                lhs = (lambda k: xx[:, k, o * 64:o * 64 + 64])
                t1 = product(f"w1{layer}", 4, lhs, xk, 0, (lambda: gather(0, (1,))) if ex == 0 else None)
                if ex == 0:
                    gs_tok, tfl, _ = gates()
                a = AC.do([t1], lambda e: e.activation(th, PS[:, 4, :], ACT.Tanh, scale=0.5))
                s = DV.do([a], lambda e: e.scalar_tensor_tensor(
                    out=sl, in0=th, scalar=1.0, in1=PS[:, 4, :], op0=ALU.add, op1=ALU.mult))
                free[4] = s
                t3 = product(f"w3{layer}", 5, lhs, xk, 0)
                if o == 1:
                    xg_free[q % 2] = t3
                hd = DV.do([t3, s, hh_free], lambda e: e.scalar_tensor_tensor(
                    out=hh, in0=sl, scalar=0.5, in1=PS[:, 5, :], op0=ALU.mult, op1=ALU.mult))
                free[5] = hd
                if ex == 3 and layer == 0:
                    odd_constants()
                if ex == 15 and layer == 1:
                    load_rows([xg_tok, gs_tok])
                if ex == 9:
                    for en in (AC, DV, PL, SP, PE):
                        en.wait([tfl])
                    flag = nc.values_load(it[0:1, 0:1], min_val=0, max_val=1)
                if o == 0 and q > 0:
                    combine(q - 1, y_tok)
                if o == 0:
                    turn_gates(q)
                    y_tok = []
                if o == 1 and q < 7:
                    gather(q + 1)
                for j in range(4):
                    t = PE.do([hd, free[6] if j == 0 else None], lambda e: e.transpose(
                        PS[:, 6, j * 128:j * 128 + 128], hh[:, j * 128:j * 128 + 128], ident[:, :]))
                hh_free = t
                free[6] = AC.do([t, h_free[i]], lambda e: e.activation(hT[i], PS[:, 6, :], ACT.Copy))
                ty = product(f"w2{layer}", 7, (lambda k: hT[i][:, (k % 4) * 128 + (k // 4) * 64:
                                                              (k % 4) * 128 + (k // 4) * 64 + 64]), [free[6]] * 2, o)
                h_free[i] = ty
                e0 = AC.do([ty, y_free[0]], lambda e: e.activation(Y[o][0:64, :], PS[0:64, 7, :], ACT.Copy))
                e1 = DV.do([ty, y_free[0]], lambda e: e.tensor_copy(Y[1 - o][64:128, :], PS[64:128, 7, :]))
                free[7] = [e0, e1]
                y_tok += [e0, e1]
            combine(7, y_tok)
            zt = []
            ev = add_residual(X, x_tok, ALPHA, Z, None)
            for h in range(2):
                for d in range(2):
                    free[2 * h + d] = ev(h, d, PS[:, 2 * h + d, :], z_tok[2 * h + d])
                    zt.append(free[2 * h + d])

            with nc.If(flag > 0):
                for en in (AC, DV, PL, SP, PE):
                    for other in (AC, DV, PL, PE):
                        en.e.wait_ge(other.sem, other.n)
                nc.all_engine_barrier()
                with nc.Fori(0, E) as e_i:
                    overflow(layer, og, e_i)
                    nc.all_engine_barrier(sems_to_clear=over_range)
                    nc.all_engine_barrier()
            return zt

        over = [sem(f"s_o{i}") for i in range(5)]
        nums = sorted(s.num for s in over)
        assert nums == list(range(nums[0], nums[0] + 5))
        over_range = range(nums[0], nums[0] + 5)

        def overflow(layer, og, e_i):
            oPE, oAC, oDV, oPL = (Eng(x.e, s) for x, s in zip((PE, AC, DV, PL), over))
            s_w = over[4]
            hid = F[:, 0:2048].rearrange("p (k t) -> p k t", k=8)
            wb = F[:, 2048:4096]
            th = F[:, 4096:4608]
            H = F[:, 4608:6656].rearrange("p (h n) -> p h n", h=2)
            oge = sm[:, 382:384]
            tg = oDV.do([], lambda e: e.tensor_copy(oge, og[:, :, bass.ds(e_i, 1)]))
            n, w_free = 0, None
            sp = Eng(SP.e, s_w)

            def dense(w, bank, lhs, lhs_tok, bank_tok):
                nonlocal n, w_free
                for c in range(4):
                    sp.wait([w_free])
                    sp.e.dma_start(wb, A[w][layer, bass.ds(e_i, 1), c].rearrange("a p n -> (a p) n"))\
                        .then_inc(s_w, 16)
                    n += 1
                    for kk in range(2):
                        k = 2 * c + kk
                        for h in range(2):
                            for d in range(2):
                                t = oPE.do([(s_w, 16 * n), lhs_tok, bank_tok if k == 0 else None],
                                           lambda e: e.matmul(
                                    PS[:, bank + 2 * h + d, :], lhs[:, k, h * 128:h * 128 + 128],
                                    wb[:, kk * 1024 + d * 512:kk * 1024 + d * 512 + 512],
                                    start=(k == 0), stop=(k == 7)))
                    w_free = t
                return t

            t1 = dense("w1", 0, XT, None, None)
            t3 = dense("w3", 4, XT, None, None)
            hd = None
            for h in range(2):
                for d in range(2):
                    b, dst = 2 * h + d, H[:, h, d * 512:d * 512 + 512]
                    a = oAC.do([t1, hd], lambda e: e.activation(th, PS[:, b, :], ACT.Tanh, scale=0.5))
                    s = oDV.do([a], lambda e: e.scalar_tensor_tensor(
                        out=dst, in0=th, scalar=1.0, in1=PS[:, b, :], op0=ALU.add, op1=ALU.mult))
                    hd = oDV.do([t3, s], lambda e: e.scalar_tensor_tensor(
                        out=dst, in0=dst, scalar=0.5, in1=PS[:, 4 + b, :], op0=ALU.mult, op1=ALU.mult))
            got = []
            for q in range(4):
                for j in range(2):
                    k = 2 * q + j
                    for h in range(2):
                        t = oPE.do([hd], lambda e: e.transpose(
                            PS[:, q, j * 256 + h * 128:j * 256 + h * 128 + 128],
                            H[:, h, k * 128:k * 128 + 128], ident[:, :]))
                got.append(oAC.do([t], lambda e: e.activation(
                    hid[:, 2 * q:2 * q + 2, :], PS[:, q, :].rearrange("p (k t) -> p k t", k=2), ACT.Copy)))
            t = dense("w2", 4, hid, got, hd)
            for h in range(2):
                for d in range(2):
                    z = Z[:, h, d * 512:d * 512 + 512]
                    oDV.do([t, tg], lambda e: e.scalar_tensor_tensor(
                        out=z, in0=PS[:, 4 + 2 * h + d, :], scalar=oge[:, h:h + 1], in1=z,
                        op0=ALU.mult, op1=ALU.add))

        def attention_a(xt_ok, x_free):
            qT = fv(2048, 8)
            kT = fv(4096, 8)
            v = F[:, 6144:8192].rearrange("p (h d) -> p h d", h=2)
            p_sb = [F[:, 8192 + i * 384:8576 + i * 384] for i in range(4)]
            dg = F[:, 12800:13312].rearrange("p (i b q) -> p i b q", i=2, b=2)
            pt = [F[:, 9728 + i * 384:10112 + i * 384] for i in range(2)]
            zf, ab, c, lf = (F[0:16, 10496 + i * 256:10752 + i * 256] for i in range(4))
            pads = [F[:, 11776 + i * 256:12032 + i * 256] for i in range(4)]
            n0 = PL.do([], lambda e: e.memset(f32(nch), 0.0))
            n0 = PL.do([], lambda e: e.memset(f32(ncl), 0.0))
            pad0 = [PL.do([xt_ok], lambda e: e.memset(F[:, 11776:12800], 0.0))] * 4
            cq = sm[:, 0:32].rearrange("p (b h) -> p b h", b=2)
            wf = col("wf")
            a = AC.do([c_ok], lambda e: e.activation(wfh[:, :], wf, ACT.Copy))
            wf_ok = DV.do([a], lambda e: e.tensor_tensor(wfl[:, :], wf, f32(wfh[:, :]), ALU.subtract))
            for k in range(8):
                t = mm3(PS[0:16, 7, 0:256], (wfh[:, k * 16:k * 16 + 16], wfl[:, k * 16:k * 16 + 16]),
                        (xh[:, k, :], xl[:, k, :]), [xt_ok[k // 2], wf_ok, free[7]], k == 0, k == 7, True)
            a = DV.do([t, bf_ok], lambda e: e.tensor_scalar(zf, PS[0:16, 7, 0:256], bft[:, 0:1], None, ALU.add))
            free[7] = a
            b = AC.do([a], lambda e: e.activation(ab, zf, ACT.Abs))
            b = AC.do([b], lambda e: e.activation(ab, ab, ACT.Exp, scale=-1.0))
            b = DV.do([b], lambda e: e.tensor_scalar(ab, ab, 1.0, None, ALU.add))
            b = AC.do([b], lambda e: e.activation(ab, ab, ACT.Ln))
            b = DV.do([b], lambda e: e.scalar_tensor_tensor(out=lf, in0=zf, scalar=0.0, in1=ab,
                                                            op0=ALU.min, op1=ALU.subtract))
            tc_ = DV.do([b, k_ones], lambda e: e.tensor_tensor_scan(c, ones[0:16, :], lf, 0.0, ALU.mult, ALU.add))
            nc3 = nch[0:16, :]
            n1 = DV.do([tc_, n0], lambda e: e.tensor_scalar(nc3[:, 0:128], c[:, 0:128], -1.0, None, ALU.mult))
            n2 = DV.do([tc_, n0], lambda e: e.tensor_scalar(nc3[:, 128:384], c, -1.0, None, ALU.mult))
            n3 = DV.do([n1, n2], lambda e: e.scalar_tensor_tensor(
                out=ncl[0:16, 128:384], in0=c, scalar=-1.0, in1=f32(nc3[:, 128:384]), op0=ALU.mult, op1=ALU.subtract))
            tn = DV.do([n3], lambda e: e.tensor_copy(ncl[0:16, 0:128], f32(ncl[0:16, 128:256])))
            for h in range(2):
                t = PE.do([tc_, free[7]], lambda e: e.transpose(
                    PS[:, 7, h * 16:h * 16 + 16], c[:, h * 128:h * 128 + 128], ident[0:16, 0:16]))
            tq = DV.do([t], lambda e: e.tensor_copy(cq, PS[:, 7, 0:32].rearrange("p (b h) -> p b h", b=2)))
            free[7] = tq
            tok = {}

            def evac(c_, b, ps, t):
                if c_ < 4:
                    tok["q", c_] = DV.do([t], lambda e: e.tensor_scalar(
                        qT[:, 2 * c_:2 * c_ + 2, :], ps, 0.125, None, ALU.mult))
                    free[b] = tok["q", c_]
                    return
                i = c_ - 4
                tok["k", i] = AC.do([t], lambda e: e.activation(kT[:, 2 * i:2 * i + 2, :], ps, ACT.Copy))
                free[b] = tok["k", i]

            proj_features("aq_in", 8, xt_ok, evac, [0, 1, 2, 3, 4, 5])

            def evac_v(c_, m, ps, t):
                dst = v[:, m, c_ * 512:c_ * 512 + 512]
                if m:
                    tok["v", c_, m] = AC.do([t], lambda e: e.activation(dst, ps, ACT.Copy))
                else:
                    tok["v", c_, m] = DV.do([t], lambda e: e.tensor_copy(dst, ps))
                return tok["v", c_, m]

            proj_cols("av_in", 2, xt_ok, evac_v, [0, 1, 2, 3])
            st = {}
            gt = [None] * 8

            def pad(h):
                r = slice(64 * (h % 2), 64 * (h % 2) + 64)
                st["pad", h] = PL.do([tok["q", h // 4], pad0, st.get(("s", h - 4))], lambda e: e.tensor_copy(
                    pads[h % 4][r, :], qT[r, h // 2, :]))

            def scores(h):
                i = h % 2
                b = i
                w = [st["pad", h], tok["k", h // 4], free[b]]
                q = pads[h % 4]
                sel = identr[:, h:h + 1].to_broadcast([128, 128])
                PE.go([w, tn, k_identr], lambda e: e.matmul(PS[:, b, 0:384], sel, nch, start=True, stop=False))
                PE.go([], lambda e: e.matmul(PS[:, b, 0:384], sel, ncl, start=False, stop=False))
                PE.go([], lambda e: e.matmul(PS[:, b, 0:128], q[:, 0:128], kT[:, h // 2, 0:128],
                                             start=False, stop=False))
                t = PE.do([], lambda e: e.matmul(PS[:, b, 128:384], q[:, 128:256], kT[:, h // 2, :],
                                                 start=False, stop=True))
                st["s", h] = t
                s = p_sb[h % 4]
                sc = sm[:, 64 + 16 * (h % 4):80 + 16 * (h % 4)]
                a0 = DV.do([t, tq, k_cmask, st.get(("t", h - 4))], lambda e: e.scalar_tensor_tensor(
                    out=s[:, 0:128], in0=PS[:, b, 0:128], scalar=cq[:, 0, h:h + 1], in1=cmask[:, 128:256],
                    op0=ALU.add, op1=ALU.add))
                a1 = DV.do([], lambda e: e.scalar_tensor_tensor(
                    out=s[:, 128:384], in0=PS[:, b, 128:384], scalar=cq[:, 1, h:h + 1], in1=cmask[:, :],
                    op0=ALU.add, op1=ALU.add))
                free[b] = a1
                m0 = DV.do([a0], lambda e: e.tensor_reduce(sc[:, 0:1], s[:, 0:128], AX, ALU.max))
                m1 = DV.do([a1], lambda e: e.tensor_reduce(sc[:, 1:2], s[:, 128:384], AX, ALU.max))
                ng = DV.do([m0, m1], lambda e: e.tensor_scalar(sc[:, 2:4], sc[:, 0:2], -1.0, None, ALU.mult))
                st["ng", h] = ng

            def exps(h):
                s = p_sb[h % 4]
                sc = sm[:, 64 + 16 * (h % 4):80 + 16 * (h % 4)]
                AC.go([st["ng", h]], lambda e: e.activation(
                    s[:, 0:128], s[:, 0:128], ACT.Exp, bias=sc[:, 2:3], accum_out=sc[:, 4:5]))
                st["e", h] = AC.do([], lambda e: e.activation(
                    s[:, 128:384], s[:, 128:384], ACT.Exp, bias=sc[:, 3:4], accum_out=sc[:, 5:6]))

            def invert(h):
                sc = sm[:, 64 + 16 * (h % 4):80 + 16 * (h % 4)]
                rc = DV.do([st["e", h]], lambda e: e.reciprocal(sc[:, 6:8], sc[:, 4:6]))
                for b in range(2):
                    d = DV.do([rc, st.get(("t", h - 2))], lambda e: e.tensor_scalar(
                        dg[:, h % 2, b, :], ident[:, :], sc[:, 6 + b:7 + b], None, ALU.mult))
                st["d", h] = d

            def turn(h):
                i, b = h % 2, 2 + h % 2
                for n in range(3):
                    t = PE.do([st["d", h], free[b] if n == 0 else None], lambda e: e.matmul(
                        PS[:, b, n * 128:n * 128 + 128], p_sb[h % 4][:, n * 128:n * 128 + 128],
                        dg[:, i, 1 if n else 0, :], start=True, stop=True))
                st["t", h] = t
                free[b] = AC.do([t, st.get(("o", h - 2))], lambda e: e.activation(pt[i], PS[:, b, 0:384], ACT.Copy))
                st["pt", h] = free[b]

            def values(h):
                i, b = h % 2, 4 + (h // 2) % 2
                r = slice(64 * i, 64 * i + 64)
                PE.go([st["pt", h], [tok["v", n, m] for n in range(2) for m in range(2)], free[b] if i == 0 else None],
                      lambda e: e.matmul(PS[r, b, 0:256], v[:, 0, h * 64:h * 64 + 64], pt[i][:, 0:256],
                                         start=True, stop=False))
                t = PE.do([], lambda e: e.matmul(PS[r, b, 128:256], v[:, 1, h * 64:h * 64 + 64],
                                                 pt[i][:, 256:384], start=False, stop=True))
                st["o", h] = t
                if i:
                    free[b] = AC.do([t, x_free], lambda e: e.activation(GT[:, h // 2, :], PS[:, b, 0:256], ACT.Copy))
                    gt[h // 2] = free[b]

            pad(0)
            pad(1)
            for i in range(20):
                if 2 <= i <= 17:
                    invert(i - 2)
                if i < 16:
                    scores(i)
                if i < 14:
                    pad(i + 2)
                if 3 <= i <= 18:
                    turn(i - 3)
                if i < 16:
                    exps(i)
                if i >= 4:
                    values(i - 4)
            return gt

        def ffn(layer, xt_ok, gt_free, half_done):
            G = fv(0, 22)
            acc = [[F[:, 5632 + (2 * i + s) * 512:6144 + (2 * i + s) * 512].rearrange("p (k t) -> p k t", k=2)
                    for s in range(2)] for i in range(2)]
            th = [F[:, 7680 + i * 512:8192 + i * 512].rearrange("p (k t) -> p k t", k=2) for i in range(2)]
            cw = col(f"fcw{layer}").rearrange("p (c k) -> p c k", c=44)
            cb = col(f"fcb{layer}")
            gt = [None] * 22
            done = {}
            st = {}

            def evac(n, bank, ps, t):
                pair, side = n // 2, n % 2
                i = pair % 2
                dst = acc[i][side]
                first = (22 if side == 0 else 0) + 2 * pair
                for j in range(2):
                    ch = first + j
                    a = AC.do([t, c_ok, st.get(pair - 2), gt_free], lambda e: e.activation(
                        dst[:, j, :], ps[:, j, :], ACT.Identity, scale=cw[:, ch, 2:3], bias=cb[:, ch:ch + 1]))

                def taps():
                    b = [a, a]
                    for n in (1, 2):
                        for j in range(2):
                            ch = first + j
                            b[j] = DV.do([b[j]], lambda e: e.scalar_tensor_tensor(
                                out=dst[:, j, n:256], in0=ps[:, j, 0:256 - n], scalar=cw[:, ch, 2 - n:3 - n],
                                in1=dst[:, j, n:256], op0=ALU.mult, op1=ALU.add))
                    free[bank] = done[pair, side] = b

                def silu():
                    b = AC.do([done[pair, 0]], lambda e: e.activation(th[i], dst, ACT.Tanh, scale=0.5))
                    b = PL.do([b], lambda e: e.tensor_scalar(th[i], th[i], 0.5, 0.5, ALU.mult, ALU.add))
                    done[pair] = PL.do([b], lambda e: e.tensor_tensor(dst, dst, th[i], ALU.mult))

                def join():
                    g = DV.do([done[pair, 1], done[pair], gt_free], lambda e: e.tensor_tensor(
                        G[:, 2 * pair:2 * pair + 2, :], acc[i][0], dst, ALU.mult))
                    gt[2 * pair] = gt[2 * pair + 1] = g
                    st[pair] = g

                defer(1, taps)
                defer(3, join if side else silu)

            proj_features(f"up{layer}", 22, xt_ok, evac, [4, 5, 6, 7], flush=False)
            out = proj_out_steps(f"down{layer}", 22, G, gt, add_residual(X, None, 1.0, X, None), half_done, True)
            next(out)
            run_deferred(True)
            for _ in out:
                pass

        def attention_b(x_tok, rms_ok):
            kT = fv(2048, 12)
            v = F[:, 5120:8192].rearrange("p (h d) -> p h d", h=2)
            qT = fv(8192, 12)
            pads = [F[:, 1024 + i * 256:1280 + i * 256] for i in range(4)]
            pad0 = PL.do([x_tok], lambda e: e.memset(F[:, 1024:2048], 0.0))
            XF = XT[:, :, :].rearrange("p k t -> p (k t)")
            S3 = [a.rearrange("p (g n) -> p g n", g=3) for a in (
                F[:, 11264:12416], F[:, 12416:13568], XF[:, 0:1152])]
            dg = XF[:, 1152:1664].rearrange("p (i b q) -> p i b q", i=2, b=2)
            xt_ok, raw_ok = [], []

            def evac2(q, ps, t):
                xt_ok.append(split_xg(q, ps, col("kvg"), t))
                return xt_ok[q]

            rms_features(rms_ok, evac2)
            for q in range(4):
                free[4 + q] = AC.do([xt_ok[q], x_tok], lambda e: e.activation(
                    XT[:, 2 * q:2 * q + 2, :], PS[:, 4 + q, :].rearrange("p (k t) -> p k t", k=2), ACT.Copy))
                raw_ok.append(free[4 + q])
            ZF = Z[:, :, :].rearrange("p h d -> p (h d)")
            dist = ZF[:, 0:1152].rearrange("p (g n) -> p g n", g=3)
            pt = [ZF[:, 1152 + i * 384:1536 + i * 384] for i in range(2)]
            di, dx = F[:, 11264:11520].bitcast(I32), F[:, 11520:11776].bitcast(I32)
            t = PL.do([xt_ok], lambda e: e.iota(di, pattern=[[-1, 256]], base=128, channel_multiplier=1))
            def build_dist():
                t0 = DV.do([t], lambda e: e.tensor_copy(dist[:, 0, 128:384], di))
                dd = [t0]
                for g, mask in ((1, 3), (2, 15)):
                    a = DV.do([t, dd], lambda e: e.tensor_scalar(dx, di, mask, None, ALU.bitwise_and))
                    a = DV.do([a], lambda e: e.tensor_scalar(dist[:, g, 128:384], dx, 0.0, -NEG, ALU.is_gt, ALU.mult))
                    dd.append(DV.do([a, t0], lambda e: e.tensor_tensor(
                        dist[:, g, 128:384], dist[:, g, 128:384], dist[:, 0, 128:384], ALU.add)))
                d0 = PL.do([dd], lambda e: e.affine_select(
                    out=dist[:, 0, 128:384], in_=dist[:, 0, 128:384], compare_op=ALU.is_ge, fill=-NEG, base=0,
                    pattern=[[1, 256]], channel_multiplier=-1))
                dl = []
                for g in range(3):
                    dl.append(PL.do([d0, dd], lambda e: e.affine_select(
                        out=dist[:, g, 128:384], in_=dist[:, g, 128:384], compare_op=ALU.is_ge, fill=-NEG,
                        base=128, pattern=[[-1, 256]], channel_multiplier=1)))
                dist_ok = DV.do([dl], lambda e: e.tensor_copy(dist[:, :, 0:128], dist[:, :, 256:384]))
                return dist_ok

            tok = {}

            def evac_k(c, b, ps, t):
                if c % 2:
                    tok["k", c] = DV.do([t], lambda e: e.tensor_copy(kT[:, 2 * c:2 * c + 2, :], ps))
                else:
                    tok["k", c] = AC.do([t], lambda e: e.activation(kT[:, 2 * c:2 * c + 2, :], ps, ACT.Copy))
                free[b] = tok["k", c]

            def evac_v(c, m, ps, t):
                dst = v[:, m, c * 512:c * 512 + 512]
                if m:
                    tok["v", c, m] = DV.do([t], lambda e: e.tensor_copy(dst, ps))
                else:
                    tok["v", c, m] = AC.do([t], lambda e: e.activation(dst, ps, ACT.Copy))
                return tok["v", c, m]

            def evac_q(c, b, ps, t):
                tok["q", c] = DV.do([t], lambda e: e.tensor_scalar(
                    qT[:, 2 * c:2 * c + 2, :], ps, 0.125, None, ALU.mult))
                free[b] = tok["q", c]

            proj_features("wk", 6, xt_ok, evac_k, [0, 1, 2, 3])
            dist_ok = build_dist()
            proj_cols("wv", 3, xt_ok, evac_v, [4, 5, 6, 7])
            q_ok = [split_xg(q, XT[:, 2 * q:2 * q + 2, :], col("mixg1"), raw_ok[q]) for q in range(4)]
            proj_features("bwq", 6, q_ok, evac_q, [0, 1, 2, 3])
            st = {}
            gt = [None] * 4

            def pad(n):
                h, g, m = n // 3, n % 3, st.get("pads", 0)
                r, tile = slice(64 * (h % 2), 64 * (h % 2) + 64), 4 * g + h // 2
                i = 2 * (h % 2) + n % 2
                st["pad", n] = PL.do([tok["q", tile // 2], pad0, st.get(("last", i))], lambda e: e.tensor_copy(
                    pads[i][r, :], qT[r, tile, :]))

            def scores(n):
                h, g, b = n // 3, n % 3, n % 4
                i = 2 * (h % 2) + n % 2
                tile, q = 4 * g + h // 2, pads[i]
                s, slope = S3[h % 3][:, g, :], 2.0 ** (-8.0 * (8 * g + h + 1) / 24)
                w = [st["pad", n], tok["k", tile // 2], free[b]]
                PE.go(w, lambda e: e.matmul(PS[:, b, 0:128], q[:, 0:128], kT[:, tile, 0:128],
                                            start=True, stop=True))
                t = PE.do([], lambda e: e.matmul(PS[:, b, 128:384], q[:, 128:256], kT[:, tile, :],
                                                 start=True, stop=True))
                st["last", i] = t
                free[b] = DV.do([t, dist_ok, st.get(("t", n - 9)), q_ok], lambda e: e.scalar_tensor_tensor(
                    out=s, in0=dist[:, g, :], scalar=-slope, in1=PS[:, b, 0:384], op0=ALU.mult, op1=ALU.add))
                st["a", n] = free[b]

            def soften(h):
                s = S3[h % 3]
                sc = sm[:, 256 + 8 * (h % 3):264 + 8 * (h % 3)]
                a = [st["a", 3 * h + g] for g in range(3)]
                m0 = DV.do([a, st.get(("d", h - 3))], lambda e: e.tensor_reduce(
                    sc[:, 0:1], s[:, :, 0:128], mybir.AxisListType.XY, ALU.max))
                m1 = DV.do([], lambda e: e.tensor_reduce(
                    sc[:, 1:2], s[:, :, 128:384], mybir.AxisListType.XY, ALU.max))
                ng = DV.do([m0, m1], lambda e: e.tensor_scalar(sc[:, 2:4], sc[:, 0:2], -1.0, None, ALU.mult))
                st["ng", h] = ng

            def exps(h):
                s = S3[h % 3]
                sc = sm[:, 256 + 8 * (h % 3):264 + 8 * (h % 3)]
                AC.go([st["ng", h]], lambda e: e.activation(
                    s[:, :, 0:128], s[:, :, 0:128], ACT.Exp, bias=sc[:, 2:3], accum_out=sc[:, 4:5]))
                st["e", h] = AC.do([], lambda e: e.activation(
                    s[:, :, 128:384], s[:, :, 128:384], ACT.Exp, bias=sc[:, 3:4], accum_out=sc[:, 5:6]))

            def invert(h):
                sc = sm[:, 256 + 8 * (h % 3):264 + 8 * (h % 3)]
                rc = DV.do([st["e", h]], lambda e: e.reciprocal(sc[:, 6:8], sc[:, 4:6]))
                for b in range(2):
                    d = DV.do([rc, st.get(("t", 3 * (h - 2) + 2))], lambda e: e.tensor_scalar(
                        dg[:, h % 2, b, :], ident[:, :], sc[:, 6 + b:7 + b], None, ALU.mult))
                st["d", h] = d

            def turn(n):
                i, b, h = n % 2, 4 + n % 2, n // 3
                s = S3[h % 3][:, n % 3, :]
                for m in range(3):
                    t = PE.do([st["d", h], free[b] if m == 0 else None], lambda e: e.matmul(
                        PS[:, b, m * 128:m * 128 + 128], s[:, m * 128:m * 128 + 128],
                        dg[:, h % 2, 1 if m else 0, :], start=True, stop=True))
                st["t", n] = t
                free[b] = AC.do([t, st.get(("o", n - 2)), q_ok], lambda e: e.activation(
                    pt[i], PS[:, b, 0:384], ACT.Copy))
                st["pt", n] = free[b]

            def values(n):
                h, g, i = n // 3, n % 3, n % 2
                b = 6 + (h // 2) % 2
                r = slice(64 * (h % 2), 64 * (h % 2) + 64)
                c0 = g * 512 + h * 64
                vt = [tok["v", c, m] for c in range(3) for m in range(2)]
                PE.go([st["pt", n], vt, free[b] if (h % 2, g) == (0, 0) else None],
                      lambda e: e.matmul(PS[r, b, 0:256], v[:, 0, c0:c0 + 64], pt[i][:, 0:256],
                                         start=(g == 0), stop=False))
                t = PE.do([], lambda e: e.matmul(PS[r, b, 128:256], v[:, 1, c0:c0 + 64],
                                                 pt[i][:, 256:384], start=False, stop=(g == 2)))
                st["o", n] = t
                if (h % 2, g) == (1, 2):
                    free[b] = DV.do([t], lambda e: e.tensor_copy(GT[:, h // 2, :], PS[:, b, 0:256]))
                    gt[h // 2] = free[b]

            pad(0)
            pad(1)
            for i in range(24 + LAG + 1):
                if i >= 4 and (i - INV) % 3 == 0 and 0 <= (i - INV) // 3 < 8:
                    invert((i - INV) // 3)
                if i < 24:
                    scores(i)
                if i < 22:
                    pad(i + 2)
                if i < 24:
                    if i % 3 == 2:
                        soften(i // 3)
                if LAG <= i < 24 + LAG:
                    turn(i - LAG)
                if i < 24 and i % 3 == 2:
                    exps(i // 3)
                if i > LAG:
                    values(i - LAG - 1)
            return gt

        def banks():
            return [free[b] for b in range(4)]

        def halves(fn):
            done = []

            def half_done(h, toks):
                done.append(fn(h, toks))
            return done, half_done

        def second_block(x_tok):
            ahead()
            rms_ok = [rms_half(h, x_tok[h]) for h in range(2)]
            xt_ok = rms_features(rms_ok, split_xt("mixg0"))
            gt = attention_a(xt_ok, None)
            for layer in range(2):
                rms_ok, half_done = halves(rms_half)
                if layer == 0:
                    proj_out("aw_out", 8, GT, gt, add_residual(X, x_tok, 1.0, X, None), half_done)
                else:
                    proj_out("bw_out", 4, GT, gt, add_residual(X, x_tok, 1.0, X, None), half_done)
                x_tok = banks()
                if dbg == f"att{layer}":
                    return [x_tok, rms_ok]
                xt_ok = rms_features(rms_ok, split_xt(f"ffng{layer}"))
                if layer == 0:
                    rms_ok, half_done = halves(rms_half)
                    ffn(layer, xt_ok, xt_ok, half_done)
                    x_tok = banks()
                    if dbg == f"ffn{layer}":
                        return [x_tok, rms_ok]
                    gt = attention_b(x_tok, rms_ok)

            gr = F[:, 12288:13312]
            AC.wait([gt, xt_ok])
            AC.e.dma_start(gr, A["rows"][2, :].partition_broadcast(128)).then_inc(s_row, 16)
            row_loads.append("final")
            g_ok = (s_row, 16 * len(row_loads))

            def finish(h, toks):
                s = AC.do([toks], lambda e: e.activation(
                    Z[:, h, :], X[:, h, :], ACT.Square, scale=1.0 / 32, accum_out=sm[:, 430 + h:431 + h]))
                r = rstd(sm[:, 430 + h:431 + h], RMS_EPS, h, [s])
                r = DV.do([r, s, g_ok], lambda e: e.scalar_tensor_tensor(
                    out=Z[:, h, :], in0=X[:, h, :], scalar=sm[:, 500 + h:501 + h], in1=gr,
                    op0=ALU.mult, op1=ALU.mult))
                SP.wait([r])
                SP.e.dma_start(out[h * 128:h * 128 + 128, :], Z[:, h, :]).then_inc(s_out, 16)

            ffn(1, xt_ok, xt_ok, finish)

        def first_block():
            done, half_done = halves(norm_half)
            even_mixer(half_done)
            zt = banks()
            for layer in range(2):
                xt_ok = normed(2 * layer, done)
                if dbg == f"x1_{layer}":
                    return to_tokens(XT, xt_ok, X, zt)
                zt = moe(layer, xt_ok, zt)
                if layer == 0:
                    ahead()
                    xt_ok = normed(1, [norm_half(h, zt) for h in range(2)])
                    if dbg == f"x2_{layer}":
                        return to_tokens(XT, xt_ok, X, zt)
                    sp = [split_x(q, XT[:, 2 * q:2 * q + 2, :], xt_ok[q]) for q in range(4)]
                    done, half_done = halves(norm_half)
                    odd_mixer(sp, lambda: to_tokens(XT, xt_ok, X, zt), half_done)
                    zt = banks()
            done = []
            for h in range(2):
                mean, r, ok = moments(Z, zt, h)
                a = DV.do([ok, zt, rows_ok], lambda e: e.scalar_tensor_tensor(
                    out=X[:, h, :], in0=Z[:, h, :], scalar=mean, in1=rows2[:, 0, :], op0=ALU.subtract, op1=ALU.mult))
                done.append(DV.do([a], lambda e: e.scalar_tensor_tensor(
                    out=X[:, h, :], in0=X[:, h, :], scalar=r, in1=rows2[:, 1, :], op0=ALU.mult, op1=ALU.add)))
            return done

        if dbg and dbg.startswith(("att", "ffn", "all")):
            W.used = 0
            fin = second_block([x_ok] * 2)
        else:
            fin = first_block()
            if not dbg:
                fin = second_block(fin)
        if dbg and fin is not None:
            SP.wait([fin])
            SP.e.wait_ge(s_br, 16)
            SP.e.wait_ge(s_bf, 16)
            if row_loads:
                SP.e.wait_ge(s_row, 16 * len(row_loads))
            for n in range(RING):
                SP.e.wait_ge(ring_sems[n], 16 * ((min(W.used + RING, len(plan)) + RING - 1 - n) // RING))
            SP.e.dma_start(out.rearrange("(h p) d -> p h d", p=128), X[:, :, :]).then_inc(s_out, 16)
            SP.e.wait_ge(s_out, 16)
        else:
            if dbg:
                SP.e.wait_ge(s_br, 16)
            SP.e.wait_ge(s_out, 32)


def _cols(w):
    k, n = w.shape
    return w.reshape(k // 128, 128, n // 256, 2, 128).transpose(2, 1, 3, 0, 4).reshape(n // 256, 128, -1)


def _blocks(w):
    k, n = w.shape
    return w.reshape(k // 512, 4, 128, n // 512, 512).transpose(3, 0, 2, 1, 4).reshape(k // 512 * (n // 512), 128, -1)


def _rows(w):
    k, n = w.shape
    return w.reshape(k // 256, 2, 128, n).transpose(0, 2, 1, 3).reshape(k // 256, 128, 2 * n)


def _feat(v):
    v = v.reshape(-1, v.shape[-1])
    return v.reshape(v.shape[0], -1, 128).transpose(2, 1, 0).reshape(128, -1)


def layout(i):
    c = np.ascontiguousarray
    a = {}
    a["x"] = i["x"][0]
    parts = {
        "a_dw": _feat(i["even_a_dw"][0]), "a_dw_b": _feat(i["even_a_dw_b"]), "a_ln_g": _feat(i["even_a_ln_g"]),
        "a_ln_b": _feat(i["even_a_ln_b"]), "b_dw": _feat(i["even_b_dw"][0]), "c_dw": _feat(i["odd_c_dw"][0]),
        "c_dw_b": _feat(i["odd_c_dw_b"]), "bga": _feat(i["odd_b_gate_a"].reshape(1, -1)),
        "bgx": _feat(i["odd_b_gate_x"].reshape(1, -1)), "lam": _feat(i["odd_lam"]),
        "mixg0": _feat(i["mix_norm_g_2"][0:1]), "mixg1": _feat(i["mix_norm_g_2"][1:2]),
        "kvg": _feat(i["kv_norm_g_2"].reshape(1, -1)),
        "ffng0": _feat(i["ffn_norm_g_2"][0:1]), "ffng1": _feat(i["ffn_norm_g_2"][1:2]),
        "fcw0": _feat(i["ffn_conv_w_2"][0]), "fcw1": _feat(i["ffn_conv_w_2"][1]),
        "fcb0": _feat(i["ffn_conv_b_2"][0:1]), "fcb1": _feat(i["ffn_conv_b_2"][1:2]),
        "lng0": _feat(i["ln1_g"][0:1]), "lnb0": _feat(i["ln1_b"][0:1]),
        "lng1": _feat(i["ln2_g"][0:1]), "lnb1": _feat(i["ln2_b"][0:1]),
        "lng2": _feat(i["ln1_g"][1:2]), "lnb2": _feat(i["ln1_b"][1:2]),
        "wr": i["w_router"].reshape(8, 128, 16).transpose(1, 0, 2).reshape(128, 128),
        "wf": i["a_w_in_2"][0][:, 3072:].reshape(8, 128, 16).transpose(1, 0, 2).reshape(128, 128),
    }
    for n, (at, w) in COLS.items():
        assert parts[n].shape == (128, w), n
    a["cols"] = c(np.concatenate([parts[n] for n in COLS], axis=1))
    a["b_router"] = c(i["b_router"].reshape(16, 1))
    a["a_b_f"] = c(i["a_b_f_2"].reshape(16, 1))
    a["rows"] = c(np.stack([i["ln2_g"][1], i["ln2_b"][1], i["final_norm_g_2"]]))
    a["even_w_in"] = c(_cols(i["even_w_in"][0]))
    a["even_w_out"] = c(_rows(i["even_w_out"][0]))
    a["odd_w_in"] = c(_cols(i["odd_w_in"][0]))
    a["odd_w_out"] = c(_rows(i["odd_w_out"][0]))
    g = np.stack([i["odd_w_gate_a"][0], i["odd_w_gate_x"][0]])
    a["odd_gates"] = c(g.reshape(2, 4, 2, 128, 256).transpose(0, 3, 1, 2, 4).reshape(2, 128, 2048))
    for k, n in (("w1", "moe_w1"), ("w3", "moe_w3"), ("w2", "moe_w2")):
        w = i[n]
        a[k] = c(w.reshape(2, 16, 4, 2, 128, 1024).transpose(0, 1, 2, 4, 3, 5).reshape(2, 16, 4, 128, 2048))
    a["a_w_in"] = c(_cols(i["a_w_in_2"][0][:, :2048]))
    a["a_w_v"] = c(_blocks(i["a_w_in_2"][0][:, 2048:3072]))
    a["a_w_out"] = c(_rows(i["a_w_out_2"][0]))
    a["w_k"] = c(_cols(i["w_kv_2"][:, :1536]))
    a["w_v"] = c(_blocks(i["w_kv_2"][:, 1536:]))
    a["b_w_q"] = c(_cols(i["b_w_q_2"][0]))
    a["b_w_out"] = c(_rows(i["b_w_out_2"][0]))
    up = [_cols(i["ffn_w_up_2"][n]) for n in range(2)]
    order = [x for p in range(11) for x in (11 + p, p)]
    a["ffn_up"] = c(np.stack([u[order] for u in up]))
    a["ffn_down"] = c(np.stack([_rows(i["ffn_w_down_2"][n]) for n in range(2)]))
    return a


def build(nc, shapes, dbg=None):
    A = {n: nc.dram_tensor(f"in_{n}", s, F32, kind="ExternalInput").ap() for n, s in shapes.items()}
    out = nc.dram_tensor("out_y", (T, D), F32, kind="ExternalOutput").ap()
    program(nc, A, out, dbg)


def kernel(**inputs):
    import concourse.bacc as _bacc
    from concourse.bass_utils import run_bass_kernel_spmd as _run

    arrays = layout({k: np.asarray(v) for k, v in inputs.items()})
    nc = _bacc.Bacc("TRN2", target_bir_lowering=False, num_devices=1)
    build(nc, {n: v.shape for n, v in arrays.items()})
    r = _run(nc, [{f"in_{n}": v for n, v in arrays.items()}], core_ids=[0])
    return r.results[0]["out_y"].reshape(1, T, D)
```
